# Optimizing a Trainium2 kernel written in Bass

```python
import math
import jax, jax.numpy as jnp
from jax import lax
import numpy as np

D_MODEL = 2048
BATCH = 1
SEQ = 256
DEPTH = 1

GRID_W = 64
CTX_LEN = 256
NA_HEADS = 8
NA_HEAD_DIM = 128
NA_WIDTH = NA_HEADS * NA_HEAD_DIM
NA_WIN_ROWS = 8
NA_WIN_COLS = 16
DIFF_HEADS = 8
DIFF_HEAD_DIM = 64
DIFF_V_DIM = 2 * DIFF_HEAD_DIM
DIFF_QK_WIDTH = DIFF_HEADS * 2 * DIFF_HEAD_DIM
DIFF_V_WIDTH = DIFF_HEADS * DIFF_V_DIM
N_QKV = 3 * NA_WIDTH + 2 * DIFF_QK_WIDTH + DIFF_V_WIDTH
N_GATE = 2 * D_MODEL
D_FF = 5632
CONV_WIDTH = 3
Q_BLOCK = 128
ROPE_BASE = 10000.0
EPS = 1e-6

kernel_name = "hybrid_natten_diffattn_convffn_dit_block"

def rms_norm(x, g):
    xf = x.astype(jnp.float32)
    y = xf * lax.rsqrt(jnp.mean(xf * xf, axis=-1, keepdims=True) + EPS)
    return (y * g.astype(jnp.float32)).astype(x.dtype)

def modulate(h, shift, scale):
    return h * (1 + scale) + shift

def axial_rope_tables(n_tokens, head_dim):
    t = jnp.arange(n_tokens)
    row = (t // GRID_W).astype(jnp.float32)
    col = (t % GRID_W).astype(jnp.float32)
    n_freq = head_dim // 4
    inv = ROPE_BASE ** (-jnp.arange(n_freq, dtype=jnp.float32) / n_freq)
    ang_r = row[:, None] * inv[None, :]
    ang_c = col[:, None] * inv[None, :]
    ang = jnp.concatenate([ang_r, ang_r, ang_c, ang_c], axis=-1)
    return jnp.cos(ang), jnp.sin(ang)

def apply_rope(x, cos, sin):
    n, d = cos.shape
    shp = (1, n) + (1,) * (x.ndim - 3) + (d,)
    cos = cos.reshape(shp).astype(x.dtype)
    sin = sin.reshape(shp).astype(x.dtype)
    q = d // 4
    x1, x2, x3, x4 = x[..., :q], x[..., q:2 * q], x[..., 2 * q:3 * q], x[..., 3 * q:]
    rot = jnp.concatenate([-x2, x1, -x4, x3], axis=-1)
    return x * cos + rot * sin

def split_projection(p):
    b, n = p.shape[:2]
    cuts = [NA_WIDTH, 2 * NA_WIDTH, 3 * NA_WIDTH,
            3 * NA_WIDTH + DIFF_QK_WIDTH, 3 * NA_WIDTH + 2 * DIFF_QK_WIDTH]
    qa, ka, va, qb, kb, vb = jnp.split(p, cuts, axis=-1)
    qa = qa.reshape(b, n, NA_HEADS, NA_HEAD_DIM)
    ka = ka.reshape(b, n, NA_HEADS, NA_HEAD_DIM)
    va = va.reshape(b, n, NA_HEADS, NA_HEAD_DIM)
    qb = qb.reshape(b, n, DIFF_HEADS, 2, DIFF_HEAD_DIM)
    kb = kb.reshape(b, n, DIFF_HEADS, 2, DIFF_HEAD_DIM)
    vb = vb.reshape(b, n, DIFF_HEADS, DIFF_V_DIM)
    return qa, ka, va, qb, kb, vb

def dense_attention(q, k, v):
    s = jnp.einsum('bqhd,bkhd->bhqk', q, k).astype(jnp.float32) * (q.shape[-1] ** -0.5)
    p = jax.nn.softmax(s, axis=-1).astype(v.dtype)
    o = jnp.einsum('bhqk,bkhd->bqhd', p, v)
    return o.reshape(o.shape[0], o.shape[1], -1)

def neighbourhood_attention_latent(q, k, v, k_ctx, v_ctx, rpb):
    b, n, h, d = q.shape
    rows = n // GRID_W
    wr = min(NA_WIN_ROWS, rows)
    wc = NA_WIN_COLS
    n_win = wr * wc
    scale = d ** -0.5
    row_start = jnp.clip(jnp.arange(rows) - wr // 2, 0, rows - wr)
    cols = jnp.arange(GRID_W)
    key_cols = jnp.clip(cols - wc // 2, 0, GRID_W - wc)[:, None] + jnp.arange(wc)[None, :]
    col_bias_idx = key_cols - cols[:, None] + NA_WIN_COLS - 1
    q_rows = q.reshape(b, rows, GRID_W, h, d).swapaxes(0, 1)

    def one_row(args):
        r, qr = args
        key_rows = row_start[r] + jnp.arange(wr)
        idx = (key_rows[None, :, None] * GRID_W + key_cols[:, None, :]).reshape(GRID_W, n_win)
        kw = jnp.take(k, idx, axis=1)
        vw = jnp.take(v, idx, axis=1)
        row_bias_idx = key_rows - r + NA_WIN_ROWS - 1
        bias = rpb[:, row_bias_idx[None, :, None], col_bias_idx[:, None, :]]
        bias = bias.reshape(h, GRID_W, n_win).astype(jnp.float32)
        s_win = jnp.einsum('bqhd,bqkhd->bhqk', qr, kw).astype(jnp.float32) * scale + bias[None]
        s_ctx = jnp.einsum('bqhd,bchd->bhqc', qr, k_ctx).astype(jnp.float32) * scale
        p = jax.nn.softmax(jnp.concatenate([s_win, s_ctx], axis=-1), axis=-1).astype(v.dtype)
        return (jnp.einsum('bhqk,bqkhd->bqhd', p[..., :n_win], vw)
                + jnp.einsum('bhqc,bchd->bqhd', p[..., n_win:], v_ctx))

    out = lax.map(one_row, (jnp.arange(rows), q_rows))
    return out.swapaxes(0, 1).reshape(b, n, h * d)

def diff_attn_block(q, k, v, lam):
    s = jnp.einsum('bqhmd,bkhmd->bhmqk', q, k).astype(jnp.float32) * (DIFF_HEAD_DIM ** -0.5)
    p = jax.nn.softmax(s, axis=-1)
    p = (p[:, :, 0] - lam * p[:, :, 1]).astype(v.dtype)
    return jnp.einsum('bhqk,bkhd->bqhd', p, v)

def diff_attention_latent(q, k, v, k_ctx, v_ctx, lam):
    b, n = q.shape[:2]
    k_all = jnp.concatenate([k, k_ctx], axis=1)
    v_all = jnp.concatenate([v, v_ctx], axis=1)
    q_blocks = q.reshape(b, n // Q_BLOCK, Q_BLOCK, DIFF_HEADS, 2, DIFF_HEAD_DIM).swapaxes(0, 1)
    out = lax.map(lambda qb: diff_attn_block(qb, k_all, v_all, lam), q_blocks)
    return out.swapaxes(0, 1).reshape(b, n, DIFF_HEADS, DIFF_V_DIM)

def diff_head_out(o, g, lambda_init):
    o = rms_norm(o, g) * (1 - lambda_init)
    return o.reshape(o.shape[0], o.shape[1], DIFF_V_WIDTH)

def merge_branches(a, bb, gate_logits, w_pa, w_pb, w_out):
    ga, gb = jnp.split(gate_logits, 2, axis=-1)
    y = jax.nn.sigmoid(ga) * (a @ w_pa) + jax.nn.sigmoid(gb) * (bb @ w_pb)
    return y @ w_out

def conv_ffn(h, w_up, conv_w, conv_b, w_down):
    u = h @ w_up
    ch = u.shape[-1]
    u = lax.conv_general_dilated(
        u, conv_w[:, None, :].astype(u.dtype), window_strides=(1,),
        padding=((CONV_WIDTH // 2, CONV_WIDTH // 2),),
        dimension_numbers=('NWC', 'WIO', 'NWC'), feature_group_count=ch) + conv_b
    gate, up = jnp.split(u, 2, axis=-1)
    return (jax.nn.silu(gate) * up) @ w_down

def setup_inputs(seed: int = 0) -> dict:
    key = jax.random.key(seed)
    ks = jax.random.split(key, 24)
    f = jnp.float32
    nrm = lambda k, shp, s: jax.random.normal(k, shp, f) * s
    return {
        "x": nrm(ks[0], (BATCH, SEQ, D_MODEL), 1.0),
        "c": nrm(ks[1], (BATCH, D_MODEL), 1.0),
        "ctx": nrm(ks[2], (BATCH, CTX_LEN, D_MODEL), 1.0),
        "c_ctx": nrm(ks[3], (D_MODEL,), 1.0),
        "ada_w": nrm(ks[4], (DEPTH, D_MODEL, 6 * D_MODEL), 0.5 * D_MODEL ** -0.5),
        "ada_b": nrm(ks[5], (DEPTH, 6 * D_MODEL), 0.02),
        "norm1_g": 1.0 + nrm(ks[6], (DEPTH, D_MODEL), 0.05),
        "w_in": nrm(ks[7], (DEPTH, D_MODEL, N_QKV + N_GATE), D_MODEL ** -0.5),
        "na_rpb": nrm(ks[8], (DEPTH, NA_HEADS, 2 * NA_WIN_ROWS - 1, 2 * NA_WIN_COLS - 1), 0.1),
        "diff_lambda": nrm(ks[9], (DEPTH, 4, DIFF_HEAD_DIM), 0.1),
        "diff_norm_g": 1.0 + nrm(ks[10], (DEPTH, DIFF_V_DIM), 0.05),
        "w_branch_a": nrm(ks[11], (DEPTH, NA_WIDTH, D_MODEL), NA_WIDTH ** -0.5),
        "w_branch_b": nrm(ks[12], (DEPTH, DIFF_V_WIDTH, D_MODEL), DIFF_V_WIDTH ** -0.5),
        "w_out": nrm(ks[13], (DEPTH, D_MODEL, D_MODEL), D_MODEL ** -0.5),
        "norm2_g": 1.0 + nrm(ks[14], (DEPTH, D_MODEL), 0.05),
        "ffn_w_up": nrm(ks[15], (DEPTH, D_MODEL, 2 * D_FF), D_MODEL ** -0.5),
        "ffn_conv_w": nrm(ks[16], (DEPTH, CONV_WIDTH, 2 * D_FF), CONV_WIDTH ** -0.5),
        "ffn_conv_b": nrm(ks[17], (DEPTH, 2 * D_FF), 0.02),
        "ffn_w_down": nrm(ks[18], (DEPTH, D_FF, D_MODEL), D_FF ** -0.5),
        "final_norm_g": 1.0 + nrm(ks[19], (D_MODEL,), 0.05),
    }

def reference(x, c, ctx, c_ctx, ada_w, ada_b, norm1_g, w_in, na_rpb, diff_lambda,
              diff_norm_g, w_branch_a, w_branch_b, w_out, norm2_g, ffn_w_up,
              ffn_conv_w, ffn_conv_b, ffn_w_down, final_norm_g):
    n_lat = x.shape[1]
    cos, sin = axial_rope_tables(n_lat, DIFF_HEAD_DIM)
    for i in range(DEPTH):
        last = i == DEPTH - 1
        lambda_init = 0.8 - 0.6 * math.exp(-0.3 * i)
        mod = jax.nn.silu(c) @ ada_w[i] + ada_b[i]
        sh1, sc1, g1, sh2, sc2, g2 = jnp.split(mod[:, None, :], 6, axis=-1)
        mod_c = jax.nn.silu(c_ctx) @ ada_w[i] + ada_b[i]
        csh1, csc1, cg1, csh2, csc2, cg2 = jnp.split(mod_c, 6, axis=-1)

        h = modulate(rms_norm(x, norm1_g[i]), sh1, sc1)
        hc = modulate(rms_norm(ctx, norm1_g[i]), csh1, csc1)
        proj = h @ w_in[i]
        qa, ka, va, qb, kb, vb = split_projection(proj[..., :N_QKV])
        gates = proj[..., N_QKV:]
        qa_c, ka_c, va_c, qb_c, kb_c, vb_c = split_projection(hc @ w_in[i][:, :N_QKV])

        lq1, lk1, lq2, lk2 = [diff_lambda[i, j].astype(jnp.float32) for j in range(4)]
        lam = jnp.exp(jnp.sum(lq1 * lk1)) - jnp.exp(jnp.sum(lq2 * lk2)) + lambda_init

        a_lat = neighbourhood_attention_latent(qa, ka, va, ka_c, va_c, na_rpb[i])
        b_lat = diff_attention_latent(apply_rope(qb, cos, sin), apply_rope(kb, cos, sin),
                                      vb, kb_c, vb_c, lam)
        b_lat = diff_head_out(b_lat, diff_norm_g[i], lambda_init)
        x = x + g1 * merge_branches(a_lat, b_lat, gates, w_branch_a[i], w_branch_b[i], w_out[i])

        h2 = modulate(rms_norm(x, norm2_g[i]), sh2, sc2)
        x = x + g2 * conv_ffn(h2, ffn_w_up[i], ffn_conv_w[i], ffn_conv_b[i], ffn_w_down[i])

        if not last:
            gates_c = hc @ w_in[i][:, N_QKV:]
            a_c = dense_attention(qa_c, ka_c, va_c)
            b_c = diff_head_out(diff_attn_block(qb_c, kb_c, vb_c, lam), diff_norm_g[i], lambda_init)
            ctx = ctx + cg1 * merge_branches(a_c, b_c, gates_c, w_branch_a[i], w_branch_b[i], w_out[i])
            hc2 = modulate(rms_norm(ctx, norm2_g[i]), csh2, csc2)
            ctx = ctx + cg2 * conv_ffn(hc2, ffn_w_up[i], ffn_conv_w[i], ffn_conv_b[i], ffn_w_down[i])
    return rms_norm(x, final_norm_g)


_drawn_inputs = setup_inputs


def setup_inputs(seed=0):
    import zlib

    import numpy as np

    out = dict(_drawn_inputs(seed))
    spreads = {}
    factors = {'norm1_g': 8.0,
     'na_rpb': 8.0,
     'diff_lambda': 8.0,
     'diff_norm_g': 7.314,
     'norm2_g': 3.541,
     'ffn_conv_b': 8.0}
    for name, (base, spread) in spreads.items():
        noise = np.random.default_rng([zlib.crc32(name.encode()), seed]).standard_normal(out[name].shape)
        drawn = base * np.exp(spread * noise) if base else spread * noise
        out[name] = __import__('jax').numpy.asarray(drawn.astype(out[name].dtype))
    for name, factor in factors.items():
        out[name] = (out[name] * factor).astype(out[name].dtype)
    return out
```

```python
import math
from contextlib import ExitStack

import numpy as np

import concourse.bass as bass
from concourse import mybir

F32 = mybir.dt.float32
F32R = mybir.dt.float32r
ACT = mybir.ActivationFunctionType
ALU = mybir.AluOpType
AX = mybir.AxisListType

P = 128
D = 2048
SEQ = 256
GRID_W = 64
ROWS = SEQ // GRID_W
HEADS = 8
HD = 128
WIDTH = HEADS * HD
WIN_ROWS = 8
WIN_COLS = 16
RPB_ROWS = 2 * WIN_ROWS - 1
RPB_COLS = 2 * WIN_COLS - 1
RPB_MARGIN = WIN_COLS
RPB_BLOCK = GRID_W * GRID_W + 2 * RPB_MARGIN
MAP_DIM = 64
D_FF = 5632
TAPS = 3
EPS = 1e-6
LAMBDA_INIT = 0.8 - 0.6 * math.exp(0.0)
NA_SCALE = HD ** -0.5
DIFF_SCALE = MAP_DIM ** -0.5
MASKED = -1e30

KC = D // P
TOK = SEQ // P
UNIT = 1024
GROUP = 512
TILES = GROUP // P
SLOTS = 8
SPLIT_SLOTS = 4
FF_TILES = D_FF // P
FF_GROUPS = D_FF // GROUP

QA, KA, VA, QB, KB, VB = (n * WIDTH for n in range(6))
GATE_A = 6 * WIDTH
GATE_B = GATE_A + D

JOB_NA = 8
JOB_DIFF = 14
JOB_MERGE = 20
JOB_OUT = 32
JOB_UP = 36
JOB_DOWN = JOB_UP + 2 * FF_GROUPS
PROJECTIONS = [("k", KA), ("k", KA + GROUP), ("v", VA), ("v", VA + GROUP), ("q", QA), ("q", QA + GROUP),
               ("k", KB), ("k", KB + GROUP), ("v", VB), ("v", VB + GROUP), ("q", QB), ("q", QB + GROUP)]
ADA_GROUPS = 16
ADA_FIRST_COL = 2 * D

C_IDENT, C_ROT, C_COS, C_SIN, C_MASK, C_SEL = 0, 128, 256, 512, 768, 832
C_ALL = 834
V_C, V_CC, V_N1, V_N2, V_ADAB, V_CONV, V_CONVB, V_DNG = 0, 16, 32, 48, 64, 160, 424, 512
V_ALL = 513


def shape_constants():
    k = np.zeros((P, C_ALL), np.float32)
    k[:, C_IDENT:C_IDENT + P] = np.eye(P)
    quarter = MAP_DIM // 4
    for m in range(P // MAP_DIM):
        for pair in range(2):
            a = m * MAP_DIM + 2 * pair * quarter
            for j in range(quarter):
                k[a + quarter + j, C_ROT + a + j] = -1.0
                k[a + j, C_ROT + a + quarter + j] = 1.0
    t = np.arange(SEQ)
    inv = (np.float32(10000.0) ** (-np.arange(quarter, dtype=np.float32) / np.float32(quarter))).astype(np.float32)
    ang_r = (t // GRID_W).astype(np.float32)[:, None] * inv[None]
    ang_c = (t % GRID_W).astype(np.float32)[:, None] * inv[None]
    ang = np.concatenate([ang_r, ang_r, ang_c, ang_c], axis=1).T
    k[:, C_COS:C_COS + SEQ] = np.tile(np.cos(ang), (2, 1))
    k[:, C_SIN:C_SIN + SEQ] = np.tile(np.sin(ang), (2, 1))
    col = np.arange(P) % GRID_W
    start = np.clip(col - WIN_COLS // 2, 0, GRID_W - WIN_COLS)[:, None]
    key = np.arange(GRID_W)[None]
    k[:, C_MASK:C_MASK + GRID_W] = np.where((key >= start) & (key < start + WIN_COLS), 0.0, MASKED)
    k[0:2, C_SEL] = 1.0
    k[2:4, C_SEL + 1] = 1.0
    return k


def block_program(nc, x, c, ctx, c_ctx, ada_w, ada_b, norm1_g, w_in, na_rpb, diff_lambda, diff_norm_g,
                  w_branch_a, w_branch_b, w_out, norm2_g, ffn_w_up, ffn_conv_w, ffn_conv_b, ffn_w_down,
                  final_norm_g, constants, out):
    base = nc.sbuf_base + (-nc.sbuf_base) % 64
    kb = 1024

    def place(name, at, shape, dtype=F32):
        return nc.alloc_sbuf_tensor_at(name, shape, dtype, offset=base + at)

    raw = place("raw", 0, [P, SLOTS, UNIT])
    w_hi = place("w_hi", 32 * kb, [P, SPLIT_SLOTS, UNIT], F32R)
    w_lo = place("w_lo", 48 * kb, [P, SPLIT_SLOTS, UNIT], F32R)
    lat, con = 64 * kb, 96 * kb
    hT = place("hT", lat, [P, 2, 2, KC, SEQ], F32R)
    junk = place("junk", lat, [P, D])
    h2T = place("h2T", lat, [P, KC, 2, SEQ], F32R)
    aT_hi = place("aT_hi", con, [P, HEADS, SEQ], F32R)
    aT_lo = place("aT_lo", con + 8 * kb, [P, HEADS, SEQ], F32R)
    bT_hi = place("bT_hi", con + 16 * kb, [P, HEADS, SEQ], F32R)
    bT_lo = place("bT_lo", con + 24 * kb, [P, HEADS, SEQ], F32R)
    rope_tmp = place("rope_tmp", con + 16 * kb, [P, 2, 2, SEQ])
    g2_rows = place("g2_rows", con, [P, D])
    final_rows = place("final_rows", con + 8 * kb, [P, D])
    conv_in = place("conv_in", con + 16 * kb, [P, TILES, SEQ])
    conv_gate = place("conv_gate", con + 20 * kb, [P, TILES, SEQ])
    conv_up = place("conv_up", con + 24 * kb, [P, TILES, SEQ])
    arena = 128 * kb
    tokens = place("tokens", arena, [P, 2 * TOK, D])
    modulated = place("modulated", arena + 32 * kb, [P, 4, 2, SEQ])
    kT = place("kT", arena, [P, HEADS, 2 * SEQ])
    v_sb = place("v_sb", arena + 16 * kb, [P, 2 * TOK, WIDTH])
    qT = place("qT", arena + 32 * kb, [P, HEADS, SEQ])
    bias = place("bias", arena + 40 * kb, [P, 2, TOK * SEQ])
    diff_pT = place("diff_pT", arena + 40 * kb, [P, 2, 2 * TOK, P])
    yT_hi = place("yT_hi", arena, [P, KC, SEQ], F32R)
    yT_lo = place("yT_lo", arena + 16 * kb, [P, KC, SEQ], F32R)
    g1_rows = place("g1_rows", arena + 32 * kb, [P, D])
    y = place("y", arena + 40 * kb, [P, TOK, GROUP])
    x2_normed = place("x2_normed", arena, [P, TOK, D])
    modulated2 = place("modulated2", arena + 16 * kb, [P, 4, 2, SEQ])
    hidden = place("hidden", arena, [P, FF_TILES, SEQ])
    att = 172 * kb
    aT = place("aT", att, [P, HEADS, SEQ])
    diff_o = place("diff_o", att, [P, HEADS * TOK, HD])
    ada_raw = place("ada_raw", att + 8 * kb, [P, 4, GROUP])
    ada_acc = place("ada_acc", att + 16 * kb, [P, 2, GROUP])
    mod_rows = place("mod_rows", att, [4, 2 * D])
    x2 = place("x2", att, [P, TOK, D])
    tmp = 192 * kb
    param_rows = place("param_rows", tmp, [P, 6, P])
    scores = place("scores", tmp, [P, 3, 2 * SEQ])
    na_pT = place("na_pT", tmp + 6 * kb, [P, 2 * TOK, P])
    diff_e = place("diff_e", tmp, [P, 2, 2, 2 * SEQ])
    diff_sq = place("diff_sq", tmp, [P, HEADS * TOK, HD])
    bT = place("bT", tmp, [P, HEADS, SEQ])
    sig_a = place("sig_a", tmp, [P, TOK, GROUP])
    sig_b = place("sig_b", tmp + 4 * kb, [P, TOK, GROUP])
    f_hi = place("f_hi", tmp, [P, SPLIT_SLOTS, SEQ], F32R)
    f_lo = place("f_lo", tmp + 4 * kb, [P, SPLIT_SLOTS, SEQ], F32R)
    final_tmp = place("final_tmp", con + 16 * kb, [P, TOK, D])
    at = 200 * kb

    def keep(name, shape, dtype=F32):
        nonlocal at
        t = place(name, at, shape, dtype)
        at += (4 * int(np.prod(shape[1:])) + 31) // 32 * 32
        return t

    consts = keep("consts", [P, C_ALL])
    vecs = keep("vecs", [P, V_ALL])
    c_parts = keep("c_parts", [P, 4 * KC + P], F32R)
    silu_c = keep("silu_c", [P, 2 * KC])
    exp_c = keep("exp_c", [P, 2 * KC])
    gain1 = keep("gain1", [P, 2, KC])
    shift1 = keep("shift1", [P, 2, KC])
    mod = keep("mod", [P, 4 * ADA_GROUPS])
    gain2 = keep("gain2", [P, KC])
    ones = keep("ones", [P, 1])
    rms1 = keep("rms1", [P, 2 * TOK])
    row_max = keep("row_max", [P, 3, 2])
    row_sum = keep("row_sum", [P, 3, 2])
    lam = keep("lam", [P, 2])
    rms_o = keep("rms_o", [P, HEADS * TOK])
    dng = keep("dng", [P, 1])
    ssq2 = keep("ssq2", [P, TOK, 4])
    rms2 = keep("rms2", [P, TOK])
    rms3 = keep("rms3", [P, TOK])
    lam_in = place("lam_in", lat + 8 * kb, [P, 4 * MAP_DIM])
    lam_prod = place("lam_prod", lat + 9 * kb, [P, 2, MAP_DIM])
    zeros = place("zeros", con, [HEADS * RPB_ROWS, RPB_BLOCK])
    ident = consts[:, C_IDENT:C_IDENT + P]

    rpb_grid = nc.dram_tensor("rpb_grid", [HEADS * RPB_ROWS, RPB_BLOCK], F32)

    ps = nc.alloc_psum_tensor("ps", [P, 8, GROUP], F32)

    with ExitStack() as es:
        def sem(name):
            return es.enter_context(nc.semaphore(name))

        def sems(name, n):
            return [sem(f"{name}{i}") for i in range(n)]

        raw_landed = sems("raw_landed", SLOTS)
        hi_ready = sems("hi_ready", SLOTS)
        lo_ready = sems("lo_ready", SLOTS)
        used = sems("used", SLOTS)
        consts_landed = sem("consts_landed")
        rows_landed = sem("rows_landed")
        rows2_landed = sem("rows2_landed")
        tokens_landed = sem("tokens_landed")
        vecs_turned = sem("vecs_turned")
        vecs_ready = sem("vecs_ready")
        exp_c_ready = sem("exp_c_ready")
        start_dve = sem("start_dve")
        ones_ready = sem("ones_ready")
        c_ready = sem("c_ready")
        lam_landed = sem("lam_landed")
        lam_step = sem("lam_step")
        lam_exp = sem("lam_exp")
        lam_ready = sem("lam_ready")
        squares1 = sem("squares1")
        rms1_step = sem("rms1_step")
        normed1 = sem("normed1")
        mod_rows_ready = sem("mod_rows_ready")
        mod_cols_ready = sem("mod_cols_ready")
        mod1_step = sem("mod1_step")
        mod1_ready = sem("mod1_ready")
        tokens_turned = sem("tokens_turned")
        modulated_ready = sem("modulated_ready")
        hT_hi_ready = sem("hT_hi_ready")
        hT_ready = sem("hT_ready")
        ada_landed = sems("ada_landed", 4)
        ada_summed = sem("ada_summed")
        mod_summed = sem("mod_summed")
        mod_ready = sem("mod_ready")
        half_read = sem("half_read")
        kv_read = sem("kv_read")
        q_read = sem("q_read")
        zeros_ready = sem("zeros_ready")
        padded = sem("padded")
        bias_landed = sems("bias_landed", 2)
        bias_ready = sem("bias_ready")
        na_scored = sem("na_scored")
        na_ctx_scaled = sem("na_ctx_scaled")
        na_biased = sem("na_biased")
        na_max = sem("na_max")
        na_exp = sem("na_exp")
        na_recip = sem("na_recip")
        na_probs = sem("na_probs")
        na_turned = sem("na_turned")
        na_pT_ready = sem("na_pT_ready")
        na_summed = sem("na_summed")
        na_out = sem("na_out")
        aT_hi_ready = sem("aT_hi_ready")
        aT_ready = sem("aT_ready")
        rotated = sem("rotated")
        rope_cos = sem("rope_cos")
        rope_sin = sem("rope_sin")
        roped = sem("roped")
        df_scored = sem("df_scored")
        df_max = sem("df_max")
        df_bias = sem("df_bias")
        df_exp = sem("df_exp")
        df_recip = sem("df_recip")
        df_lam = sem("df_lam")
        df_first = sem("df_first")
        df_probs = sem("df_probs")
        df_turned = sem("df_turned")
        df_pT_ready = sem("df_pT_ready")
        df_summed = sem("df_summed")
        df_out = sem("df_out")
        o_step = sem("o_step")
        o_normed = sem("o_normed")
        o_turned = sem("o_turned")
        bT_scaled = sem("bT_scaled")
        bT_hi_ready = sem("bT_hi_ready")
        bT_ready = sem("bT_ready")
        g1_spread = sem("g1_spread")
        g1_ready = sem("g1_ready")
        sig_a_ready = sem("sig_a_ready")
        sig_b_ready = sem("sig_b_ready")
        y_a = sem("y_a")
        y_b = sem("y_b")
        y_ready = sem("y_ready")
        y_turned = sem("y_turned")
        yT_hi_ready = sem("yT_hi_ready")
        yT_ready = sem("yT_ready")
        x2_landed = sem("x2_landed")
        out_gated = sem("out_gated")
        x2_added = sem("x2_added")
        squares2 = sem("squares2")
        rms2_step = sem("rms2_step")
        x2_norm_ready = sem("x2_norm_ready")
        gain2_ready = sem("gain2_ready")
        g2_spread = sem("g2_spread")
        g2_ready = sem("g2_ready")
        x2_turned = sem("x2_turned")
        modulated2_ready = sem("modulated2_ready")
        h2T_hi_ready = sem("h2T_hi_ready")
        h2T_ready = sem("h2T_ready")
        up_half_read = sem("up_half_read")
        up_read = sem("up_read")
        conv_mid = sem("conv_mid")
        conv_left = sem("conv_left")
        conv_done = sem("conv_done")
        gate_done = sem("gate_done")
        hidden_ready = sem("hidden_ready")
        f_hi_ready = sem("f_hi_ready")
        f_lo_ready = sem("f_lo_ready")
        final_landed = sem("final_landed")
        out3_gated = sem("out3_gated")
        x3_ready = sem("x3_ready")
        squares3 = sem("squares3")
        rms3_step = sem("rms3_step")
        out_ready = sem("out_ready")
        out_stored = sem("out_stored")

        block = es.enter_context(nc.Block())

        w_in_v = w_in[0].rearrange("(k p) n -> p k n", p=P)
        ada_v = ada_w[0].rearrange("(k p) n -> p k n", p=P)
        pa_v = w_branch_a[0].rearrange("(k p) n -> p k n", p=P)
        pb_v = w_branch_b[0].rearrange("(k p) n -> p k n", p=P)
        out_v = w_out[0].rearrange("(k p) n -> p k n", p=P)
        up_v = ffn_w_up[0].rearrange("(k p) n -> p k n", p=P)
        down_v = ffn_w_down[0].rearrange("(k p) n -> p k n", p=P)

        def results_read(j):
            mine = PROJECTIONS[j - JOB_NA][0] == "q"
            n = sum((kind == "q") == mine for kind, _ in PROJECTIONS[:j - JOB_NA + 1])
            return (q_read if mine else kv_read), n

        def ada_bank(j):
            if j < JOB_MERGE:
                return 4 * (j % 2) + 3
            return 7 if (j - JOB_MERGE) % 3 == 0 else 6

        def is_first(j):
            return isinstance(j, int) and j == 0

        @block.sync
        def _(sp):
            def load(j, s, src, parts=2):
                if not is_first(j):
                    sp.wait_ge(lo_ready[s], j)
                dst = raw[:, s, :].rearrange("p (a n) -> p a n", a=parts)
                sp.dma_start(dst, src).then_inc(raw_landed[s], 16)

            sp.dma_start(consts[:], constants).then_inc(consts_landed, 16)
            sp.dma_start(param_rows[0:16, 0, :], c.rearrange("a (k p) -> (a k) p", p=P)).then_inc(rows_landed, 16)
            sp.dma_start(param_rows[16:32, 0, :], c_ctx.rearrange("(k p) -> k p", p=P)).then_inc(rows_landed, 16)
            sp.dma_start(param_rows[32:48, 0, :],
                         norm1_g.rearrange("a (k p) -> (a k) p", p=P)).then_inc(rows_landed, 16)
            sp.dma_start(param_rows[48:64, 0, :],
                         norm2_g.rearrange("a (k p) -> (a k) p", p=P)).then_inc(rows_landed, 16)
            for j in range(JOB_NA):
                for s in range(SLOTS):
                    kc = SLOTS * (j % 2) + s
                    load(j, s, ada_v[:, kc:kc + 1, UNIT * (j // 2):UNIT * (j // 2) + UNIT], parts=1)
                if j == 1:
                    sp.dma_start(tokens[:, 0:TOK, :],
                                 x[0].rearrange("(t p) n -> p t n", p=P)).then_inc(tokens_landed, 16)
                    sp.dma_start(tokens[:, TOK:2 * TOK, :],
                                 ctx[0].rearrange("(t p) n -> p t n", p=P)).then_inc(tokens_landed, 16)
            for n, (_, col) in enumerate(PROJECTIONS):
                for s in range(SLOTS):
                    load(JOB_NA + n, s, w_in_v[:, 2 * s:2 * s + 2, col:col + GROUP])
            with sp.Fori(1, D // GROUP + 1) as g:
                jobs = [sp.snap(3 * g + (JOB_MERGE - 3 + n)) for n in range(3)]
                cols = [g * GROUP + (col - GROUP) for col in (GATE_A, GATE_B, 0)]
                for n in range(2):
                    for s in range(SLOTS):
                        load(jobs[n], s, w_in_v[:, 2 * s:2 * s + 2, bass.ds(cols[n], GROUP)])
                col = cols[2]
                for s in range(SLOTS):
                    src = (pa_v, pb_v)[s // 4]
                    load(jobs[2], s, src[:, 2 * (s % 4):2 * (s % 4) + 2, bass.ds(col, GROUP)])
            with sp.Fori(1, D // GROUP + 1) as g:
                job, col = sp.snap(g + (JOB_OUT - 1)), g * GROUP - GROUP
                for s in range(SLOTS):
                    load(job, s, out_v[:, 2 * s:2 * s + 2, bass.ds(col, GROUP)])
            with sp.Fori(1, FF_GROUPS + 1) as g:
                jobs = [sp.snap(2 * g + (JOB_UP - 2 + half)) for half in range(2)]
                cols = [g * GROUP + (half * D_FF - GROUP) for half in range(2)]
                for half in range(2):
                    for s in range(SLOTS):
                        load(jobs[half], s, up_v[:, 2 * s:2 * s + 2, bass.ds(cols[half], GROUP)])
            with sp.Fori(1, FF_GROUPS + 1) as g:
                job = sp.snap(g + (JOB_DOWN - 1))
                rows = [TILES * g + (t - TILES) for t in range(TILES)]
                for s in range(SLOTS):
                    load(job, s, down_v[:, bass.ds(rows[s // 2], 1), UNIT * (s % 2):UNIT * (s % 2) + UNIT],
                         parts=1)
            for t in range(TOK):
                sp.wait_ge(out_ready, t + 1)
                sp.dma_start(out[0, t * P:(t + 1) * P, :], final_tmp[:, t, :]).then_inc(out_stored, 16)
            sp.wait_ge(out_stored, 16 * TOK)

        @block.gpsimd
        def _(pool):
            pool.memset(zeros[:], 0.0).then_inc(zeros_ready, 1)
            pool.wait_ge(zeros_ready, 1)
            pool.dma_start(rpb_grid.ap(), zeros[:]).then_inc(padded, 16)
            pool.dma_start(lam_in[:], diff_lambda.rearrange("a m d -> a (m d)").to_broadcast([P, 4 * MAP_DIM]))\
                .then_inc(lam_landed, 16)
            pool.wait_ge(padded, 16)
            pool.dma_start(bass.AP(rpb_grid, RPB_MARGIN - (WIN_COLS - 1),
                                   [[RPB_BLOCK, HEADS * RPB_ROWS], [GRID_W + 1, GRID_W], [1, RPB_COLS]]),
                           na_rpb[0].rearrange("h r w -> (h r) w").unsqueeze(1)
                           .to_broadcast([HEADS * RPB_ROWS, GRID_W, RPB_COLS])).then_inc(padded, 16)
            pool.wait_ge(padded, 32)

            def load_ada(g, skip_wait=False):
                for kc in range(KC):
                    if not (skip_wait and kc < 4):
                        pool.wait_ge(ada_summed, KC * g + kc - 3)
                    pool.dma_start(ada_raw[:, kc % 4:kc % 4 + 1, :],
                                   ada_v[:, kc:kc + 1, bass.ds(g * GROUP + ADA_FIRST_COL, GROUP)])\
                        .then_inc(ada_landed[kc % 4], 16)

            pool.wait_ge(mod_cols_ready, 1)
            load_ada(0, skip_wait=True)

            def load_bias(h):
                for r in range(ROWS):
                    src = bass.AP(rpb_grid, (h * RPB_ROWS + WIN_ROWS - 1 - r) * RPB_BLOCK + RPB_MARGIN,
                                  [[GRID_W, GRID_W], [RPB_BLOCK, ROWS], [1, GRID_W]])
                    dst = bias[(r % 2) * GRID_W:(r % 2 + 1) * GRID_W, h % 2,
                               (r // 2) * SEQ:(r // 2 + 1) * SEQ].rearrange("p (a b) -> p a b", a=ROWS)
                    pool.dma_start(dst, src).then_inc(bias_landed[h % 2], 16)

            pool.wait_ge(hT_ready, KC)
            load_bias(0)
            load_bias(1)
            with pool.Fori(1, 6) as g:
                load_ada(g)
            for h in range(2, HEADS):
                pool.wait_ge(na_biased, TOK * (h - 1))
                load_bias(h)
            with pool.Fori(6, ADA_GROUPS) as g:
                load_ada(g)
            pool.wait_ge(mod_ready, ADA_GROUPS)
            pool.wait_ge(bT_ready, 1)
            pool.dma_start(x2[:], x[0].rearrange("(t p) n -> p t n", p=P)).then_inc(x2_landed, 16)
            pool.wait_ge(used[7], JOB_OUT)
            pool.dma_start(final_rows[:], final_norm_g.rearrange("(a n) -> a n", a=1).to_broadcast([P, D]))\
                .then_inc(final_landed, 16)

        @block.scalar
        def _(act):
            def round_hi(j, s):
                act.wait_ge(raw_landed[s], 16 * j + 16)
                if s >= SPLIT_SLOTS:
                    act.wait_ge(used[s - SPLIT_SLOTS], j + 1)
                elif not is_first(j):
                    act.wait_ge(used[s + SPLIT_SLOTS], j)
                act.copy(w_hi[:, s % SPLIT_SLOTS, :], raw[:, s, :]).then_inc(hi_ready[s], 1)

            act.dma_start(param_rows[0:96, 1, :], ada_b.rearrange("a (k p) -> (a k) p", p=P))\
                .then_inc(rows2_landed, 16)
            for tap in range(TAPS):
                act.dma_start(param_rows[0:88, 2 + tap, :],
                              ffn_conv_w[0, tap:tap + 1, :].rearrange("a (k p) -> (a k) p", p=P))\
                    .then_inc(rows2_landed, 16)
            act.dma_start(param_rows[0:88, 5, :], ffn_conv_b.rearrange("a (k p) -> (a k) p", p=P))\
                .then_inc(rows2_landed, 16)
            act.dma_start(param_rows[88:89, 5, :], diff_norm_g).then_inc(rows2_landed, 16)
            act.wait_ge(vecs_ready, 1)
            act.activation(exp_c[:], vecs[:, V_C:V_C + 2 * KC], ACT.Exp, scale=-1.0).then_inc(exp_c_ready, 1)
            act.wait_ge(lam_step, 2)
            act.activation(lam[:], lam[:], ACT.Exp).then_inc(lam_exp, 1)

            def read_mod_rows(g):
                act.wait_ge(used[7], 2 * g + 2)
                act.copy(mod_rows[:, g * UNIT:(g + 1) * UNIT].rearrange("p (a n) -> p a n", a=2),
                         ps[0:4, 2 * g:2 * g + 2, :]).then_inc(mod_rows_ready, 1)

            for j in range(JOB_NA):
                for s in range(SLOTS):
                    round_hi(j, s)
                    if s == 3 and j % 2 == 0 and j:
                        read_mod_rows(j // 2 - 1)
                    if j in (3, 4) and s in (1, 5):
                        t = 2 * (j - 3) + s // 4
                        act.wait_ge(tokens_landed, 32)
                        if t == 0:
                            act.wait_ge(lam_step, 2)
                        else:
                            act.wait_ge(squares1, t)
                        act.activation(junk[:], tokens[:, t, :], ACT.Square,
                                       accum_out=rms1[:, t:t + 1]).then_inc(squares1, 1)
                if j == 5:
                    act.wait_ge(rms1_step, 1)
                    act.activation(rms1[:], rms1[:], ACT.Sqrt).then_inc(rms1_step, 1)

            def modulate(kc):
                act.wait_ge(tokens_turned, kc + 1)
                if kc >= 4:
                    act.wait_ge(hT_ready, kc - 3)
                for st in range(2):
                    act.activation(modulated[:, kc % 4, st, :], ps[:, 4 + kc % 4, st * SEQ:(st + 1) * SEQ],
                                   ACT.Identity, bias=shift1[:, st, kc:kc + 1],
                                   scale=gain1[:, st, kc:kc + 1]).then_inc(modulated_ready, 1)

            def read_result(j):
                kind, col = PROJECTIONS[j - JOB_NA]
                g = (col // GROUP) % 2
                b = 4 * (j % 2)
                act.wait_ge(used[7], j + 1)
                if kind == "k":
                    act.copy(kT[:, TILES * g:TILES * (g + 1), :], ps[:, b:b + 4, :]).then_inc(kv_read, 1)
                elif kind == "v":
                    act.copy(v_sb[:, :, g * GROUP:(g + 1) * GROUP], ps[:, b:b + 4, :])\
                        .then_inc(kv_read, 1)
                else:
                    act.copy(qT[:, TILES * g:TILES * (g + 1), :], ps[:, b:b + 4, 0:SEQ]).then_inc(half_read, 1)

            for s in range(SPLIT_SLOTS):
                round_hi(JOB_NA, s)
            read_mod_rows(3)
            act.wait_ge(mod1_ready, 1)
            for s in range(SLOTS):
                modulate(2 * s)
                modulate(2 * s + 1)
                if s < SPLIT_SLOTS:
                    round_hi(JOB_NA, s + SPLIT_SLOTS)
            for j in range(JOB_NA + 1, JOB_DIFF):
                for s in range(SLOTS):
                    round_hi(j, s)
                    if s == 3:
                        read_result(j - 1)
            for s in range(SPLIT_SLOTS):
                round_hi(JOB_DIFF, s)
            read_result(JOB_DIFF - 1)

            def scale_ctx(n):
                act.wait_ge(na_scored, n + 1)
                if n >= 3:
                    act.wait_ge(na_turned, n - 2)
                act.mul(scores[:, n % 3, SEQ:2 * SEQ], ps[:, 6 + n % 2, 0:SEQ], NA_SCALE)\
                    .then_inc(na_ctx_scaled, 1)

            def na_exponent(n):
                act.wait_ge(na_max, n + 1)
                act.activation(scores[:, n % 3, :], scores[:, n % 3, :], ACT.Exp, bias=row_max[:, n % 3, 0:1],
                               accum_out=row_sum[:, n % 3, 0:1]).then_inc(na_exp, 1)

            N = HEADS * TOK
            scale_ctx(0)
            scale_ctx(1)
            na_exponent(0)
            for n in range(N):
                if n + 2 < N:
                    scale_ctx(n + 2)
                if n + 1 < N:
                    na_exponent(n + 1)
                act.wait_ge(na_turned, n + 1)
                if n >= 1:
                    act.wait_ge(na_summed, n)
                act.copy(na_pT[:], ps[:, 2 + n % 2, :].rearrange("p (a b) -> p a b", a=4)).then_inc(na_pT_ready, 1)

            for j in range(JOB_DIFF, JOB_MERGE):
                for s in range(SLOTS):
                    if j > JOB_DIFF or s >= SPLIT_SLOTS:
                        round_hi(j, s)
                    if s == 3 and j > JOB_DIFF:
                        read_result(j - 1)
            for s in range(SPLIT_SLOTS):
                round_hi(JOB_MERGE, s)
            read_result(JOB_MERGE - 1)
            act.wait_ge(na_out, HEADS * TOK)
            act.copy(aT_hi[:], aT[:]).then_inc(aT_hi_ready, 1)

            def df_exponents(n):
                act.wait_ge(df_bias, n + 1)
                if n >= 2:
                    act.wait_ge(df_turned, n - 1)
                for m in range(2):
                    act.activation(diff_e[:, n % 2, m, :], ps[:, 2 * (n % 2) + m, :], ACT.Exp,
                                   bias=row_max[:, n % 3, m:m + 1], scale=DIFF_SCALE,
                                   accum_out=row_sum[:, n % 3, m:m + 1]).then_inc(df_exp, 1)

            df_exponents(0)
            for n in range(N):
                if n + 1 < N:
                    df_exponents(n + 1)
                act.wait_ge(df_turned, n + 1)
                if n >= 2:
                    act.wait_ge(df_summed, n - 1)
                act.copy(diff_pT[:, n % 2, :, :], ps[:, 4, :].rearrange("p (a b) -> p a b", a=4))\
                    .then_inc(df_pT_ready, 1)
                if n >= 1:
                    act.wait_ge(df_summed, n)
                    act.copy(diff_o[:, n - 1, :], ps[:, 6 + (n - 1) % 2, 0:P]).then_inc(df_out, 1)
            act.wait_ge(df_summed, N)
            act.copy(diff_o[:, N - 1, :], ps[:, 6 + (N - 1) % 2, 0:P]).then_inc(df_out, 1)
            act.wait_ge(o_step, 3)
            act.activation(rms_o[:], rms_o[:], ACT.Sqrt).then_inc(o_step, 1)

            act.wait_ge(o_turned, 1)
            act.mul(bT[:].rearrange("p h q -> p (h q)"), ps[:, 4:8, :].rearrange("p a n -> p (a n)"), dng[:])\
                .then_inc(bT_scaled, 1)
            act.wait_ge(bT_scaled, 1)
            act.copy(bT_hi[:], bT[:]).then_inc(bT_hi_ready, 1)

            def turn_hi(g):
                act.wait_ge(y_turned, g + 1)
                act.copy(yT_hi[:, bass.ds(g * TILES, TILES), :],
                         ps[:, 4:6, :].rearrange("p a (b q) -> p (a b) q", b=2)).then_inc(yT_hi_ready, 1)

            def merge_group(g, first):
                j = 3 * g + JOB_MERGE
                for s in range(SLOTS):
                    if not first or s >= SPLIT_SLOTS:
                        round_hi(j, s)
                if not first:
                    turn_hi(g - 1)
                for s in range(SLOTS):
                    round_hi(j + 1, s)
                    if s == 3:
                        act.wait_ge(used[7], j + 1)
                        if not first:
                            act.wait_ge(y_a, g)
                        else:
                            act.wait_ge(bT_ready, 1)
                        act.activation(sig_a[:], ps[:, 0:2, :], ACT.Sigmoid).then_inc(sig_a_ready, 1)
                if first:
                    act.wait_ge(g1_spread, 1)
                    act.copy(g1_rows[:], ps[:, 4:8, :].rearrange("p a n -> p (a n)")).then_inc(g1_ready, 1)
                for s in range(SLOTS):
                    round_hi(j + 2, s)
                    if s == 3:
                        act.wait_ge(used[7], j + 2)
                        if not first:
                            act.wait_ge(y_ready, g)
                        act.activation(sig_b[:], ps[:, 2:4, :], ACT.Sigmoid).then_inc(sig_b_ready, 1)

            merge_group(0, True)
            with act.Fori(1, D // GROUP) as g:
                merge_group(g, False)

            def square_group(g):
                for t in range(TOK):
                    act.wait_ge(x2_added, g + 1)
                    if g or t:
                        act.wait_ge(squares2, TOK * g + t)
                    act.activation(sig_b[:, t, :], x2[:, t, g * GROUP:(g + 1) * GROUP], ACT.Square,
                                   accum_out=ssq2[:, t, g:g + 1]).then_inc(squares2, 1)

            for g in range(4):
                for s in range(SLOTS):
                    round_hi(JOB_OUT + g, s)
                    if s == 4 and g:
                        square_group(g - 1)
                if g == 0:
                    turn_hi(3)
            for s in range(SPLIT_SLOTS):
                round_hi(JOB_UP, s)
            act.wait_ge(g2_spread, 1)
            act.copy(g2_rows[:], ps[:, 0:4, :].rearrange("p a n -> p (a n)")).then_inc(g2_ready, 1)
            square_group(3)
            act.wait_ge(rms2_step, 2)
            act.activation(rms2[:], rms2[:], ACT.Sqrt).then_inc(rms2_step, 1)
            act.wait_ge(gain2_ready, 2)
            for m in range(KC // 2):
                act.wait_ge(x2_turned, m + 1)
                if m >= 4:
                    act.wait_ge(h2T_ready, m - 3)
                for h in range(2):
                    kc = 2 * m + h
                    act.activation(modulated2[:, m % 4, h, :], ps[:, 4 + m % 4, h * SEQ:(h + 1) * SEQ],
                                   ACT.Identity, bias=mod[:, KC + kc:KC + kc + 1],
                                   scale=gain2[:, kc:kc + 1]).then_inc(modulated2_ready, 1)
                if m < SPLIT_SLOTS:
                    round_hi(JOB_UP, m + SPLIT_SLOTS)

            def conv_begin(n, b):
                act.wait_ge(used[7], n + JOB_UP + 1)
                if not is_first(n):
                    act.wait_ge(conv_done, n)
                act.copy(conv_in[:], ps[:, b:b + 4, 0:SEQ]).then_inc(up_half_read, 1)

            def conv_middle(n, tile, dst):
                act.wait_ge(up_read, n + 1)
                for t in range(TILES):
                    act.activation(dst[:, t, :], conv_in[:, t, :], ACT.Identity,
                                   bias=vecs[:, bass.ds(tile + (V_CONVB + t), 1)],
                                   scale=vecs[:, bass.ds(tile + (V_CONV + 88 + t), 1)]).then_inc(conv_mid, 1)

            def gate_steps(i, s):
                n = 2 * i
                if s == 3:
                    conv_begin(n, 0)
                if s == 4:
                    if not is_first(i):
                        act.wait_ge(hidden_ready, i)
                    conv_middle(n, TILES * i, conv_gate)
                if s == 6:
                    act.wait_ge(conv_done, n + 1)
                    act.activation(conv_gate[:], conv_gate[:], ACT.Silu).then_inc(gate_done, 1)

            def up_steps(i, s):
                n = 2 * i + 1
                if s == 3:
                    conv_begin(n, 4)
                if s == 4:
                    conv_middle(n, TILES * i + FF_TILES, conv_up)

            def ffn_pair(i, first):
                for s in range(SLOTS):
                    if not first:
                        round_hi(2 * i + JOB_UP, s)
                        up_steps(i - 1, s)
                for s in range(SLOTS):
                    round_hi(2 * i + JOB_UP + 1, s)
                    gate_steps(i, s)

            ffn_pair(0, True)
            with act.Fori(1, FF_GROUPS) as i:
                ffn_pair(i, False)

            def f_high(i, t, first):
                if not first:
                    act.wait_ge(used[2 * t + 1], i + JOB_DOWN)
                act.copy(f_hi[:, t:t + 1, :], hidden[:, bass.ds(TILES * i + t, 1), :])\
                    .then_inc(f_hi_ready, 1)

            def down_job(i, first):
                for s in range(SLOTS):
                    round_hi(i + JOB_DOWN, s)
                    if s % 2 == 0:
                        f_high(i, s // 2, first)
                    if first:
                        up_steps(FF_GROUPS - 1, s)
                        if s == 6:
                            act.wait_ge(hidden_ready, FF_GROUPS)

            down_job(0, True)
            with act.Fori(1, FF_GROUPS) as i:
                down_job(i, False)

            for t in range(TOK):
                act.wait_ge(x3_ready, t + 1)
                act.activation(final_tmp[:, t, :], x2[:, t, :], ACT.Square,
                               accum_out=rms3[:, t:t + 1]).then_inc(squares3, 1)
                act.wait_ge(rms3_step, 3 * t + 1)
                act.activation(rms3[:, t:t + 1], rms3[:, t:t + 1], ACT.Sqrt).then_inc(rms3_step, 1)

        @block.vector
        def _(dve):
            def split_lo(j, s):
                dve.wait_ge(hi_ready[s], j + 1)
                dve.tensor_tensor(w_lo[:, s % SPLIT_SLOTS, :], raw[:, s, :], w_hi[:, s % SPLIT_SLOTS, :],
                                  ALU.subtract).then_inc(lo_ready[s], 1)

            steps = 0

            def step(ins):
                nonlocal steps
                steps += 1
                ins.then_inc(start_dve, 1)
                dve.wait_ge(start_dve, steps)

            dve.memset(ones[:], 1.0).then_inc(ones_ready, 1)
            step(dve.memset(c_parts[:].bitcast(F32), 0.0))
            dve.wait_ge(vecs_turned, 1)
            dve.tensor_copy(vecs[:, 0:64], ps[:, 5, 0:64]).then_inc(vecs_ready, 1)
            dve.wait_ge(vecs_ready, 1)
            dve.wait_ge(exp_c_ready, 1)
            step(dve.tensor_scalar(exp_c[:], exp_c[:], 1.0, None, ALU.add))
            step(dve.reciprocal(exp_c[:], exp_c[:]))
            step(dve.tensor_tensor(silu_c[:], vecs[:, V_C:V_C + 2 * KC], exp_c[:], ALU.mult))
            for st in range(2):
                part = c_parts[:, 0:4 * KC].rearrange("p (k f) -> p f k", f=4)
                step(dve.tensor_copy(part[:, 2 * st, :], silu_c[:, st * KC:(st + 1) * KC]))
                dve.tensor_tensor(part[:, 2 * st + 1, :], silu_c[:, st * KC:(st + 1) * KC], part[:, 2 * st, :],
                                  ALU.subtract).then_inc(c_ready, 1)
            dve.wait_ge(vecs_turned, 2)
            dve.tensor_copy(vecs[:, 64:512], ps[:, 6, 64:512]).then_inc(vecs_ready, 1)
            dve.tensor_copy(vecs[:, 512:513], ps[:, 7, 88:89]).then_inc(vecs_ready, 1)
            dve.wait_ge(vecs_ready, 3)
            dve.tensor_scalar(dng[:], vecs[:, V_DNG:V_DNG + 1], 1.0 - LAMBDA_INIT, None, ALU.mult)\
                .then_inc(vecs_ready, 1)
            dve.wait_ge(lam_landed, 16)
            for m in range(2):
                dve.tensor_tensor_reduce(lam_prod[:, m, :], lam_in[:, 2 * m * MAP_DIM:(2 * m + 1) * MAP_DIM],
                                         lam_in[:, (2 * m + 1) * MAP_DIM:(2 * m + 2) * MAP_DIM], 1.0, 0.0,
                                         ALU.mult, ALU.add, lam[:, m:m + 1]).then_inc(lam_step, 1)
            dve.wait_ge(lam_exp, 1)
            step(dve.tensor_tensor(lam[:, 0:1], lam[:, 1:2], lam[:, 0:1], ALU.subtract))
            dve.tensor_scalar(lam[:, 0:1], lam[:, 0:1], -LAMBDA_INIT, None, ALU.add).then_inc(lam_ready, 1)

            for j in range(JOB_NA):
                for s in range(SLOTS):
                    split_lo(j, s)
                if j == 4:
                    dve.wait_ge(squares1, 4)
                    dve.tensor_scalar(rms1[:], rms1[:], 1.0 / D, EPS, ALU.mult, ALU.add).then_inc(rms1_step, 1)
                if j == 5:
                    dve.wait_ge(rms1_step, 2)
                    dve.reciprocal(rms1[:], rms1[:]).then_inc(rms1_step, 1)
                    dve.wait_ge(rms1_step, 3)
                if j in (5, 6):
                    for t in (2 * j - 10, 2 * j - 9):
                        dve.tensor_scalar(tokens[:, t, :], tokens[:, t, :], rms1[:, t:t + 1], None, ALU.mult)\
                            .then_inc(normed1, 1)

            def modulation1():
                sums = ps[:, 3, 0:4 * KC].rearrange("p (m k s) -> p m s k", m=2, s=2)
                b_shift = vecs[:, V_ADAB:V_ADAB + KC].unsqueeze(1).to_broadcast([P, 2, KC])
                b_scale = vecs[:, V_ADAB + KC:V_ADAB + 2 * KC].unsqueeze(1).to_broadcast([P, 2, KC])
                g = vecs[:, V_N1:V_N1 + KC].unsqueeze(1).to_broadcast([P, 2, KC])
                dve.wait_ge(mod_cols_ready, 1)
                dve.wait_ge(vecs_ready, 4)
                dve.tensor_tensor(shift1[:], sums[:, 0], b_shift, ALU.add).then_inc(mod1_step, 1)
                dve.tensor_tensor(gain1[:], sums[:, 1], b_scale, ALU.add).then_inc(mod1_step, 1)
                dve.wait_ge(mod1_step, 2)
                dve.scalar_tensor_tensor(gain1[:], gain1[:], 1.0, g, ALU.add, ALU.mult).then_inc(mod1_ready, 1)

            def split_modulated(kc):
                dve.wait_ge(modulated_ready, 2 * kc + 2)
                dve.tensor_copy(hT[:, :, 0, kc, :], modulated[:, kc % 4, :, :]).then_inc(hT_hi_ready, 1)
                dve.wait_ge(hT_hi_ready, kc + 1)
                dve.tensor_tensor(hT[:, :, 1, kc, :], modulated[:, kc % 4, :, :], hT[:, :, 0, kc, :],
                                  ALU.subtract).then_inc(hT_ready, 1)

            def ada_step(g, kc):
                dve.wait_ge(ada_landed[kc % 4], 64 * g + 16 * (kc // 4) + 16)
                acc = ada_acc[:, g % 2, :]
                if kc == 0:
                    if g >= 2:
                        dve.wait_ge(mod_summed, g - 1)
                    dve.tensor_scalar(acc, ada_raw[:, 0, :], silu_c[:, 0:1], None, ALU.mult)\
                        .then_inc(ada_summed, 1)
                else:
                    dve.wait_ge(ada_summed, KC * g + kc)
                    dve.scalar_tensor_tensor(acc, ada_raw[:, kc % 4, :], silu_c[:, kc:kc + 1], acc,
                                             ALU.mult, ALU.add).then_inc(ada_summed, 1)

            def read_mod(g):
                b = ada_bank(g + JOB_NA + 1)
                dve.wait_ge(mod_summed, g + 1)
                dve.tensor_tensor(mod[:, 4 * g:4 * g + 4], ps[:, b, 0:4],
                                  vecs[:, V_ADAB + 2 * KC + 4 * g:V_ADAB + 2 * KC + 4 * g + 4],
                                  ALU.add).then_inc(mod_ready, 1)

            def read_result(j):
                kind, col = PROJECTIONS[j - JOB_NA]
                if kind != "q":
                    return
                g = (col // GROUP) % 2
                b = 4 * (j % 2)
                q = qT[:, TILES * g:TILES * (g + 1), :]
                dve.wait_ge(half_read, g + 1 + (2 if j >= JOB_DIFF else 0))
                dve.tensor_tensor(q, q, ps[:, b:b + 4, SEQ:2 * SEQ], ALU.add).then_inc(q_read, 1)

            def after_slot(j, s):
                g = j - JOB_NA
                if s == 3 and g >= 1 and j != JOB_MERGE:
                    read_mod(g - 1)
                if g < ADA_GROUPS:
                    ada_step(g, 2 * s)
                    ada_step(g, 2 * s + 1)

            for s in range(SPLIT_SLOTS):
                split_lo(JOB_NA, s)
            modulation1()
            for s in range(SLOTS):
                split_modulated(2 * s)
                split_modulated(2 * s + 1)
                if s < SPLIT_SLOTS:
                    split_lo(JOB_NA, s + SPLIT_SLOTS)
                after_slot(JOB_NA, s)
            for j in range(JOB_NA + 1, JOB_DIFF):
                for s in range(SLOTS):
                    split_lo(j, s)
                    if s == 3:
                        read_result(j - 1)
                    after_slot(j, s)
            for s in range(SPLIT_SLOTS):
                split_lo(JOB_DIFF, s)
            read_result(JOB_DIFF - 1)

            mask = consts[:, C_MASK:C_MASK + GRID_W].unsqueeze(1).to_broadcast([P, TOK * ROWS, GRID_W])

            def na_bias(n):
                h, t = divmod(n, TOK)
                if t == 0:
                    dve.wait_ge(bias_landed[h % 2], 64 * (h // 2 + 1))
                    b = bias[:, h % 2, :].rearrange("p (a b) -> p a b", b=GRID_W)
                    dve.tensor_tensor(b, b, mask, ALU.add).then_inc(bias_ready, 1)
                    dve.wait_ge(bias_ready, h + 1)
                dve.wait_ge(na_scored, n + 1)
                if n >= 3:
                    dve.wait_ge(na_turned, n - 2)
                dve.scalar_tensor_tensor(scores[:, n % 3, 0:SEQ], ps[:, n % 2, 0:SEQ], NA_SCALE,
                                         bias[:, h % 2, t * SEQ:(t + 1) * SEQ], ALU.mult, ALU.add)\
                    .then_inc(na_biased, 1)
                dve.wait_ge(na_biased, n + 1)
                dve.wait_ge(na_ctx_scaled, n + 1)
                dve.tensor_reduce(row_max[:, n % 3, 0:1], scores[:, n % 3, :], AX.X, ALU.max, negate=True)\
                    .then_inc(na_max, 1)

            def na_result(n):
                h, t = divmod(n, TOK)
                dve.wait_ge(na_summed, n + 1)
                dve.tensor_copy(aT[:, h, t * P:(t + 1) * P], ps[:, 4 + n % 2, 0:P]).then_inc(na_out, 1)

            N = HEADS * TOK
            na_bias(0)
            na_bias(1)
            for n in range(N):
                dve.wait_ge(na_exp, n + 1)
                dve.reciprocal(row_sum[:, n % 3, 0:1], row_sum[:, n % 3, 0:1]).then_inc(na_recip, 1)
                dve.wait_ge(na_recip, n + 1)
                dve.tensor_scalar(scores[:, n % 3, :], scores[:, n % 3, :], row_sum[:, n % 3, 0:1], None, ALU.mult)\
                    .then_inc(na_probs, 1)
                if n + 2 < N:
                    na_bias(n + 2)
                if n >= 1:
                    na_result(n - 1)
            na_result(N - 1)

            for j in range(JOB_DIFF, JOB_MERGE):
                for s in range(SLOTS):
                    if j > JOB_DIFF or s >= SPLIT_SLOTS:
                        split_lo(j, s)
                    if s == 3 and j > JOB_DIFF:
                        read_result(j - 1)
                    after_slot(j, s)
            for s in range(SPLIT_SLOTS):
                split_lo(JOB_MERGE, s)
            read_result(JOB_MERGE - 1)
            dve.wait_ge(aT_hi_ready, 1)
            dve.tensor_tensor(aT_lo[:], aT[:], aT_hi[:], ALU.subtract).then_inc(aT_ready, 1)
            dve.wait_ge(aT_ready, 1)

            cos = consts[:, C_COS:C_COS + SEQ]
            sin = consts[:, C_SIN:C_SIN + SEQ]

            def rope(h):
                dve.wait_ge(rotated, h + 1)
                for m, t in enumerate((kT, qT)):
                    dve.tensor_tensor(rope_tmp[:, h % 2, m, :], ps[:, 5, m * SEQ:(m + 1) * SEQ], sin, ALU.mult)\
                        .then_inc(rope_sin, 1)
                    dve.tensor_tensor(t[:, h, 0:SEQ], t[:, h, 0:SEQ], cos, ALU.mult).then_inc(rope_cos, 1)
                dve.wait_ge(rope_sin, 2 * h + 2)
                dve.wait_ge(rope_cos, 2 * h + 2)
                for m, t in enumerate((kT, qT)):
                    dve.tensor_tensor(t[:, h, 0:SEQ], t[:, h, 0:SEQ], rope_tmp[:, h % 2, m, :], ALU.add)\
                        .then_inc(roped, 1)

            def df_maxima(n):
                dve.wait_ge(df_scored, 2 * n + 2)
                dve.tensor_reduce(row_max[:, n % 3, :], ps[:, 2 * (n % 2):2 * (n % 2) + 2, :], AX.X, ALU.max,
                                  negate=True).then_inc(df_max, 1)
                dve.wait_ge(df_max, n + 1)
                dve.tensor_scalar(row_max[:, n % 3, :], row_max[:, n % 3, :], DIFF_SCALE, None, ALU.mult)\
                    .then_inc(df_bias, 1)

            rope(0)
            df_maxima(0)
            df_maxima(1)
            rope(1)
            for n in range(N):
                dve.wait_ge(df_exp, 2 * n + 2)
                dve.reciprocal(row_sum[:, n % 3, :], row_sum[:, n % 3, :]).then_inc(df_recip, 1)
                dve.wait_ge(df_recip, n + 1)
                dve.tensor_scalar(row_sum[:, n % 3, 1:2], row_sum[:, n % 3, 1:2], lam[:, 0:1], None, ALU.mult)\
                    .then_inc(df_lam, 1)
                dve.tensor_scalar(diff_e[:, n % 2, 0, :], diff_e[:, n % 2, 0, :], row_sum[:, n % 3, 0:1], None,
                                  ALU.mult).then_inc(df_first, 1)
                dve.wait_ge(df_lam, n + 1)
                dve.wait_ge(df_first, n + 1)
                dve.scalar_tensor_tensor(diff_e[:, n % 2, 0, :], diff_e[:, n % 2, 1, :], row_sum[:, n % 3, 1:2],
                                         diff_e[:, n % 2, 0, :], ALU.mult, ALU.add).then_inc(df_probs, 1)
                if n + 2 < N:
                    df_maxima(n + 2)
                if n % 2 == 0 and n // 2 + 2 < HEADS:
                    rope(n // 2 + 2)
            dve.wait_ge(df_out, N)
            read_mod(JOB_MERGE - JOB_NA - 1)
            dve.tensor_tensor(diff_sq[:], diff_o[:], diff_o[:], ALU.mult).then_inc(o_step, 1)
            dve.wait_ge(o_step, 1)
            dve.tensor_reduce(rms_o[:], diff_sq[:], AX.X, ALU.add).then_inc(o_step, 1)
            dve.wait_ge(o_step, 2)
            dve.tensor_scalar(rms_o[:], rms_o[:], 1.0 / HD, EPS, ALU.mult, ALU.add).then_inc(o_step, 1)
            dve.wait_ge(o_step, 4)
            dve.reciprocal(rms_o[:], rms_o[:]).then_inc(o_step, 1)
            dve.wait_ge(o_step, 5)
            dve.tensor_tensor(diff_o[:], diff_o[:], rms_o[:].unsqueeze(2).to_broadcast([P, HEADS * TOK, HD]),
                              ALU.mult).then_inc(o_normed, 1)
            dve.wait_ge(bT_hi_ready, 1)
            dve.tensor_tensor(bT_lo[:], bT[:], bT_hi[:], ALU.subtract).then_inc(bT_ready, 1)

            def merge_y(g, n):
                dve.wait_ge(used[7], 3 * g + JOB_MERGE + 3)
                dve.wait_ge(sig_a_ready, n)
                dve.wait_ge(sig_b_ready, n)
                if not (isinstance(g, int) and g == 0):
                    dve.wait_ge(y_turned, g)
                dve.tensor_tensor(y[:], ps[:, 4:6, :], sig_a[:], ALU.mult).then_inc(y_a, 1)
                dve.tensor_tensor(sig_b[:], ps[:, 6:8, :], sig_b[:], ALU.mult).then_inc(y_b, 1)
                dve.wait_ge(y_a, n)
                dve.wait_ge(y_b, n)
                dve.tensor_tensor(y[:], y[:], sig_b[:], ALU.add).then_inc(y_ready, 1)

            def turn_lo(g):
                dve.wait_ge(yT_hi_ready, g + 1)
                dve.tensor_tensor(yT_lo[:, bass.ds(g * TILES, TILES), :],
                                  ps[:, 4:6, :].rearrange("p a (b q) -> p (a b) q", b=2),
                                  yT_hi[:, bass.ds(g * TILES, TILES), :], ALU.subtract).then_inc(yT_ready, 1)

            def merge_group(g, first, ada_jobs):
                j = 3 * g + JOB_MERGE
                for s in range(SLOTS):
                    if not first or s >= SPLIT_SLOTS:
                        split_lo(j, s)
                    if s == 3 and not first:
                        merge_y(g - 1, g)
                    if ada_jobs > 0:
                        after_slot(j, s)
                if not first:
                    turn_lo(g - 1)
                for s in range(SLOTS):
                    split_lo(j + 1, s)
                    if ada_jobs > 1:
                        after_slot(j + 1, s)
                for s in range(SLOTS):
                    split_lo(j + 2, s)
                    if ada_jobs > 2:
                        after_slot(j + 2, s)

            merge_group(0, True, 3)
            merge_group(1, False, 2)
            with dve.Fori(2, D // GROUP) as g:
                merge_group(g, False, 0)

            def add_out(g):
                b = 2 * g
                dve.wait_ge(used[7], JOB_OUT + g + 1)
                dve.wait_ge(g1_ready, 1)
                rows = g1_rows[:, g * GROUP:(g + 1) * GROUP].unsqueeze(1).to_broadcast([P, TOK, GROUP])
                part = x2[:, :, g * GROUP:(g + 1) * GROUP]
                if g:
                    dve.wait_ge(x2_added, g)
                else:
                    dve.wait_ge(x2_landed, 16)
                dve.tensor_tensor(sig_a[:], ps[:, b:b + 2, :], rows, ALU.mult).then_inc(out_gated, 1)
                dve.wait_ge(out_gated, g + 1)
                dve.tensor_tensor(part, part, sig_a[:], ALU.add).then_inc(x2_added, 1)

            for g in range(4):
                for s in range(SLOTS):
                    split_lo(JOB_OUT + g, s)
                    if s == 3:
                        if g == 0:
                            merge_y(3, 4)
                        else:
                            add_out(g - 1)
                if g == 0:
                    turn_lo(3)
            for s in range(SPLIT_SLOTS):
                split_lo(JOB_UP, s)
            add_out(3)
            dve.tensor_scalar(gain2[:], mod[:, 2 * KC:3 * KC], 1.0, None, ALU.add).then_inc(gain2_ready, 1)
            dve.wait_ge(gain2_ready, 1)
            dve.tensor_tensor(gain2[:], gain2[:], vecs[:, V_N2:V_N2 + KC], ALU.mult).then_inc(gain2_ready, 1)
            dve.wait_ge(squares2, 4 * TOK)
            dve.tensor_reduce(rms2[:], ssq2[:], AX.X, ALU.add).then_inc(rms2_step, 1)
            dve.wait_ge(rms2_step, 1)
            dve.tensor_scalar(rms2[:], rms2[:], 1.0 / D, EPS, ALU.mult, ALU.add).then_inc(rms2_step, 1)
            dve.wait_ge(rms2_step, 3)
            dve.reciprocal(rms2[:], rms2[:]).then_inc(rms2_step, 1)
            dve.wait_ge(rms2_step, 4)
            for g in range(4):
                for t in range(TOK):
                    dve.tensor_scalar(x2_normed[:, t, g * GROUP:(g + 1) * GROUP],
                                      x2[:, t, g * GROUP:(g + 1) * GROUP], rms2[:, t:t + 1], None, ALU.mult)\
                        .then_inc(x2_norm_ready, 1)
            for m in range(KC // 2):
                dve.wait_ge(modulated2_ready, 2 * m + 2)
                dve.tensor_copy(h2T[:, 2 * m:2 * m + 2, 0, :], modulated2[:, m % 4, :, :])\
                    .then_inc(h2T_hi_ready, 1)
                dve.wait_ge(h2T_hi_ready, m + 1)
                dve.tensor_tensor(h2T[:, 2 * m:2 * m + 2, 1, :], modulated2[:, m % 4, :, :],
                                  h2T[:, 2 * m:2 * m + 2, 0, :], ALU.subtract).then_inc(h2T_ready, 1)
                if m < SPLIT_SLOTS:
                    split_lo(JOB_UP, m + SPLIT_SLOTS)

            def conv_sum(n, b):
                dve.wait_ge(up_half_read, n + 1)
                dve.tensor_tensor(conv_in[:], conv_in[:], ps[:, b:b + 4, SEQ:2 * SEQ], ALU.add)\
                    .then_inc(up_read, 1)

            def conv_sides(n, tile, dst):
                dve.wait_ge(conv_mid, TILES * n + TILES)
                for t in range(TILES):
                    dve.scalar_tensor_tensor(dst[:, t, 1:SEQ], conv_in[:, t, 0:SEQ - 1],
                                             vecs[:, bass.ds(tile + (V_CONV + t), 1)],
                                             dst[:, t, 1:SEQ], ALU.mult, ALU.add).then_inc(conv_left, 1)
                dve.wait_ge(conv_left, TILES * n + TILES)
                for t in range(TILES):
                    ins = dve.scalar_tensor_tensor(dst[:, t, 0:SEQ - 1], conv_in[:, t, 1:SEQ],
                                                   vecs[:, bass.ds(tile + (V_CONV + 176 + t), 1)],
                                                   dst[:, t, 0:SEQ - 1], ALU.mult, ALU.add)
                ins.then_inc(conv_done, 1)

            def gate_steps(i, s):
                n = 2 * i
                if s == 3:
                    conv_sum(n, 0)
                if s == 4:
                    conv_sides(n, TILES * i, conv_gate)

            def up_steps(i, s):
                n = 2 * i + 1
                if s == 3:
                    conv_sum(n, 4)
                if s == 4:
                    conv_sides(n, TILES * i + FF_TILES, conv_up)
                if s == 5:
                    dve.wait_ge(conv_done, n + 1)
                    dve.wait_ge(gate_done, i + 1)
                    dve.tensor_tensor(hidden[:, bass.ds(TILES * i, TILES), :], conv_gate[:], conv_up[:], ALU.mult)\
                        .then_inc(hidden_ready, 1)

            def ffn_pair(i, first):
                for s in range(SLOTS):
                    if not first:
                        split_lo(2 * i + JOB_UP, s)
                        up_steps(i - 1, s)
                for s in range(SLOTS):
                    split_lo(2 * i + JOB_UP + 1, s)
                    gate_steps(i, s)

            ffn_pair(0, True)
            with dve.Fori(1, FF_GROUPS) as i:
                ffn_pair(i, False)

            def down_job(i, first):
                for s in range(SLOTS):
                    split_lo(i + JOB_DOWN, s)
                    if s % 2 == 0:
                        t = s // 2
                        dve.wait_ge(f_hi_ready, TILES * i + t + 1)
                        dve.tensor_tensor(f_lo[:, t:t + 1, :], hidden[:, bass.ds(TILES * i + t, 1), :],
                                          f_hi[:, t:t + 1, :], ALU.subtract).then_inc(f_lo_ready, 1)
                    if first:
                        up_steps(FF_GROUPS - 1, s)

            down_job(0, True)
            with dve.Fori(1, FF_GROUPS) as i:
                down_job(i, False)

            dve.wait_ge(used[7], JOB_DOWN + FF_GROUPS)
            dve.wait_ge(g2_ready, 1)
            for t in range(TOK):
                sums = ps[:].rearrange("p (h t q) n -> p t h (q n)", h=2, t=TOK)[:, t]
                dve.tensor_tensor(final_tmp[:, t, :].rearrange("p (h m) -> p h m", h=2), sums,
                                  g2_rows[:].rearrange("p (h m) -> p h m", h=2), ALU.mult).then_inc(out3_gated, 1)
                dve.wait_ge(out3_gated, t + 1)
                dve.tensor_tensor(x2[:, t, :], x2[:, t, :], final_tmp[:, t, :], ALU.add).then_inc(x3_ready, 1)
            dve.wait_ge(final_landed, 16)
            for t in range(TOK):
                dve.wait_ge(squares3, t + 1)
                dve.tensor_scalar(rms3[:, t:t + 1], rms3[:, t:t + 1], 1.0 / D, EPS, ALU.mult, ALU.add)\
                    .then_inc(rms3_step, 1)
                dve.wait_ge(rms3_step, 3 * t + 2)
                dve.reciprocal(rms3[:, t:t + 1], rms3[:, t:t + 1]).then_inc(rms3_step, 1)
                dve.wait_ge(rms3_step, 3 * t + 3)
                dve.scalar_tensor_tensor(final_tmp[:, t, :], x2[:, t, :], rms3[:, t:t + 1], final_rows[:],
                                         ALU.mult, ALU.mult).then_inc(out_ready, 1)

        @block.tensor
        def _(pe):
            def take(j, s):
                pe.wait_ge(lo_ready[s], j + 1)

            def row4(s):
                return s % SPLIT_SLOTS

            pe.wait_ge(consts_landed, 16)
            pe.wait_ge(rows_landed, 64)
            pe.transpose(ps[:, 5, 0:64], param_rows[0:64, 0, :], consts[0:64, 0:64]).then_inc(vecs_turned, 1)
            pe.wait_ge(rows2_landed, 96)
            pe.transpose(ps[:, 6, V_ADAB:V_ADAB + 96], param_rows[0:96, 1, :], consts[0:96, 0:96])
            for tap in range(TAPS):
                pe.transpose(ps[:, 6, V_CONV + 88 * tap:V_CONV + 88 * (tap + 1)], param_rows[0:88, 2 + tap, :],
                             consts[0:88, 0:88])
            pe.transpose(ps[:, 6, V_CONVB:V_CONVB + 88], param_rows[0:88, 5, :], consts[0:88, 0:88])
            pe.transpose(ps[:, 7, 0:89], param_rows[0:89, 5, :], consts[0:89, 0:89]).then_inc(vecs_turned, 1)

            pe.wait_ge(c_ready, 2)
            for j in range(JOB_NA):
                if j == 6:
                    pe.wait_ge(vecs_ready, 3)
                for s in range(SLOTS):
                    take(j, s)
                    kc = SLOTS * (j % 2) + s
                    for half in range(2):
                        for w in (w_hi, w_lo):
                            mm = pe.matmul(ps[:, 2 * (j // 2) + half, :], c_parts[:, 4 * kc:4 * kc + P],
                                           w[:, row4(s), half * GROUP:(half + 1) * GROUP],
                                           start=(kc == 0 and w is w_hi), stop=(kc == KC - 1 and w is w_lo))
                    mm.then_inc(used[s], 1)
            pe.wait_ge(mod_rows_ready, 4)
            for n in range(2 * KC):
                mm = pe.matmul(ps[:, 3, 2 * n:2 * n + 2], mod_rows[:, n * P:(n + 1) * P],
                               consts[0:4, C_SEL:C_SEL + 2], start=True, stop=True)
            mm.then_inc(mod_cols_ready, 1)

            def turn_tokens(kc):
                for t in range(2 * TOK):
                    mm = pe.transpose(ps[:, 4 + kc % 4, t * P:(t + 1) * P], tokens[:, t, kc * P:(kc + 1) * P], ident)
                mm.then_inc(tokens_turned, 1)

            def sum_mod(j):
                g = j - JOB_NA - 1
                b = ada_bank(j)
                pe.wait_ge(ada_summed, KC * (g + 1))
                for n in range(TILES):
                    mm = pe.matmul(ps[:, b, n:n + 1], ada_acc[:, g % 2, n * P:(n + 1) * P], ones[:],
                                   start=True, stop=True)
                mm.then_inc(mod_summed, 1)

            def unit_k(s, b):
                for t in range(TILES):
                    for i in range(2):
                        kc = 2 * s + i
                        o = ps[:, b + t, :].rearrange("p (a n) -> p a n", a=2)
                        at = slice(i * GROUP + t * P, i * GROUP + (t + 1) * P)
                        pe.matmul(o, w_hi[:, row4(s), at], hT[:, :, 0, kc, :], start=(kc == 0), stop=False)
                        pe.matmul(o, w_hi[:, row4(s), at], hT[:, :, 1, kc, :], start=False, stop=False)
                        mm = pe.matmul(o, w_lo[:, row4(s), at], hT[:, :, 0, kc, :], start=False,
                                       stop=(kc == KC - 1))
                return mm

            def unit_paired(s, t, b, both, high):
                for i in range(2):
                    kc = 2 * s + i
                    o = ps[:, b + t, :].rearrange("p (a n) -> p a n", a=2)
                    at = slice(i * GROUP + t * P, i * GROUP + (t + 1) * P)
                    if kc == 0:
                        pe.matmul(o, w_hi[:, row4(s), at], both(kc), start=True, stop=False)
                        mm = pe.matmul(ps[:, b + t, 0:SEQ], w_lo[:, row4(s), at], high(kc), start=False, stop=False)
                    else:
                        pe.matmul(ps[:, b + t, 0:SEQ], w_lo[:, row4(s), at], high(kc), start=False, stop=False)
                        mm = pe.matmul(o, w_hi[:, row4(s), at], both(kc), start=False, stop=(kc == KC - 1))
                return mm

            def moving_weights(s, banks, stationary_hi, stationary_lo, kcs, last):
                for n, b in enumerate(banks):
                    for i, kc in enumerate(kcs):
                        at = slice(i * GROUP, (i + 1) * GROUP)
                        hi, lo = stationary_hi(kc, n), stationary_lo(kc, n)
                        pe.matmul(ps[:, b, :], hi, w_hi[:, row4(s), at], start=(kc == 0), stop=False)
                        pe.matmul(ps[:, b, :], hi, w_lo[:, row4(s), at], start=False, stop=False)
                        mm = pe.matmul(ps[:, b, :], lo, w_hi[:, row4(s), at], start=False, stop=(kc == last))
                return mm

            def tok(part):
                return lambda kc, n: hT[:, n // TOK, part, kc, (n % TOK) * P:(n % TOK + 1) * P]

            def projection(j):
                kind, _ = PROJECTIONS[j - JOB_NA]
                b = 4 * (j % 2)
                if j >= JOB_NA + 2:
                    pe.wait_ge(*results_read(j - 2))
                if j > JOB_NA:
                    sum_mod(j)
                for s in range(SLOTS):
                    if j == JOB_NA:
                        pe.wait_ge(hT_ready, 2 * s + 2)
                        for kc in (2 * s + 4, 2 * s + 5):
                            if kc < KC:
                                turn_tokens(kc)
                    take(j, s)
                    if kind == "k":
                        if s == 0 and j > JOB_NA:
                            pe.wait_ge(mod_ready, j - JOB_NA)
                        mm = unit_k(s, b)
                    elif kind == "v":
                        if s == 0:
                            pe.wait_ge(mod_ready, j - JOB_NA)
                        mm = moving_weights(s, range(b, b + 4), tok(0), tok(1), (2 * s, 2 * s + 1), KC - 1)
                    else:
                        for t in range(TILES):
                            if s == 0 and t == 3:
                                pe.wait_ge(mod_ready, j - JOB_NA)
                            mm = unit_paired(s, t, b, lambda kc: hT[:, 0, :, kc, :], lambda kc: hT[:, 0, 0, kc, :])
                    mm.then_inc(used[s], 1)

            pe.wait_ge(normed1, 4)
            for kc in range(4):
                turn_tokens(kc)
            pe.wait_ge(mod1_ready, 1)
            for j in range(JOB_NA, JOB_DIFF):
                projection(j)

            pe.wait_ge(*results_read(JOB_DIFF - 2))
            pe.wait_ge(*results_read(JOB_DIFF - 1))
            N = HEADS * TOK

            def na_scores(n):
                h, t = divmod(n, TOK)
                if n >= 2:
                    pe.wait_ge(na_biased, n - 1)
                    pe.wait_ge(na_ctx_scaled, n - 1)
                for b, keys in ((0, slice(0, SEQ)), (6, slice(SEQ, 2 * SEQ))):
                    mm = pe.matmul(ps[:, b + n % 2, 0:SEQ], qT[:, h, t * P:(t + 1) * P], kT[:, h, keys],
                                   start=True, stop=True)
                mm.then_inc(na_scored, 1)

            def na_turn(n):
                pe.wait_ge(na_probs, n + 1)
                if n >= 2:
                    pe.wait_ge(na_pT_ready, n - 1)
                for k in range(2 * TOK):
                    mm = pe.transpose(ps[:, 2 + n % 2, k * P:(k + 1) * P], scores[:, n % 3, k * P:(k + 1) * P], ident)
                mm.then_inc(na_turned, 1)

            def na_values(n):
                h = n // TOK
                pe.wait_ge(na_pT_ready, n + 1)
                if n >= 2:
                    pe.wait_ge(na_out, n - 1)
                for k in range(2 * TOK):
                    mm = pe.matmul(ps[:, 4 + n % 2, 0:P], v_sb[:, k, h * HD:(h + 1) * HD], na_pT[:, k, :],
                                   start=(k == 0), stop=(k == 2 * TOK - 1))
                mm.then_inc(na_summed, 1)

            na_scores(0)
            na_scores(1)
            for n in range(N):
                if n + 2 < N:
                    na_scores(n + 2)
                if n:
                    na_values(n - 1)
                na_turn(n)
            na_values(N - 1)
            pe.wait_ge(na_out, N)
            pe.wait_ge(na_pT_ready, N)

            for j in range(JOB_DIFF, JOB_MERGE):
                projection(j)
            pe.wait_ge(*results_read(JOB_MERGE - 2))
            pe.wait_ge(*results_read(JOB_MERGE - 1))

            def rotate(h):
                if h:
                    pe.wait_ge(rope_sin, 2 * h)
                rot = consts[:, C_ROT:C_ROT + P]
                pe.matmul(ps[:, 5, 0:SEQ], rot, kT[:, h, 0:SEQ], start=True, stop=True)
                pe.matmul(ps[:, 5, SEQ:2 * SEQ], rot, qT[:, h, :], start=True, stop=True).then_inc(rotated, 1)

            def df_scores(n):
                h, t = divmod(n, TOK)
                pe.wait_ge(roped, 2 * h + 2)
                if n >= 2:
                    pe.wait_ge(df_exp, 2 * n - 2)
                for m in range(2):
                    half = slice(m * MAP_DIM, (m + 1) * MAP_DIM)
                    pe.matmul(ps[:, 2 * (n % 2) + m, :], qT[half, h, t * P:(t + 1) * P], kT[half, h, :],
                              start=True, stop=True).then_inc(df_scored, 1)

            def df_turn(n):
                pe.wait_ge(df_probs, n + 1)
                if n >= 1:
                    pe.wait_ge(df_pT_ready, n)
                for k in range(2 * TOK):
                    mm = pe.transpose(ps[:, 4, k * P:(k + 1) * P], diff_e[:, n % 2, 0, k * P:(k + 1) * P],
                                      ident)
                mm.then_inc(df_turned, 1)

            def df_values(n):
                h = n // TOK
                pe.wait_ge(df_pT_ready, n + 1)
                if n >= 2:
                    pe.wait_ge(df_out, n - 1)
                for k in range(2 * TOK):
                    mm = pe.matmul(ps[:, 6 + n % 2, 0:P], diff_pT[:, n % 2, k, :],
                                   v_sb[:, k, h * HD:(h + 1) * HD], start=(k == 0), stop=(k == 2 * TOK - 1))
                mm.then_inc(df_summed, 1)

            rotate(0)
            df_scores(0)
            df_scores(1)
            rotate(1)
            for n in range(N):
                if n + 2 < N:
                    df_scores(n + 2)
                if n % 2 == 0 and n // 2 + 2 < HEADS:
                    rotate(n // 2 + 2)
                if n:
                    df_values(n - 1)
                df_turn(n)
            df_values(N - 1)

            def part(t):
                return lambda kc, n: t[:, kc, n * P:(n + 1) * P]

            def spread(n, col, b):
                for kc in range(KC):
                    mm = pe.matmul(ps[:, b + kc // 4, (kc % 4) * P:(kc % 4 + 1) * P],
                                   mod[:, col + kc:col + kc + 1].to_broadcast([P, P]), ident,
                                   start=True, stop=True)
                mm.then_inc(n, 1)

            def turn_y(g):
                pe.wait_ge(y_ready, g + 1)
                for n in range(TILES):
                    for t in range(TOK):
                        at = ((n % 2) * TOK + t) * P
                        mm = pe.transpose(ps[:, 4 + n // 2, at:at + P], y[:, t, n * P:(n + 1) * P], ident)
                mm.then_inc(y_turned, 1)

            def merge_group(g, first, ada_jobs):
                j = 3 * g + JOB_MERGE
                if first:
                    pe.wait_ge(df_out, HEADS * TOK)
                    sum_mod(j)
                if not first:
                    pe.wait_ge(sig_a_ready, g)
                for s in range(SLOTS):
                    take(j, s)
                    moving_weights(s, (0, 1), tok(0), tok(1), (2 * s, 2 * s + 1), KC - 1).then_inc(used[s], 1)
                    if s == 3:
                        if first:
                            pe.wait_ge(mod_ready, j - JOB_NA)
                            pe.wait_ge(o_normed, 1)
                            for n in range(HEADS * TOK):
                                mm = pe.transpose(ps[:, 4 + n // 4, (n % 4) * P:(n % 4 + 1) * P], diff_o[:, n, :],
                                                  ident)
                            mm.then_inc(o_turned, 1)
                        else:
                            turn_y(g - 1)
                            if ada_jobs > 0:
                                sum_mod(j)
                if not first:
                    pe.wait_ge(sig_b_ready, g)
                if ada_jobs > 1:
                    if first:
                        pe.wait_ge(bT_scaled, 1)
                    sum_mod(j + 1)
                for s in range(SLOTS):
                    take(j + 1, s)
                    moving_weights(s, (2, 3), tok(0), tok(1), (2 * s, 2 * s + 1), KC - 1).then_inc(used[s], 1)
                    if s == 3 and first:
                        pe.wait_ge(mod_ready, j + 1 - JOB_NA)
                        spread(g1_spread, 0, 4)
                if first:
                    pe.wait_ge(g1_ready, 1)
                    pe.wait_ge(bT_ready, 1)
                    pe.wait_ge(aT_ready, 1)
                else:
                    pe.wait_ge(yT_ready, g)
                if ada_jobs > 2:
                    sum_mod(j + 2)
                    pe.wait_ge(mod_ready, j + 2 - JOB_NA)
                elif ada_jobs > 0:
                    pe.wait_ge(mod_ready, ADA_GROUPS)
                for s in range(SLOTS):
                    take(j + 2, s)
                    kcs = (2 * (s % 4), 2 * (s % 4) + 1)
                    if s < 4:
                        mm = moving_weights(s, (4, 5), part(aT_hi), part(aT_lo), kcs, HEADS - 1)
                    else:
                        mm = moving_weights(s, (6, 7), part(bT_hi), part(bT_lo), kcs, HEADS - 1)
                    mm.then_inc(used[s], 1)

            merge_group(0, True, 3)
            merge_group(1, False, 2)
            with pe.Fori(2, D // GROUP) as g:
                merge_group(g, False, 0)

            for g in range(4):
                if g == 0:
                    pe.wait_ge(sig_a_ready, 4)
                if g == 1:
                    pe.wait_ge(sig_b_ready, 4)
                if g == 2:
                    pe.wait_ge(yT_ready, 4)
                for s in range(SLOTS):
                    if g == 0 and s == 6:
                        pe.wait_ge(yT_ready, 4)
                    elif g == 0 and s == 0:
                        pe.wait_ge(yT_ready, 3)
                    take(JOB_OUT + g, s)
                    moving_weights(s, (2 * g, 2 * g + 1), part(yT_hi), part(yT_lo), (2 * s, 2 * s + 1), KC - 1)\
                        .then_inc(used[s], 1)
                    if g == 0 and s == 3:
                        turn_y(3)
            pe.wait_ge(x2_added, 2)
            spread(g2_spread, 3 * KC, 0)

            def turn_x2(m):
                for h in range(2):
                    kc = 2 * m + h
                    for t in range(TOK):
                        at = (h * TOK + t) * P
                        mm = pe.transpose(ps[:, 4 + m % 4, at:at + P], x2_normed[:, t, kc * P:(kc + 1) * P], ident)
                mm.then_inc(x2_turned, 1)

            for m in range(4):
                pe.wait_ge(x2_norm_ready, TOK * (m // 2 + 1))
                turn_x2(m)
            pe.wait_ge(g2_ready, 1)

            def both(kc):
                return h2T[:, kc, :, :]

            def high(kc):
                return h2T[:, kc, 0, :]

            def up_job(n, b, ready):
                for s in range(SLOTS):
                    if ready:
                        pe.wait_ge(h2T_ready, s + 1)
                    take(n + JOB_UP, s)
                    for t in range(TILES):
                        mm = unit_paired(s, t, b, both, high)
                    mm.then_inc(used[s], 1)
                    if ready and s + 4 < KC // 2:
                        pe.wait_ge(modulated2_ready, 2 * s + 2)
                        pe.wait_ge(x2_norm_ready, TOK * ((s + 4) // 2 + 1))
                        turn_x2(s + 4)

            up_job(0, 0, True)
            pe.wait_ge(modulated2_ready, KC)
            up_job(1, 4, False)
            with pe.Fori(1, FF_GROUPS) as i:
                for half in range(2):
                    pe.wait_ge(up_read, 2 * i + half - 1)
                    up_job(2 * i + half, 4 * half, False)

            def down_job(i, first, last):
                for s in range(SLOTS):
                    take(i + JOB_DOWN, s)
                    t, half = divmod(s, 2)
                    if half == 0:
                        pe.wait_ge(f_lo_ready, TILES * i + t + 1)
                    if first and s < 2:
                        pe.wait_ge(up_read, 2 * FF_GROUPS - 1 + s)
                    for n in range(TOK):
                        for q in range(2):
                            b = 4 * half + 2 * n + q
                            at = slice(q * GROUP, (q + 1) * GROUP)
                            hi, lo = f_hi[:, t, n * P:(n + 1) * P], f_lo[:, t, n * P:(n + 1) * P]
                            pe.matmul(ps[:, b, :], hi, w_hi[:, row4(s), at], start=(first and t == 0), stop=False)
                            pe.matmul(ps[:, b, :], hi, w_lo[:, row4(s), at], start=False, stop=False)
                            mm = pe.matmul(ps[:, b, :], lo, w_hi[:, row4(s), at], start=False,
                                           stop=(last and t == 3))
                    mm.then_inc(used[s], 1)

            down_job(0, True, False)
            with pe.Fori(1, FF_GROUPS - 1) as i:
                down_job(i, False, False)
            down_job(FF_GROUPS - 1, False, True)


_INS = ["x", "c", "ctx", "c_ctx", "ada_w", "ada_b", "norm1_g", "w_in", "na_rpb", "diff_lambda", "diff_norm_g",
        "w_branch_a", "w_branch_b", "w_out", "norm2_g", "ffn_w_up", "ffn_conv_w", "ffn_conv_b", "ffn_w_down",
        "final_norm_g"]


def kernel(**inputs):
    import concourse.bacc as bacc
    from concourse.bass_utils import run_bass_kernel_spmd

    nc = bacc.Bacc("TRN2", target_bir_lowering=False, num_devices=1)
    arrays, args = {}, []
    for name in _INS:
        a = np.ascontiguousarray(inputs[name])
        arrays[f"in_{name}"] = a
        args.append(nc.dram_tensor(f"in_{name}", a.shape, F32, kind="ExternalInput").ap())
    arrays["in_constants"] = shape_constants()
    args.append(nc.dram_tensor("in_constants", (P, C_ALL), F32, kind="ExternalInput").ap())
    result = nc.dram_tensor("out_0", (1, SEQ, D), F32, kind="ExternalOutput").ap()
    block_program(nc, *args, result)
    r = run_bass_kernel_spmd(nc, [arrays], core_ids=[0])
    return r.results[0]["out_0"]
```

```python
import math
from contextlib import ExitStack

import numpy as np

import concourse.bass as bass
from concourse import mybir

F32 = mybir.dt.float32
F32R = mybir.dt.float32r
ACT = mybir.ActivationFunctionType
ALU = mybir.AluOpType
AX = mybir.AxisListType

P = 128
D = 2048
SEQ = 256
GRID_W = 64
ROWS = SEQ // GRID_W
HEADS = 8
HD = 128
WIDTH = HEADS * HD
WIN_ROWS = 8
WIN_COLS = 16
RPB_ROWS = 2 * WIN_ROWS - 1
RPB_COLS = 2 * WIN_COLS - 1
RPB_MARGIN = WIN_COLS
RPB_BLOCK = GRID_W * GRID_W + 2 * RPB_MARGIN
ZERO_PARTS = 8
MAP_DIM = 64
D_FF = 5632
TAPS = 3
EPS = 1e-6
LAMBDA_INIT = 0.8 - 0.6 * math.exp(0.0)
NA_SCALE = HD ** -0.5
DIFF_SCALE = MAP_DIM ** -0.5
MASKED = -1e30

KC = D // P
TOK = SEQ // P
UNIT = 1024
GROUP = 512
TILES = GROUP // P
SLOTS = 8
SPLIT_SLOTS = 4
ADA_SLOTS = 4
FF_TILES = D_FF // P
FF_GROUPS = D_FF // GROUP

QA, KA, VA, QB, KB, VB = (n * WIDTH for n in range(6))
GATE_A = 6 * WIDTH
GATE_B = GATE_A + D

JOB_NA = 8
JOB_DIFF = 14
JOB_MERGE = 20
JOB_OUT = 32
JOB_UP = 36
JOB_DOWN = JOB_UP + 2 * FF_GROUPS
PROJECTIONS = [("k", KA), ("k", KA + GROUP), ("v", VA), ("v", VA + GROUP), ("q", QA), ("q", QA + GROUP),
               ("k", KB), ("k", KB + GROUP), ("v", VB), ("v", VB + GROUP), ("q", QB), ("q", QB + GROUP)]
ADA_JOBS = [9, 9, 10, 10, 11, 11, 12, 13, 14, 14, 15, 15, 16, 16, 17, 17]
ADA_GROUPS = len(ADA_JOBS)
ADA_BEFORE_NA = sum(j < JOB_DIFF for j in ADA_JOBS)
ADA_FIRST_COL = 2 * D

C_IDENT, C_ROT, C_COS, C_SIN, C_MASK, C_SEL = 0, 128, 256, 512, 768, 832
C_ALL = 834
V_C, V_CC, V_N1, V_N2, V_ADAB, V_CONV, V_CONVB, V_DNG = 0, 16, 32, 48, 64, 160, 424, 512
V_ALL = 513


def shape_constants():
    k = np.zeros((P, C_ALL), np.float32)
    k[:, C_IDENT:C_IDENT + P] = np.eye(P)
    quarter = MAP_DIM // 4
    for m in range(P // MAP_DIM):
        for pair in range(2):
            a = m * MAP_DIM + 2 * pair * quarter
            for j in range(quarter):
                k[a + quarter + j, C_ROT + a + j] = -1.0
                k[a + j, C_ROT + a + quarter + j] = 1.0
    t = np.arange(SEQ)
    inv = (np.float32(10000.0) ** (-np.arange(quarter, dtype=np.float32) / np.float32(quarter))).astype(np.float32)
    ang_r = (t // GRID_W).astype(np.float32)[:, None] * inv[None]
    ang_c = (t % GRID_W).astype(np.float32)[:, None] * inv[None]
    ang = np.concatenate([ang_r, ang_r, ang_c, ang_c], axis=1).T
    k[:, C_COS:C_COS + SEQ] = np.tile(np.cos(ang), (2, 1))
    k[:, C_SIN:C_SIN + SEQ] = np.tile(np.sin(ang), (2, 1))
    col = np.arange(P) % GRID_W
    start = np.clip(col - WIN_COLS // 2, 0, GRID_W - WIN_COLS)[:, None]
    key = np.arange(GRID_W)[None]
    k[:, C_MASK:C_MASK + GRID_W] = np.where((key >= start) & (key < start + WIN_COLS), 0.0, MASKED)
    k[0:2, C_SEL] = 1.0
    k[2:4, C_SEL + 1] = 1.0
    return k


def block_program(nc, x, c, ctx, c_ctx, ada_w, ada_b, norm1_g, w_in, na_rpb, diff_lambda, diff_norm_g,
                  w_branch_a, w_branch_b, w_out, norm2_g, ffn_w_up, ffn_conv_w, ffn_conv_b, ffn_w_down,
                  final_norm_g, constants, out):
    base = nc.sbuf_base + (-nc.sbuf_base) % 64
    kb = 1024

    def place(name, at, shape, dtype=F32):
        return nc.alloc_sbuf_tensor_at(name, shape, dtype, offset=base + at)

    raw = place("raw", 0, [P, SLOTS, UNIT])
    w_hi = place("w_hi", 32 * kb, [P, SPLIT_SLOTS, UNIT], F32R)
    w_lo = place("w_lo", 48 * kb, [P, SPLIT_SLOTS, UNIT], F32R)
    lat, con = 64 * kb, 96 * kb
    hT = place("hT", lat, [P, 2, 2, KC, SEQ], F32R)
    junk = place("junk", lat, [P, D])
    h2T = place("h2T", lat, [P, KC, 2, SEQ], F32R)
    aT_hi = place("aT_hi", con, [P, HEADS, SEQ], F32R)
    aT_lo = place("aT_lo", con + 8 * kb, [P, HEADS, SEQ], F32R)
    bT_hi = place("bT_hi", con + 16 * kb, [P, HEADS, SEQ], F32R)
    bT_lo = place("bT_lo", con + 24 * kb, [P, HEADS, SEQ], F32R)
    rope_tmp = place("rope_tmp", con + 16 * kb, [P, 2, 2, SEQ])
    g2_rows = place("g2_rows", con, [P, D])
    final_rows = place("final_rows", con + 8 * kb, [P, D])
    conv_in = place("conv_in", con + 16 * kb, [P, TILES, SEQ])
    conv_gate = place("conv_gate", con + 20 * kb, [P, TILES, SEQ])
    conv_up = place("conv_up", con + 24 * kb, [P, TILES, SEQ])
    arena = 128 * kb
    tokens = place("tokens", arena, [P, 2 * TOK, D])
    modulated = place("modulated", arena + 32 * kb, [P, 4, 2, SEQ])
    kT = place("kT", arena, [P, HEADS, 2 * SEQ])
    v_sb = place("v_sb", arena + 16 * kb, [P, 2 * TOK, WIDTH])
    qT = place("qT", arena + 32 * kb, [P, HEADS, SEQ])
    bias = place("bias", arena + 40 * kb, [P, 2, TOK * SEQ])
    diff_pT = place("diff_pT", arena + 40 * kb, [P, 2, 2 * TOK, P])
    yT_hi = place("yT_hi", arena, [P, KC, SEQ], F32R)
    yT_lo = place("yT_lo", arena + 16 * kb, [P, KC, SEQ], F32R)
    g1_rows = place("g1_rows", arena + 32 * kb, [P, D])
    y = place("y", arena + 40 * kb, [P, TOK, GROUP])
    x2_normed = place("x2_normed", arena, [P, TOK, D])
    modulated2 = place("modulated2", arena + 16 * kb, [P, 4, 2, SEQ])
    hidden = place("hidden", arena, [P, FF_TILES, SEQ])
    att = 172 * kb
    aT = place("aT", att, [P, HEADS, SEQ])
    diff_o = place("diff_o", att, [P, HEADS * TOK, HD])
    ada_acc = place("ada_acc", att + 8 * kb, [P, 2, GROUP])
    ada_raw = place("ada_raw", att + 12 * kb, [P, ADA_SLOTS, 2, GROUP])
    mod_rows = place("mod_rows", att, [4, 2 * D])
    x2 = place("x2", att, [P, TOK, D])
    tmp = 192 * kb
    param_rows = place("param_rows", tmp, [P, 6, P])
    scores = place("scores", tmp, [P, 3, 2 * SEQ])
    na_pT = place("na_pT", tmp + 6 * kb, [P, 2 * TOK, P])
    diff_e = place("diff_e", tmp, [P, 2, 2, 2 * SEQ])
    diff_sq = place("diff_sq", tmp, [P, HEADS * TOK, HD])
    bT = place("bT", tmp, [P, HEADS, SEQ])
    sig_a = place("sig_a", tmp, [P, TOK, GROUP])
    sig_b = place("sig_b", tmp + 4 * kb, [P, TOK, GROUP])
    f_hi = place("f_hi", tmp, [P, SPLIT_SLOTS, SEQ], F32R)
    f_lo = place("f_lo", tmp + 4 * kb, [P, SPLIT_SLOTS, SEQ], F32R)
    squares_out = place("squares_out", lat, [P, UNIT])
    final_tmp = place("final_tmp", con + 16 * kb, [P, TOK, D])
    at = 200 * kb

    def keep(name, shape, dtype=F32):
        nonlocal at
        t = place(name, at, shape, dtype)
        at += (4 * int(np.prod(shape[1:])) + 31) // 32 * 32
        return t

    consts = keep("consts", [P, C_ALL])
    vecs = keep("vecs", [P, V_ALL])
    c_parts = keep("c_parts", [P, 4 * KC + P], F32R)
    silu_c = keep("silu_c", [P, 2 * KC])
    exp_c = keep("exp_c", [P, 2 * KC])
    gain1 = keep("gain1", [P, 2, KC])
    shift1 = keep("shift1", [P, 2, KC])
    mod = keep("mod", [P, 4 * ADA_GROUPS])
    gain2 = keep("gain2", [P, KC])
    ones = keep("ones", [P, 1])
    rms1 = keep("rms1", [P, 2 * TOK])
    row_max = keep("row_max", [P, 3, 2])
    row_sum = keep("row_sum", [P, 3, 2])
    lam = keep("lam", [P, 2])
    warm = keep("warm", [P, 1])
    rms_o = keep("rms_o", [P, HEADS * TOK])
    dng = keep("dng", [P, 1])
    ssq2 = keep("ssq2", [P, TOK, 4])
    rms2 = keep("rms2", [P, TOK])
    ssq3 = keep("ssq3", [P, TOK, 2])
    rms3 = keep("rms3", [P, TOK])
    lam_in = place("lam_in", lat + 8 * kb, [P, 4 * MAP_DIM])
    lam_prod = place("lam_prod", lat + 9 * kb, [P, 2, MAP_DIM])
    zeros = place("zeros", arena + 40 * kb, [HEADS * RPB_ROWS, RPB_BLOCK // ZERO_PARTS])
    ident = consts[:, C_IDENT:C_IDENT + P]

    rpb_grid = nc.dram_tensor("rpb_grid", [HEADS * RPB_ROWS, RPB_BLOCK], F32)

    ps = nc.alloc_psum_tensor("ps", [P, 8, GROUP], F32)

    with ExitStack() as es:
        def sem(name):
            return es.enter_context(nc.semaphore(name))

        def sems(name, n):
            return [sem(f"{name}{i}") for i in range(n)]

        raw_landed = sems("raw_landed", SLOTS)
        hi_ready = sems("hi_ready", SLOTS)
        lo_ready = sems("lo_ready", SLOTS)
        used = sems("used", SLOTS)
        consts_landed = sem("consts_landed")
        rows_landed = sem("rows_landed")
        rows2_landed = sem("rows2_landed")
        tokens_landed = sem("tokens_landed")
        vecs_turned = sem("vecs_turned")
        vecs_ready = sem("vecs_ready")
        exp_c_ready = sem("exp_c_ready")
        start_dve = sem("start_dve")
        ones_ready = sem("ones_ready")
        c_ready = sem("c_ready")
        lam_landed = sem("lam_landed")
        lam_step = sem("lam_step")
        lam_exp = sem("lam_exp")
        lam_ready = sem("lam_ready")
        squares1 = sem("squares1")
        rms1_step = sem("rms1_step")
        normed1 = sem("normed1")
        mod_rows_ready = sem("mod_rows_ready")
        mod_cols_ready = sem("mod_cols_ready")
        mod1_step = sem("mod1_step")
        mod1_ready = sem("mod1_ready")
        tokens_turned = sem("tokens_turned")
        modulated_ready = sem("modulated_ready")
        hT_hi_ready = sem("hT_hi_ready")
        hT_ready = sem("hT_ready")
        ada_landed = sems("ada_landed", ADA_SLOTS)
        ada_summed = sem("ada_summed")
        mod_summed = sem("mod_summed")
        mod_ready = sem("mod_ready")
        half_read = sem("half_read")
        kv_read = sem("kv_read")
        q_read = sem("q_read")
        zeros_ready = sem("zeros_ready")
        padded = sem("padded")
        bias_landed = sems("bias_landed", 2)
        bias_ready = sem("bias_ready")
        na_scored = sem("na_scored")
        na_ctx_scaled = sem("na_ctx_scaled")
        na_biased = sem("na_biased")
        na_max = sem("na_max")
        na_exp = sem("na_exp")
        na_recip = sem("na_recip")
        na_probs = sem("na_probs")
        na_turned = sem("na_turned")
        na_pT_ready = sem("na_pT_ready")
        na_summed = sem("na_summed")
        na_out = sem("na_out")
        aT_hi_ready = sem("aT_hi_ready")
        aT_ready = sem("aT_ready")
        rotated = sem("rotated")
        rope_cos = sem("rope_cos")
        rope_sin = sem("rope_sin")
        roped = sem("roped")
        df_scored = sem("df_scored")
        df_max = sem("df_max")
        df_bias = sem("df_bias")
        df_exp = sem("df_exp")
        df_recip = sem("df_recip")
        df_lam = sem("df_lam")
        df_first = sem("df_first")
        df_probs = sem("df_probs")
        df_turned = sem("df_turned")
        df_pT_ready = sem("df_pT_ready")
        df_summed = sem("df_summed")
        df_out = sem("df_out")
        o_step = sem("o_step")
        o_normed = sem("o_normed")
        o_turned = sem("o_turned")
        bT_scaled = sem("bT_scaled")
        bT_hi_ready = sem("bT_hi_ready")
        bT_ready = sem("bT_ready")
        g1_spread = sem("g1_spread")
        g1_ready = sem("g1_ready")
        sig_a_ready = sem("sig_a_ready")
        sig_b_ready = sem("sig_b_ready")
        y_a = sem("y_a")
        y_b = sem("y_b")
        y_ready = sem("y_ready")
        y_turned = sem("y_turned")
        yT_hi_ready = sem("yT_hi_ready")
        yT_ready = sem("yT_ready")
        x2_landed = sem("x2_landed")
        out_gated = sem("out_gated")
        x2_added = sem("x2_added")
        squares2 = sem("squares2")
        rms2_step = sem("rms2_step")
        x2_norm_ready = sem("x2_norm_ready")
        gain2_ready = sem("gain2_ready")
        g2_spread = sem("g2_spread")
        g2_ready = sem("g2_ready")
        x2_turned = sem("x2_turned")
        modulated2_ready = sem("modulated2_ready")
        h2T_hi_ready = sem("h2T_hi_ready")
        h2T_ready = sem("h2T_ready")
        up_half_read = sem("up_half_read")
        up_read = sem("up_read")
        conv_mid = sem("conv_mid")
        conv_left = sem("conv_left")
        conv_done = sem("conv_done")
        gate_done = sem("gate_done")
        hidden_ready = sem("hidden_ready")
        f_hi_ready = sem("f_hi_ready")
        f_lo_ready = sem("f_lo_ready")
        final_landed = sem("final_landed")
        out3_gated = sem("out3_gated")
        x3_ready = sem("x3_ready")
        squares3 = sem("squares3")
        rms3_step = sem("rms3_step")
        x3_weighted = sem("x3_weighted")
        out_ready = sem("out_ready")
        out1_ready = sem("out1_ready")
        out_stored = sem("out_stored")

        block = es.enter_context(nc.Block())

        w_in_v = w_in[0].rearrange("(k p) n -> p k n", p=P)
        ada_v = ada_w[0].rearrange("(k p) n -> p k n", p=P)
        pa_v = w_branch_a[0].rearrange("(k p) n -> p k n", p=P)
        pb_v = w_branch_b[0].rearrange("(k p) n -> p k n", p=P)
        out_v = w_out[0].rearrange("(k p) n -> p k n", p=P)
        up_v = ffn_w_up[0].rearrange("(k p) n -> p k n", p=P)
        down_v = ffn_w_down[0].rearrange("(k p) n -> p k n", p=P)

        def results_read(j):
            mine = PROJECTIONS[j - JOB_NA][0] == "q"
            n = sum((kind == "q") == mine for kind, _ in PROJECTIONS[:j - JOB_NA + 1])
            return (q_read if mine else kv_read), n

        def ada_groups(j):
            return [g for g, job in enumerate(ADA_JOBS) if job == j]

        def ada_bank(j):
            return 4 * (j % 2) + 3

        def rotation(n):
            if n < 4:
                return kT, 2 * n, 4 + n
            return qT, 2 * (n - 4), (n - 4 if n < 6 else 5)

        LATE_ROTATIONS = {1: 6, 3: 7}

        def is_first(j):
            return isinstance(j, int) and j == 0

        @block.sync
        def _(sp):
            def load(j, s, src, parts=2):
                if not is_first(j):
                    sp.wait_ge(lo_ready[s], j)
                dst = raw[:, s, :].rearrange("p (a n) -> p a n", a=parts)
                sp.dma_start(dst, src).then_inc(raw_landed[s], 16)

            sp.dma_start(consts[:], constants).then_inc(consts_landed, 16)
            sp.dma_start(param_rows[0:16, 0, :], c.rearrange("a (k p) -> (a k) p", p=P)).then_inc(rows_landed, 16)
            sp.dma_start(param_rows[16:32, 0, :], c_ctx.rearrange("(k p) -> k p", p=P)).then_inc(rows_landed, 16)
            sp.dma_start(param_rows[32:48, 0, :],
                         norm1_g.rearrange("a (k p) -> (a k) p", p=P)).then_inc(rows_landed, 16)
            sp.dma_start(param_rows[48:64, 0, :],
                         norm2_g.rearrange("a (k p) -> (a k) p", p=P)).then_inc(rows_landed, 16)
            for j in range(JOB_NA):
                for s in range(SLOTS):
                    kc = SLOTS * (j % 2) + s
                    load(j, s, ada_v[:, kc:kc + 1, UNIT * (j // 2):UNIT * (j // 2) + UNIT], parts=1)
                if j == 1:
                    sp.dma_start(tokens[:, 0:TOK, :],
                                 x[0].rearrange("(t p) n -> p t n", p=P)).then_inc(tokens_landed, 16)
                    sp.dma_start(tokens[:, TOK:2 * TOK, :],
                                 ctx[0].rearrange("(t p) n -> p t n", p=P)).then_inc(tokens_landed, 16)
            for n, (_, col) in enumerate(PROJECTIONS):
                for s in range(SLOTS):
                    load(JOB_NA + n, s, w_in_v[:, 2 * s:2 * s + 2, col:col + GROUP])
            with sp.Fori(1, D // GROUP + 1) as g:
                jobs = [sp.snap(3 * g + (JOB_MERGE - 3 + n)) for n in range(3)]
                cols = [g * GROUP + (col - GROUP) for col in (GATE_A, GATE_B, 0)]
                for n in range(2):
                    for s in range(SLOTS):
                        load(jobs[n], s, w_in_v[:, 2 * s:2 * s + 2, bass.ds(cols[n], GROUP)])
                col = cols[2]
                for s in range(SLOTS):
                    src = (pa_v, pb_v)[s // 4]
                    load(jobs[2], s, src[:, 2 * (s % 4):2 * (s % 4) + 2, bass.ds(col, GROUP)])
            with sp.Fori(1, D // GROUP + 1) as g:
                job, col = sp.snap(g + (JOB_OUT - 1)), g * GROUP - GROUP
                for s in range(SLOTS):
                    load(job, s, out_v[:, 2 * s:2 * s + 2, bass.ds(col, GROUP)])
            with sp.Fori(1, FF_GROUPS + 1) as g:
                jobs = [sp.snap(2 * g + (JOB_UP - 2 + half)) for half in range(2)]
                cols = [g * GROUP + (half * D_FF - GROUP) for half in range(2)]
                for half in range(2):
                    for s in range(SLOTS):
                        load(jobs[half], s, up_v[:, 2 * s:2 * s + 2, bass.ds(cols[half], GROUP)])
            with sp.Fori(1, FF_GROUPS) as g:
                job = sp.snap(g + (JOB_DOWN - 1))
                rows = [TILES * g + (t - TILES) for t in range(TILES)]
                for s in range(SLOTS):
                    load(job, s, down_v[:, bass.ds(rows[s // 2], 1), UNIT * (s % 2):UNIT * (s % 2) + UNIT],
                         parts=1)
            for s in range(SLOTS):
                row, half = FF_TILES - TILES + s % TILES, s // TILES
                load(JOB_DOWN + FF_GROUPS - 1, s, down_v[:, row:row + 1, UNIT * half:UNIT * (half + 1)], parts=1)
            for half in range(2):
                at = slice(half * UNIT, (half + 1) * UNIT)
                for t, ready in enumerate((out_ready, out1_ready)):
                    sp.wait_ge(ready, half + 1)
                    sp.dma_start(out[0, t * P:(t + 1) * P, at], final_tmp[:, t, at]).then_inc(out_stored, 16)
            sp.wait_ge(out_stored, 16 * 2 * TOK)

        @block.gpsimd
        def _(pool):
            pool.memset(zeros[:], 0.0).then_inc(zeros_ready, 1)
            pool.dma_start(lam_in[:], diff_lambda.rearrange("a m d -> a (m d)").to_broadcast([P, 4 * MAP_DIM]))\
                .then_inc(lam_landed, 16)

            def load_ada(g, skip_wait=False, between=lambda pair: None):
                for pair in range(KC // 2):
                    if not (skip_wait and pair < ADA_SLOTS):
                        pool.wait_ge(ada_summed, KC * g + 2 * (pair - ADA_SLOTS + 1))
                    pool.dma_start(ada_raw[:, pair % ADA_SLOTS, :, :],
                                   ada_v[:, 2 * pair:2 * pair + 2, bass.ds(g * GROUP + ADA_FIRST_COL, GROUP)])\
                        .then_inc(ada_landed[pair % ADA_SLOTS], 16)
                    between(pair)

            pool.wait_ge(mod_cols_ready, 2)
            pool.wait_ge(zeros_ready, 1)
            pool.dma_start(rpb_grid.ap().rearrange("p (a n) -> p a n", a=ZERO_PARTS),
                           zeros[:].unsqueeze(1)
                           .to_broadcast([HEADS * RPB_ROWS, ZERO_PARTS, RPB_BLOCK // ZERO_PARTS]))\
                .then_inc(padded, 16)

            def scatter_bias(pair):
                if pair == ADA_SLOTS - 1:
                    pool.wait_ge(padded, 16)
                    pool.dma_start(bass.AP(rpb_grid, RPB_MARGIN - (WIN_COLS - 1),
                                           [[RPB_BLOCK, HEADS * RPB_ROWS], [GRID_W + 1, GRID_W], [1, RPB_COLS]]),
                                   na_rpb[0].rearrange("h r w -> (h r) w").unsqueeze(1)
                                   .to_broadcast([HEADS * RPB_ROWS, GRID_W, RPB_COLS])).then_inc(padded, 16)

            load_ada(0, skip_wait=True, between=scatter_bias)
            pool.wait_ge(padded, 32)

            def load_bias(h, r):
                src = bass.AP(rpb_grid, (h * RPB_ROWS + WIN_ROWS - 1 - r) * RPB_BLOCK + RPB_MARGIN,
                              [[GRID_W, GRID_W], [RPB_BLOCK, ROWS], [1, GRID_W]])
                dst = bias[(r % 2) * GRID_W:(r % 2 + 1) * GRID_W, h % 2,
                           (r // 2) * SEQ:(r // 2 + 1) * SEQ].rearrange("p (a b) -> p a b", a=ROWS)
                pool.dma_start(dst, src).then_inc(bias_landed[h % 2], 16)

            def load_first_biases(pair):
                load_bias(pair // ROWS, pair % ROWS)

            pool.wait_ge(hT_ready, KC)
            load_ada(1, between=load_first_biases)
            with pool.Fori(2, ADA_BEFORE_NA) as g:
                load_ada(g)
            for h in range(2, HEADS):
                pool.wait_ge(na_biased, TOK * (h - 1))
                for r in range(ROWS):
                    load_bias(h, r)
            pool.wait_ge(na_out, HEADS * TOK)
            with pool.Fori(ADA_BEFORE_NA, ADA_GROUPS) as g:
                load_ada(g)
            pool.wait_ge(mod_ready, ADA_GROUPS)
            pool.wait_ge(bT_ready, 1)
            pool.dma_start(x2[:], x[0].rearrange("(t p) n -> p t n", p=P)).then_inc(x2_landed, 16)
            pool.wait_ge(used[7], JOB_OUT)
            pool.dma_start(final_rows[:], final_norm_g.rearrange("(a n) -> a n", a=1).to_broadcast([P, D]))\
                .then_inc(final_landed, 16)

        @block.scalar
        def _(act):
            def round_hi(j, s):
                act.wait_ge(raw_landed[s], 16 * j + 16)
                if s >= SPLIT_SLOTS:
                    act.wait_ge(used[s - SPLIT_SLOTS], j + 1)
                elif not is_first(j):
                    act.wait_ge(used[s + SPLIT_SLOTS], j)
                act.copy(w_hi[:, s % SPLIT_SLOTS, :], raw[:, s, :]).then_inc(hi_ready[s], 1)

            def warm_up(func):
                act.activation(warm[:], ones[:], func)

            act.dma_start(param_rows[0:96, 1, :], ada_b.rearrange("a (k p) -> (a k) p", p=P))\
                .then_inc(rows2_landed, 16)
            for tap in range(TAPS):
                act.dma_start(param_rows[0:88, 2 + tap, :],
                              ffn_conv_w[0, tap:tap + 1, :].rearrange("a (k p) -> (a k) p", p=P))\
                    .then_inc(rows2_landed, 16)
            act.dma_start(param_rows[0:88, 5, :], ffn_conv_b.rearrange("a (k p) -> (a k) p", p=P))\
                .then_inc(rows2_landed, 16)
            act.dma_start(param_rows[88:89, 5, :], diff_norm_g).then_inc(rows2_landed, 16)
            act.wait_ge(vecs_ready, 1)
            act.activation(exp_c[:], vecs[:, V_C:V_C + 2 * KC], ACT.Exp, scale=-1.0).then_inc(exp_c_ready, 1)
            act.wait_ge(lam_step, 2)
            act.activation(lam[:], lam[:], ACT.Exp).then_inc(lam_exp, 1)

            def read_mod_rows(g):
                act.wait_ge(used[7], 2 * g + 2)
                b = 2 * (g % 2)
                act.copy(mod_rows[:, g * UNIT:(g + 1) * UNIT].rearrange("p (a n) -> p a n", a=2),
                         ps[0:4, b:b + 2, :]).then_inc(mod_rows_ready, 1)

            for j in range(JOB_NA):
                for s in range(SLOTS):
                    round_hi(j, s)
                    if s == 2 and j % 2 == 0 and j:
                        read_mod_rows(j // 2 - 1)
                    if j in (3, 4) and s in (1, 5):
                        t = 2 * (j - 3) + s // 4
                        act.wait_ge(tokens_landed, 32)
                        if t == 0:
                            act.wait_ge(lam_step, 2)
                        else:
                            act.wait_ge(squares1, t)
                        act.activation(junk[:], tokens[:, t, :], ACT.Square,
                                       accum_out=rms1[:, t:t + 1]).then_inc(squares1, 1)
                if j == 5:
                    act.wait_ge(rms1_step, 1)
                    act.activation(rms1[:], rms1[:], ACT.Sqrt).then_inc(rms1_step, 1)

            def modulate(kc):
                act.wait_ge(tokens_turned, kc + 1)
                if kc >= 4:
                    act.wait_ge(hT_ready, kc - 3)
                for st in range(2):
                    act.activation(modulated[:, kc % 4, st, :], ps[:, 4 + kc % 4, st * SEQ:(st + 1) * SEQ],
                                   ACT.Identity, bias=shift1[:, st, kc:kc + 1],
                                   scale=gain1[:, st, kc:kc + 1]).then_inc(modulated_ready, 1)

            def read_result(j):
                kind, col = PROJECTIONS[j - JOB_NA]
                g = (col // GROUP) % 2
                b = 4 * (j % 2)
                act.wait_ge(used[7], j + 1)
                if kind == "k":
                    act.copy(kT[:, TILES * g:TILES * (g + 1), :], ps[:, b:b + 4, :]).then_inc(kv_read, 1)
                elif kind == "v":
                    act.copy(v_sb[:, :, g * GROUP:(g + 1) * GROUP], ps[:, b:b + 4, :])\
                        .then_inc(kv_read, 1)
                else:
                    act.copy(qT[:, TILES * g:TILES * (g + 1), :], ps[:, b:b + 4, 0:SEQ]).then_inc(half_read, 1)

            for s in range(SPLIT_SLOTS):
                round_hi(JOB_NA, s)
            read_mod_rows(3)
            act.wait_ge(mod1_ready, 1)
            for kc in range(4):
                modulate(kc)
            for s in range(SLOTS):
                for kc in (2 * s + 4, 2 * s + 5):
                    if kc < KC:
                        modulate(kc)
                if s < SPLIT_SLOTS:
                    round_hi(JOB_NA, s + SPLIT_SLOTS)
            for j in range(JOB_NA + 1, JOB_DIFF):
                for s in range(SLOTS):
                    round_hi(j, s)
                    if s == 3:
                        read_result(j - 1)
            for s in range(SPLIT_SLOTS - 1):
                round_hi(JOB_DIFF, s)

            def scale_ctx(n):
                act.wait_ge(na_scored, n + 1)
                if n >= 3:
                    act.wait_ge(na_turned, n - 2)
                act.mul(scores[:, n % 3, SEQ:2 * SEQ], ps[:, 2 + n % 2, 0:SEQ], NA_SCALE)\
                    .then_inc(na_ctx_scaled, 1)

            def na_exponent(n):
                act.wait_ge(na_max, n + 1)
                act.activation(scores[:, n % 3, :], scores[:, n % 3, :], ACT.Exp, bias=row_max[:, n % 3, 0:1],
                               accum_out=row_sum[:, n % 3, 0:1]).then_inc(na_exp, 1)

            N = HEADS * TOK
            warm_up(ACT.Exp)
            act.wait_ge(ada_summed, KC * ADA_BEFORE_NA)
            scale_ctx(0)
            read_result(JOB_DIFF - 1)
            scale_ctx(1)
            na_exponent(0)
            for n in range(N):
                if n + 2 < N:
                    scale_ctx(n + 2)
                if n + 1 < N:
                    na_exponent(n + 1)
                act.wait_ge(na_turned, n + 1)
                if n >= 1:
                    act.wait_ge(na_summed, n)
                act.copy(na_pT[:], ps[:, 6 + n % 2, :].rearrange("p (a b) -> p a b", a=4)).then_inc(na_pT_ready, 1)

            for j in range(JOB_DIFF, JOB_MERGE):
                for s in range(SLOTS):
                    if j > JOB_DIFF or s >= SPLIT_SLOTS - 1:
                        round_hi(j, s)
                    if s == 3 and j > JOB_DIFF:
                        read_result(j - 1)
                    if s == 4 and j == JOB_MERGE - 1:
                        act.wait_ge(na_out, HEADS * TOK)
                        act.copy(aT_hi[:], aT[:]).then_inc(aT_hi_ready, 1)
            for s in range(SPLIT_SLOTS - 1):
                round_hi(JOB_MERGE, s)
            read_result(JOB_MERGE - 1)

            def df_exponents(n):
                act.wait_ge(df_bias, n + 1)
                if n >= 2:
                    act.wait_ge(df_turned, n - 1)
                for m in range(2):
                    act.activation(diff_e[:, n % 2, m, :], ps[:, 2 * (n % 2) + m, :], ACT.Exp,
                                   bias=row_max[:, n % 3, m:m + 1], scale=DIFF_SCALE,
                                   accum_out=row_sum[:, n % 3, m:m + 1]).then_inc(df_exp, 1)

            warm_up(ACT.Exp)
            act.wait_ge(ada_summed, KC * ADA_GROUPS)
            df_exponents(0)
            for n in range(N):
                if n + 1 < N:
                    df_exponents(n + 1)
                act.wait_ge(df_turned, n + 1)
                if n >= 2:
                    act.wait_ge(df_summed, n - 1)
                act.copy(diff_pT[:, n % 2, :, :], ps[:, 4, :].rearrange("p (a b) -> p a b", a=4))\
                    .then_inc(df_pT_ready, 1)
                if n >= 1:
                    act.wait_ge(df_summed, n)
                    act.copy(diff_o[:, n - 1, :], ps[:, 6 + (n - 1) % 2, 0:P]).then_inc(df_out, 1)
            act.wait_ge(df_summed, N)
            act.copy(diff_o[:, N - 1, :], ps[:, 6 + (N - 1) % 2, 0:P]).then_inc(df_out, 1)
            for s in (SPLIT_SLOTS - 1, SPLIT_SLOTS):
                round_hi(JOB_MERGE, s)
            act.wait_ge(o_step, 3)
            act.activation(rms_o[:], rms_o[:], ACT.Sqrt).then_inc(o_step, 1)

            for s in range(SPLIT_SLOTS + 1, SLOTS):
                round_hi(JOB_MERGE, s)
            for s in range(2):
                round_hi(JOB_MERGE + 1, s)
            act.wait_ge(o_turned, 1)
            act.mul(bT[:].rearrange("p h q -> p (h q)"), ps[:, 4:8, :].rearrange("p a n -> p (a n)"), dng[:])\
                .then_inc(bT_scaled, 1)
            act.wait_ge(bT_scaled, 1)
            act.copy(bT_hi[:], bT[:]).then_inc(bT_hi_ready, 1)

            def turn_hi(g):
                act.wait_ge(y_turned, g + 1)
                act.copy(yT_hi[:, bass.ds(g * TILES, TILES), :],
                         ps[:, 4:6, :].rearrange("p a (b q) -> p (a b) q", b=2)).then_inc(yT_hi_ready, 1)

            def merge_group(g, first):
                j = 3 * g + JOB_MERGE
                if not first:
                    for s in range(SLOTS):
                        round_hi(j, s)
                    turn_hi(g - 1)
                for s in range(SLOTS):
                    if not first or s >= 2:
                        round_hi(j + 1, s)
                    if s == 3:
                        act.wait_ge(used[7], j + 1)
                        if not first:
                            act.wait_ge(y_a, g)
                        else:
                            act.wait_ge(bT_ready, 1)
                        act.activation(sig_a[:], ps[:, 0:2, :], ACT.Sigmoid).then_inc(sig_a_ready, 1)
                if first:
                    act.wait_ge(g1_spread, 1)
                    act.copy(g1_rows[:], ps[:, 4:8, :].rearrange("p a n -> p (a n)")).then_inc(g1_ready, 1)
                for s in range(SLOTS):
                    round_hi(j + 2, s)
                    if s == 3:
                        act.wait_ge(used[7], j + 2)
                        if not first:
                            act.wait_ge(y_ready, g)
                        act.activation(sig_b[:], ps[:, 2:4, :], ACT.Sigmoid).then_inc(sig_b_ready, 1)

            merge_group(0, True)
            with act.Fori(1, D // GROUP) as g:
                merge_group(g, False)

            def square_group(g):
                for t in range(TOK):
                    act.wait_ge(x2_added, g + 1)
                    if g or t:
                        act.wait_ge(squares2, TOK * g + t)
                    act.activation(sig_b[:, t, :], x2[:, t, g * GROUP:(g + 1) * GROUP], ACT.Square,
                                   accum_out=ssq2[:, t, g:g + 1]).then_inc(squares2, 1)

            for g in range(4):
                for s in range(SLOTS):
                    round_hi(JOB_OUT + g, s)
                    if s == 4 and g:
                        square_group(g - 1)
                if g == 0:
                    turn_hi(3)
            for s in range(SPLIT_SLOTS):
                round_hi(JOB_UP, s)
            warm_up(ACT.Sqrt)
            square_group(3)
            act.wait_ge(rms2_step, 2)
            act.activation(rms2[:], rms2[:], ACT.Sqrt).then_inc(rms2_step, 1)
            act.wait_ge(g2_spread, 1)
            act.copy(g2_rows[:], ps[:, 0:4, :].rearrange("p a n -> p (a n)")).then_inc(g2_ready, 1)
            act.wait_ge(gain2_ready, 2)

            def modulate2(m):
                act.wait_ge(x2_turned, m + 1)
                if m >= 4:
                    act.wait_ge(h2T_ready, m - 3)
                for h in range(2):
                    kc = 2 * m + h
                    act.activation(modulated2[:, m % 4, h, :], ps[:, 4 + m % 4, h * SEQ:(h + 1) * SEQ],
                                   ACT.Identity, bias=mod[:, KC + kc:KC + kc + 1],
                                   scale=gain2[:, kc:kc + 1]).then_inc(modulated2_ready, 1)

            for m in range(4):
                modulate2(m)
            for s in range(SPLIT_SLOTS):
                modulate2(s + 4)
                round_hi(JOB_UP, s + SPLIT_SLOTS)

            def conv_begin(n, b):
                act.wait_ge(used[7], n + JOB_UP + 1)
                if not is_first(n):
                    act.wait_ge(conv_done, n)
                act.copy(conv_in[:], ps[:, b:b + 4, 0:SEQ]).then_inc(up_half_read, 1)

            def conv_middle(n, tile, dst):
                act.wait_ge(up_read, n + 1)
                for t in range(TILES):
                    act.activation(dst[:, t, :], conv_in[:, t, :], ACT.Identity,
                                   bias=vecs[:, bass.ds(tile + (V_CONVB + t), 1)],
                                   scale=vecs[:, bass.ds(tile + (V_CONV + 88 + t), 1)]).then_inc(conv_mid, 1)

            def gate_steps(i, s):
                n = 2 * i
                if s == 3:
                    conv_begin(n, 0)
                if s == 4:
                    if not is_first(i):
                        act.wait_ge(hidden_ready, i)
                    conv_middle(n, TILES * i, conv_gate)
                if s == 6:
                    act.wait_ge(conv_done, n + 1)
                    act.activation(conv_gate[:], conv_gate[:], ACT.Silu).then_inc(gate_done, 1)

            def up_steps(i, s):
                n = 2 * i + 1
                if s == 3:
                    conv_begin(n, 4)
                if s == 4:
                    conv_middle(n, TILES * i + FF_TILES, conv_up)

            def ffn_pair(i, first):
                for s in range(SLOTS):
                    if not first:
                        round_hi(2 * i + JOB_UP, s)
                        up_steps(i - 1, s)
                for s in range(SLOTS):
                    round_hi(2 * i + JOB_UP + 1, s)
                    gate_steps(i, s)

            ffn_pair(0, True)
            with act.Fori(1, FF_GROUPS) as i:
                ffn_pair(i, False)

            def f_high(i, t, first):
                if not first:
                    act.wait_ge(used[2 * t + 1], i + JOB_DOWN)
                act.copy(f_hi[:, t:t + 1, :], hidden[:, bass.ds(TILES * i + t, 1), :])\
                    .then_inc(f_hi_ready, 1)

            def down_job(i, first, last=False):
                for s in range(SLOTS):
                    round_hi(i + JOB_DOWN, s)
                    if last and s < TILES:
                        f_high(i, s, first)
                    if not last and s % 2 == 0:
                        f_high(i, s // 2, first)
                    if first:
                        up_steps(FF_GROUPS - 1, s)
                        if s == 6:
                            act.wait_ge(hidden_ready, FF_GROUPS)

            down_job(0, True)
            with act.Fori(1, FF_GROUPS - 1) as i:
                down_job(i, False)
            down_job(FF_GROUPS - 1, False, last=True)

            warm_up(ACT.Sqrt)
            for half in range(2):
                for t in range(TOK):
                    if half or t:
                        act.wait_ge(squares3, TOK * half + t)
                    act.wait_ge(x3_ready, TOK * half + t + 1)
                    act.activation(squares_out[:], x2[:, t, half * UNIT:(half + 1) * UNIT], ACT.Square,
                                   accum_out=ssq3[:, t, half:half + 1]).then_inc(squares3, 1)
            act.wait_ge(rms3_step, 2)
            act.activation(rms3[:], rms3[:], ACT.Sqrt).then_inc(rms3_step, 1)
            act.wait_ge(rms3_step, 4)
            for half in range(2):
                act.wait_ge(x3_weighted, 2 * half + 2)
                part = final_tmp[:, 1, half * UNIT:(half + 1) * UNIT]
                act.mul(part, part, rms3[:, 1:2]).then_inc(out1_ready, 1)

        @block.vector
        def _(dve):
            def split_lo(j, s):
                dve.wait_ge(hi_ready[s], j + 1)
                dve.tensor_tensor(w_lo[:, s % SPLIT_SLOTS, :], raw[:, s, :], w_hi[:, s % SPLIT_SLOTS, :],
                                  ALU.subtract).then_inc(lo_ready[s], 1)

            steps = 0

            def step(ins):
                nonlocal steps
                steps += 1
                ins.then_inc(start_dve, 1)
                dve.wait_ge(start_dve, steps)

            dve.memset(ones[:], 1.0).then_inc(ones_ready, 1)
            step(dve.memset(c_parts[:].bitcast(F32), 0.0))
            dve.wait_ge(vecs_turned, 1)
            dve.tensor_copy(vecs[:, 0:64], ps[:, 5, 0:64]).then_inc(vecs_ready, 1)
            dve.wait_ge(vecs_ready, 1)
            dve.wait_ge(exp_c_ready, 1)
            step(dve.tensor_scalar(exp_c[:], exp_c[:], 1.0, None, ALU.add))
            step(dve.reciprocal(exp_c[:], exp_c[:]))
            step(dve.tensor_tensor(silu_c[:], vecs[:, V_C:V_C + 2 * KC], exp_c[:], ALU.mult))
            for st in range(2):
                part = c_parts[:, 0:4 * KC].rearrange("p (k f) -> p f k", f=4)
                step(dve.tensor_copy(part[:, 2 * st, :], silu_c[:, st * KC:(st + 1) * KC]))
                dve.tensor_tensor(part[:, 2 * st + 1, :], silu_c[:, st * KC:(st + 1) * KC], part[:, 2 * st, :],
                                  ALU.subtract).then_inc(c_ready, 1)
            dve.wait_ge(vecs_turned, 2)
            dve.tensor_copy(vecs[:, 64:512], ps[:, 6, 64:512]).then_inc(vecs_ready, 1)
            dve.tensor_copy(vecs[:, 512:513], ps[:, 7, 88:89]).then_inc(vecs_ready, 1)
            dve.wait_ge(vecs_ready, 3)
            dve.tensor_scalar(dng[:], vecs[:, V_DNG:V_DNG + 1], 1.0 - LAMBDA_INIT, None, ALU.mult)\
                .then_inc(vecs_ready, 1)
            dve.wait_ge(lam_landed, 16)
            for m in range(2):
                dve.tensor_tensor_reduce(lam_prod[:, m, :], lam_in[:, 2 * m * MAP_DIM:(2 * m + 1) * MAP_DIM],
                                         lam_in[:, (2 * m + 1) * MAP_DIM:(2 * m + 2) * MAP_DIM], 1.0, 0.0,
                                         ALU.mult, ALU.add, lam[:, m:m + 1]).then_inc(lam_step, 1)
            dve.wait_ge(lam_exp, 1)
            step(dve.tensor_tensor(lam[:, 0:1], lam[:, 1:2], lam[:, 0:1], ALU.subtract))
            dve.tensor_scalar(lam[:, 0:1], lam[:, 0:1], -LAMBDA_INIT, None, ALU.add).then_inc(lam_ready, 1)

            for j in range(JOB_NA):
                for s in range(SLOTS):
                    split_lo(j, s)
                if j == 4:
                    dve.wait_ge(squares1, 4)
                    dve.tensor_scalar(rms1[:], rms1[:], 1.0 / D, EPS, ALU.mult, ALU.add).then_inc(rms1_step, 1)
                if j == 5:
                    dve.wait_ge(rms1_step, 2)
                    dve.reciprocal(rms1[:], rms1[:]).then_inc(rms1_step, 1)
                    dve.wait_ge(rms1_step, 3)
                if j in (5, 6):
                    for t in (2 * j - 10, 2 * j - 9):
                        dve.tensor_scalar(tokens[:, t, :], tokens[:, t, :], rms1[:, t:t + 1], None, ALU.mult)\
                            .then_inc(normed1, 1)

            def modulation1():
                sums = ps[:, 0, 0:4 * KC].rearrange("p (m k s) -> p m s k", m=2, s=2)
                b_shift = vecs[:, V_ADAB:V_ADAB + KC].unsqueeze(1).to_broadcast([P, 2, KC])
                b_scale = vecs[:, V_ADAB + KC:V_ADAB + 2 * KC].unsqueeze(1).to_broadcast([P, 2, KC])
                g = vecs[:, V_N1:V_N1 + KC].unsqueeze(1).to_broadcast([P, 2, KC])
                dve.wait_ge(mod_cols_ready, 2)
                dve.wait_ge(vecs_ready, 4)
                dve.tensor_tensor(shift1[:], sums[:, 0], b_shift, ALU.add).then_inc(mod1_step, 1)
                dve.tensor_tensor(gain1[:], sums[:, 1], b_scale, ALU.add).then_inc(mod1_step, 1)
                dve.wait_ge(mod1_step, 2)
                dve.scalar_tensor_tensor(gain1[:], gain1[:], 1.0, g, ALU.add, ALU.mult).then_inc(mod1_ready, 1)

            def split_modulated(kc):
                dve.wait_ge(modulated_ready, 2 * kc + 2)
                dve.tensor_copy(hT[:, :, 0, kc, :], modulated[:, kc % 4, :, :]).then_inc(hT_hi_ready, 1)
                dve.wait_ge(hT_hi_ready, kc + 1)
                dve.tensor_tensor(hT[:, :, 1, kc, :], modulated[:, kc % 4, :, :], hT[:, :, 0, kc, :],
                                  ALU.subtract).then_inc(hT_ready, 1)

            def ada_step(g, kc):
                slot, turns = kc // 2 % ADA_SLOTS, KC // 2 // ADA_SLOTS
                dve.wait_ge(ada_landed[slot], 16 * (turns * g + kc // 2 // ADA_SLOTS + 1))
                raw_columns = ada_raw[:, slot, kc % 2, :]
                acc = ada_acc[:, g % 2, :]
                if kc == 0:
                    if g >= 2:
                        dve.wait_ge(mod_summed, g - 1)
                    dve.tensor_scalar(acc, raw_columns, silu_c[:, 0:1], None, ALU.mult)\
                        .then_inc(ada_summed, 1)
                else:
                    dve.wait_ge(ada_summed, KC * g + kc)
                    dve.scalar_tensor_tensor(acc, raw_columns, silu_c[:, kc:kc + 1], acc,
                                             ALU.mult, ALU.add).then_inc(ada_summed, 1)

            def read_mod(j):
                groups = ada_groups(j - 1)
                if groups:
                    first, n = 4 * groups[0], 4 * len(groups)
                    dve.wait_ge(mod_summed, groups[-1] + 1)
                    dve.tensor_tensor(mod[:, first:first + n], ps[:, ada_bank(j), 0:n],
                                      vecs[:, V_ADAB + 2 * KC + first:V_ADAB + 2 * KC + first + n],
                                      ALU.add).then_inc(mod_ready, len(groups))

            def read_result(j):
                kind, col = PROJECTIONS[j - JOB_NA]
                if kind != "q":
                    return
                g = (col // GROUP) % 2
                b = 4 * (j % 2)
                q = qT[:, TILES * g:TILES * (g + 1), :]
                dve.wait_ge(half_read, g + 1 + (2 if j >= JOB_DIFF else 0))
                dve.tensor_tensor(q, q, ps[:, b:b + 4, SEQ:2 * SEQ], ALU.add).then_inc(q_read, 1)

            def ada_steps(j, s):
                steps = [(g, kc) for g in ada_groups(j) for kc in range(KC)]
                n = len(steps) // SLOTS
                for g, kc in steps[s * n:(s + 1) * n]:
                    ada_step(g, kc)

            for s in range(SPLIT_SLOTS):
                split_lo(JOB_NA, s)
            modulation1()
            for kc in range(4):
                split_modulated(kc)
            for s in range(SLOTS):
                for kc in (2 * s + 4, 2 * s + 5):
                    if kc < KC:
                        split_modulated(kc)
                if s < SPLIT_SLOTS:
                    split_lo(JOB_NA, s + SPLIT_SLOTS)
            for j in range(JOB_NA + 1, JOB_DIFF):
                for s in range(SLOTS):
                    if s == 3:
                        read_mod(j)
                    split_lo(j, s)
                    if s == 3:
                        read_result(j - 1)
                    ada_steps(j, s)
            for s in range(SPLIT_SLOTS - 1):
                split_lo(JOB_DIFF, s)

            mask = consts[:, C_MASK:C_MASK + GRID_W].unsqueeze(1).to_broadcast([P, TOK * ROWS, GRID_W])

            def na_bias(n):
                h, t = divmod(n, TOK)
                if t == 0:
                    dve.wait_ge(bias_landed[h % 2], 64 * (h // 2 + 1))
                    b = bias[:, h % 2, :].rearrange("p (a b) -> p a b", b=GRID_W)
                    dve.tensor_tensor(b, b, mask, ALU.add).then_inc(bias_ready, 1)
                    dve.wait_ge(bias_ready, h + 1)
                dve.wait_ge(na_scored, n + 1)
                if n >= 3:
                    dve.wait_ge(na_turned, n - 2)
                dve.scalar_tensor_tensor(scores[:, n % 3, 0:SEQ], ps[:, n % 2, 0:SEQ], NA_SCALE,
                                         bias[:, h % 2, t * SEQ:(t + 1) * SEQ], ALU.mult, ALU.add)\
                    .then_inc(na_biased, 1)
                dve.wait_ge(na_biased, n + 1)
                dve.wait_ge(na_ctx_scaled, n + 1)
                dve.tensor_reduce(row_max[:, n % 3, 0:1], scores[:, n % 3, :], AX.X, ALU.max, negate=True)\
                    .then_inc(na_max, 1)

            def na_result(n):
                h, t = divmod(n, TOK)
                dve.wait_ge(na_summed, n + 1)
                dve.tensor_copy(aT[:, h, t * P:(t + 1) * P], ps[:, 4 + n % 2, 0:P]).then_inc(na_out, 1)

            N = HEADS * TOK
            dve.wait_ge(ada_summed, KC * ADA_BEFORE_NA)
            na_bias(0)
            read_result(JOB_DIFF - 1)
            na_bias(1)
            for n in range(N):
                dve.wait_ge(na_exp, n + 1)
                dve.reciprocal(row_sum[:, n % 3, 0:1], row_sum[:, n % 3, 0:1]).then_inc(na_recip, 1)
                dve.wait_ge(na_recip, n + 1)
                dve.tensor_scalar(scores[:, n % 3, :], scores[:, n % 3, :], row_sum[:, n % 3, 0:1], None, ALU.mult)\
                    .then_inc(na_probs, 1)
                if n + 2 < N:
                    na_bias(n + 2)
                if n >= 1:
                    na_result(n - 1)
            na_result(N - 1)

            cos = consts[:, C_COS:C_COS + SEQ].unsqueeze(1).to_broadcast([P, 2, SEQ])
            sin = consts[:, C_SIN:C_SIN + SEQ].unsqueeze(1).to_broadcast([P, 2, SEQ])

            def rope(n):
                t, h, b = rotation(n)
                x = t[:, h:h + 2, 0:SEQ]
                dve.wait_ge(rotated, n + 1)
                if n >= 2:
                    dve.wait_ge(roped, n - 1)
                dve.tensor_tensor(rope_tmp[:, n % 2, :, :], ps[:, b, :].rearrange("p (a q) -> p a q", a=2), sin,
                                  ALU.mult).then_inc(rope_sin, 1)
                dve.tensor_tensor(x, x, cos, ALU.mult).then_inc(rope_cos, 1)
                dve.wait_ge(rope_sin, n + 1)
                dve.wait_ge(rope_cos, n + 1)
                dve.tensor_tensor(x, x, rope_tmp[:, n % 2, :, :], ALU.add).then_inc(roped, 1)

            for j in range(JOB_DIFF, JOB_MERGE):
                for s in range(SLOTS):
                    if s == (3 if j > JOB_DIFF else 0):
                        read_mod(j)
                    if j > JOB_DIFF or s >= SPLIT_SLOTS - 1:
                        split_lo(j, s)
                    if s == 3 and j > JOB_DIFF:
                        read_result(j - 1)
                    ada_steps(j, s)
                    if j == JOB_MERGE - 2 and s >= 4:
                        rope(s - 4)
                    if j == JOB_MERGE - 1:
                        if s == 7:
                            dve.wait_ge(aT_hi_ready, 1)
                            dve.tensor_tensor(aT_lo[:], aT[:], aT_hi[:], ALU.subtract).then_inc(aT_ready, 1)
                        if s in (4, 5):
                            rope(s)
            for s in range(SPLIT_SLOTS - 1):
                split_lo(JOB_MERGE, s)

            def df_maxima(n):
                dve.wait_ge(df_scored, 2 * n + 2)
                dve.tensor_reduce(row_max[:, n % 3, :], ps[:, 2 * (n % 2):2 * (n % 2) + 2, :], AX.X, ALU.max,
                                  negate=True).then_inc(df_max, 1)
                dve.wait_ge(df_max, n + 1)
                dve.tensor_scalar(row_max[:, n % 3, :], row_max[:, n % 3, :], DIFF_SCALE, None, ALU.mult)\
                    .then_inc(df_bias, 1)

            df_maxima(0)
            read_result(JOB_MERGE - 1)
            df_maxima(1)
            for n in range(N):
                dve.wait_ge(df_exp, 2 * n + 2)
                dve.reciprocal(row_sum[:, n % 3, :], row_sum[:, n % 3, :]).then_inc(df_recip, 1)
                dve.wait_ge(df_recip, n + 1)
                dve.tensor_scalar(row_sum[:, n % 3, 1:2], row_sum[:, n % 3, 1:2], lam[:, 0:1], None, ALU.mult)\
                    .then_inc(df_lam, 1)
                dve.tensor_scalar(diff_e[:, n % 2, 0, :], diff_e[:, n % 2, 0, :], row_sum[:, n % 3, 0:1], None,
                                  ALU.mult).then_inc(df_first, 1)
                dve.wait_ge(df_lam, n + 1)
                dve.wait_ge(df_first, n + 1)
                dve.scalar_tensor_tensor(diff_e[:, n % 2, 0, :], diff_e[:, n % 2, 1, :], row_sum[:, n % 3, 1:2],
                                         diff_e[:, n % 2, 0, :], ALU.mult, ALU.add).then_inc(df_probs, 1)
                if n + 2 < N:
                    df_maxima(n + 2)
                if n in LATE_ROTATIONS:
                    rope(LATE_ROTATIONS[n])
            dve.wait_ge(df_out, N)
            dve.tensor_tensor(diff_sq[:], diff_o[:], diff_o[:], ALU.mult).then_inc(o_step, 1)
            dve.wait_ge(o_step, 1)
            dve.tensor_reduce(rms_o[:], diff_sq[:], AX.X, ALU.add).then_inc(o_step, 1)
            dve.wait_ge(o_step, 2)
            dve.tensor_scalar(rms_o[:], rms_o[:], 1.0 / HD, EPS, ALU.mult, ALU.add).then_inc(o_step, 1)
            for s in (SPLIT_SLOTS - 1, SPLIT_SLOTS):
                split_lo(JOB_MERGE, s)
            dve.wait_ge(o_step, 4)
            dve.reciprocal(rms_o[:], rms_o[:]).then_inc(o_step, 1)
            dve.wait_ge(o_step, 5)
            dve.tensor_tensor(diff_o[:], diff_o[:], rms_o[:].unsqueeze(2).to_broadcast([P, HEADS * TOK, HD]),
                              ALU.mult).then_inc(o_normed, 1)
            for s in range(SPLIT_SLOTS + 1, SLOTS):
                split_lo(JOB_MERGE, s)
            for s in range(2):
                split_lo(JOB_MERGE + 1, s)
            dve.wait_ge(bT_hi_ready, 1)
            dve.tensor_tensor(bT_lo[:], bT[:], bT_hi[:], ALU.subtract).then_inc(bT_ready, 1)

            def merge_y(g, n):
                dve.wait_ge(used[7], 3 * g + JOB_MERGE + 3)
                dve.wait_ge(sig_a_ready, n)
                dve.wait_ge(sig_b_ready, n)
                if not (isinstance(g, int) and g == 0):
                    dve.wait_ge(y_turned, g)
                dve.tensor_tensor(y[:], ps[:, 4:6, :], sig_a[:], ALU.mult).then_inc(y_a, 1)
                dve.tensor_tensor(sig_b[:], ps[:, 6:8, :], sig_b[:], ALU.mult).then_inc(y_b, 1)
                dve.wait_ge(y_a, n)
                dve.wait_ge(y_b, n)
                dve.tensor_tensor(y[:], y[:], sig_b[:], ALU.add).then_inc(y_ready, 1)

            def turn_lo(g):
                dve.wait_ge(yT_hi_ready, g + 1)
                dve.tensor_tensor(yT_lo[:, bass.ds(g * TILES, TILES), :],
                                  ps[:, 4:6, :].rearrange("p a (b q) -> p (a b) q", b=2),
                                  yT_hi[:, bass.ds(g * TILES, TILES), :], ALU.subtract).then_inc(yT_ready, 1)

            def merge_group(g, first):
                j = 3 * g + JOB_MERGE
                if not first:
                    for s in range(SLOTS):
                        split_lo(j, s)
                        if s == 3:
                            merge_y(g - 1, g)
                    turn_lo(g - 1)
                for s in range(SLOTS):
                    if not first or s >= 2:
                        split_lo(j + 1, s)
                for s in range(SLOTS):
                    split_lo(j + 2, s)

            merge_group(0, True)
            with dve.Fori(1, D // GROUP) as g:
                merge_group(g, False)

            def add_out(g):
                b = 2 * g
                dve.wait_ge(used[7], JOB_OUT + g + 1)
                dve.wait_ge(g1_ready, 1)
                rows = g1_rows[:, g * GROUP:(g + 1) * GROUP].unsqueeze(1).to_broadcast([P, TOK, GROUP])
                part = x2[:, :, g * GROUP:(g + 1) * GROUP]
                if g:
                    dve.wait_ge(x2_added, g)
                else:
                    dve.wait_ge(x2_landed, 16)
                dve.tensor_tensor(sig_a[:], ps[:, b:b + 2, :], rows, ALU.mult).then_inc(out_gated, 1)
                dve.wait_ge(out_gated, g + 1)
                dve.tensor_tensor(part, part, sig_a[:], ALU.add).then_inc(x2_added, 1)

            for g in range(4):
                for s in range(SLOTS):
                    split_lo(JOB_OUT + g, s)
                    if s == 3:
                        if g == 0:
                            merge_y(3, 4)
                        else:
                            add_out(g - 1)
                if g == 0:
                    turn_lo(3)
            for s in range(SPLIT_SLOTS - 1):
                split_lo(JOB_UP, s)
            add_out(3)
            split_lo(JOB_UP, SPLIT_SLOTS - 1)
            dve.tensor_scalar(gain2[:], mod[:, 2 * KC:3 * KC], 1.0, None, ALU.add).then_inc(gain2_ready, 1)
            dve.wait_ge(gain2_ready, 1)
            dve.tensor_tensor(gain2[:], gain2[:], vecs[:, V_N2:V_N2 + KC], ALU.mult).then_inc(gain2_ready, 1)
            dve.wait_ge(squares2, 4 * TOK)
            dve.tensor_reduce(rms2[:], ssq2[:], AX.X, ALU.add).then_inc(rms2_step, 1)
            dve.wait_ge(rms2_step, 1)
            dve.tensor_scalar(rms2[:], rms2[:], 1.0 / D, EPS, ALU.mult, ALU.add).then_inc(rms2_step, 1)
            dve.wait_ge(rms2_step, 3)
            dve.reciprocal(rms2[:], rms2[:]).then_inc(rms2_step, 1)
            dve.wait_ge(rms2_step, 4)
            for g in range(4):
                for t in range(TOK):
                    dve.tensor_scalar(x2_normed[:, t, g * GROUP:(g + 1) * GROUP],
                                      x2[:, t, g * GROUP:(g + 1) * GROUP], rms2[:, t:t + 1], None, ALU.mult)\
                        .then_inc(x2_norm_ready, 1)

            def split_modulated2(m):
                dve.wait_ge(modulated2_ready, 2 * m + 2)
                dve.tensor_copy(h2T[:, 2 * m:2 * m + 2, 0, :], modulated2[:, m % 4, :, :])\
                    .then_inc(h2T_hi_ready, 1)
                dve.wait_ge(h2T_hi_ready, m + 1)
                dve.tensor_tensor(h2T[:, 2 * m:2 * m + 2, 1, :], modulated2[:, m % 4, :, :],
                                  h2T[:, 2 * m:2 * m + 2, 0, :], ALU.subtract).then_inc(h2T_ready, 1)

            for m in range(4):
                split_modulated2(m)
            for s in range(SPLIT_SLOTS):
                split_modulated2(s + 4)
                split_lo(JOB_UP, s + SPLIT_SLOTS)

            def conv_sum(n, b):
                dve.wait_ge(up_half_read, n + 1)
                dve.tensor_tensor(conv_in[:], conv_in[:], ps[:, b:b + 4, SEQ:2 * SEQ], ALU.add)\
                    .then_inc(up_read, 1)

            def conv_sides(n, tile, dst):
                dve.wait_ge(conv_mid, TILES * n + TILES)
                for t in range(TILES):
                    dve.scalar_tensor_tensor(dst[:, t, 1:SEQ], conv_in[:, t, 0:SEQ - 1],
                                             vecs[:, bass.ds(tile + (V_CONV + t), 1)],
                                             dst[:, t, 1:SEQ], ALU.mult, ALU.add).then_inc(conv_left, 1)
                dve.wait_ge(conv_left, TILES * n + TILES)
                for t in range(TILES):
                    ins = dve.scalar_tensor_tensor(dst[:, t, 0:SEQ - 1], conv_in[:, t, 1:SEQ],
                                                   vecs[:, bass.ds(tile + (V_CONV + 176 + t), 1)],
                                                   dst[:, t, 0:SEQ - 1], ALU.mult, ALU.add)
                ins.then_inc(conv_done, 1)

            def gate_steps(i, s):
                n = 2 * i
                if s == 3:
                    conv_sum(n, 0)
                if s == 4:
                    conv_sides(n, TILES * i, conv_gate)

            def up_steps(i, s):
                n = 2 * i + 1
                if s == 3:
                    conv_sum(n, 4)
                if s == 4:
                    conv_sides(n, TILES * i + FF_TILES, conv_up)
                if s == 5:
                    dve.wait_ge(conv_done, n + 1)
                    dve.wait_ge(gate_done, i + 1)
                    dve.tensor_tensor(hidden[:, bass.ds(TILES * i, TILES), :], conv_gate[:], conv_up[:], ALU.mult)\
                        .then_inc(hidden_ready, 1)

            def ffn_pair(i, first):
                for s in range(SLOTS):
                    if not first:
                        split_lo(2 * i + JOB_UP, s)
                        up_steps(i - 1, s)
                for s in range(SLOTS):
                    split_lo(2 * i + JOB_UP + 1, s)
                    gate_steps(i, s)

            ffn_pair(0, True)
            with dve.Fori(1, FF_GROUPS) as i:
                ffn_pair(i, False)

            def down_job(i, first, last=False):
                for s in range(SLOTS):
                    split_lo(i + JOB_DOWN, s)
                    t = s if last else s // 2
                    if (last and s < TILES) or (not last and s % 2 == 0):
                        dve.wait_ge(f_hi_ready, TILES * i + t + 1)
                        dve.tensor_tensor(f_lo[:, t:t + 1, :], hidden[:, bass.ds(TILES * i + t, 1), :],
                                          f_hi[:, t:t + 1, :], ALU.subtract).then_inc(f_lo_ready, 1)
                    if first:
                        up_steps(FF_GROUPS - 1, s)

            def add_down(half):
                at = slice(half * UNIT, (half + 1) * UNIT)
                for t in range(TOK):
                    b = 4 * half + 2 * t
                    dve.tensor_tensor(final_tmp[:, t, at], ps[:, b:b + 2, :].rearrange("p a n -> p (a n)"),
                                      g2_rows[:, at], ALU.mult).then_inc(out3_gated, 1)
                    dve.wait_ge(out3_gated, 2 * half + t + 1)
                    dve.tensor_tensor(x2[:, t, at], x2[:, t, at], final_tmp[:, t, at], ALU.add)\
                        .then_inc(x3_ready, 1)

            def weigh(half):
                at = slice(half * UNIT, (half + 1) * UNIT)
                for t in range(TOK):
                    dve.wait_ge(x3_ready, TOK * half + t + 1)
                    dve.tensor_tensor(final_tmp[:, t, at], x2[:, t, at], final_rows[:, at], ALU.mult)\
                        .then_inc(x3_weighted, 1)

            down_job(0, True)
            with dve.Fori(1, FF_GROUPS - 1) as i:
                down_job(i, False)
            down_job(FF_GROUPS - 1, False, last=True)

            dve.wait_ge(g2_ready, 1)
            dve.wait_ge(used[3], JOB_DOWN + FF_GROUPS)
            add_down(0)
            dve.wait_ge(final_landed, 16)
            weigh(0)
            dve.wait_ge(used[7], JOB_DOWN + FF_GROUPS)
            add_down(1)
            weigh(1)

            dve.wait_ge(squares3, 2 * TOK)
            dve.tensor_reduce(rms3[:], ssq3[:], AX.X, ALU.add).then_inc(rms3_step, 1)
            dve.wait_ge(rms3_step, 1)
            dve.tensor_scalar(rms3[:], rms3[:], 1.0 / D, EPS, ALU.mult, ALU.add).then_inc(rms3_step, 1)
            dve.wait_ge(rms3_step, 3)
            dve.reciprocal(rms3[:], rms3[:]).then_inc(rms3_step, 1)
            dve.wait_ge(rms3_step, 4)
            dve.wait_ge(x3_weighted, 2 * TOK)
            for half in range(2):
                part = final_tmp[:, 0, half * UNIT:(half + 1) * UNIT]
                dve.tensor_scalar(part, part, rms3[:, 0:1], None, ALU.mult).then_inc(out_ready, 1)

        @block.tensor
        def _(pe):
            def take(j, s):
                pe.wait_ge(lo_ready[s], j + 1)

            def row4(s):
                return s % SPLIT_SLOTS

            pe.wait_ge(consts_landed, 16)
            pe.wait_ge(rows_landed, 64)
            pe.transpose(ps[:, 5, 0:64], param_rows[0:64, 0, :], consts[0:64, 0:64]).then_inc(vecs_turned, 1)
            pe.wait_ge(rows2_landed, 96)
            pe.transpose(ps[:, 6, V_ADAB:V_ADAB + 96], param_rows[0:96, 1, :], consts[0:96, 0:96])
            for tap in range(TAPS):
                pe.transpose(ps[:, 6, V_CONV + 88 * tap:V_CONV + 88 * (tap + 1)], param_rows[0:88, 2 + tap, :],
                             consts[0:88, 0:88])
            pe.transpose(ps[:, 6, V_CONVB:V_CONVB + 88], param_rows[0:88, 5, :], consts[0:88, 0:88])
            pe.transpose(ps[:, 7, 0:89], param_rows[0:89, 5, :], consts[0:89, 0:89]).then_inc(vecs_turned, 1)

            pe.wait_ge(c_ready, 2)
            def turn_tokens(kc):
                for t in range(2 * TOK):
                    mm = pe.transpose(ps[:, 4 + kc % 4, t * P:(t + 1) * P], tokens[:, t, kc * P:(kc + 1) * P], ident)
                mm.then_inc(tokens_turned, 1)

            def mod_cols(tiles):
                for n in tiles:
                    mm = pe.matmul(ps[:, 0, 2 * n:2 * n + 2], mod_rows[:, n * P:(n + 1) * P],
                                   consts[0:4, C_SEL:C_SEL + 2], start=True, stop=True)
                mm.then_inc(mod_cols_ready, 1)

            for j in range(JOB_NA):
                if j in (4, 6):
                    pe.wait_ge(mod_rows_ready, j // 2 - 1)
                for s in range(SLOTS):
                    take(j, s)
                    kc = SLOTS * (j % 2) + s
                    for half in range(2):
                        for w in (w_hi, w_lo):
                            mm = pe.matmul(ps[:, 2 * (j // 2 % 2) + half, :], c_parts[:, 4 * kc:4 * kc + P],
                                           w[:, row4(s), half * GROUP:(half + 1) * GROUP],
                                           start=(kc == 0 and w is w_hi), stop=(kc == KC - 1 and w is w_lo))
                    mm.then_inc(used[s], 1)
                    if j == JOB_NA - 1:
                        if s == 0:
                            pe.wait_ge(vecs_ready, 3)
                            pe.wait_ge(normed1, 4)
                        if s < 4:
                            turn_tokens(s)
                        if s == 4:
                            pe.wait_ge(mod_rows_ready, 3)
                            mod_cols(range(3 * KC // 2))
            pe.wait_ge(mod_rows_ready, 4)
            mod_cols(range(3 * KC // 2, 2 * KC))

            def sum_mod(g, j):
                b, col = ada_bank(j), TILES * ada_groups(j - 1).index(g)
                pe.wait_ge(ada_summed, KC * (g + 1))
                for n in range(TILES):
                    mm = pe.matmul(ps[:, b, col + n:col + n + 1], ada_acc[:, g % 2, n * P:(n + 1) * P], ones[:],
                                   start=True, stop=True)
                mm.then_inc(mod_summed, 1)

            def unit_k(s, t, b):
                for i in range(2):
                    kc = 2 * s + i
                    o = ps[:, b + t, :].rearrange("p (a n) -> p a n", a=2)
                    at = slice(i * GROUP + t * P, i * GROUP + (t + 1) * P)
                    pe.matmul(o, w_hi[:, row4(s), at], hT[:, :, 0, kc, :], start=(kc == 0), stop=False)
                    pe.matmul(o, w_hi[:, row4(s), at], hT[:, :, 1, kc, :], start=False, stop=False)
                    mm = pe.matmul(o, w_lo[:, row4(s), at], hT[:, :, 0, kc, :], start=False,
                                   stop=(kc == KC - 1))
                return mm

            def unit_paired(s, t, b, both, high):
                for i in range(2):
                    kc = 2 * s + i
                    o = ps[:, b + t, :].rearrange("p (a n) -> p a n", a=2)
                    at = slice(i * GROUP + t * P, i * GROUP + (t + 1) * P)
                    if kc == 0:
                        pe.matmul(o, w_hi[:, row4(s), at], both(kc), start=True, stop=False)
                        mm = pe.matmul(ps[:, b + t, 0:SEQ], w_lo[:, row4(s), at], high(kc), start=False, stop=False)
                    else:
                        pe.matmul(ps[:, b + t, 0:SEQ], w_lo[:, row4(s), at], high(kc), start=False, stop=False)
                        mm = pe.matmul(o, w_hi[:, row4(s), at], both(kc), start=False, stop=(kc == KC - 1))
                return mm

            def moving_weights(s, banks, stationary_hi, stationary_lo, kcs, last):
                for n, b in enumerate(banks):
                    for i, kc in enumerate(kcs):
                        at = slice(i * GROUP, (i + 1) * GROUP)
                        hi, lo = stationary_hi(kc, n), stationary_lo(kc, n)
                        pe.matmul(ps[:, b, :], hi, w_hi[:, row4(s), at], start=(kc == 0), stop=False)
                        pe.matmul(ps[:, b, :], hi, w_lo[:, row4(s), at], start=False, stop=False)
                        mm = pe.matmul(ps[:, b, :], lo, w_hi[:, row4(s), at], start=False, stop=(kc == last))
                return mm

            def tok(part):
                return lambda kc, n: hT[:, n // TOK, part, kc, (n % TOK) * P:(n % TOK + 1) * P]

            def projection(j):
                kind, _ = PROJECTIONS[j - JOB_NA]
                b = 4 * (j % 2)
                if j >= JOB_NA + 2:
                    pe.wait_ge(*results_read(j - 2))
                if j == JOB_MERGE - 1:
                    pe.wait_ge(rope_sin, 4)
                done = ada_groups(j - 1)
                if done:
                    sum_mod(done[-1], j)
                for s in range(SLOTS):
                    if j == JOB_NA:
                        pe.wait_ge(hT_ready, 2 * s + 2)
                        for kc in (2 * s + 4, 2 * s + 5):
                            if kc < KC:
                                turn_tokens(kc)
                    take(j, s)
                    for t in range(TILES):
                        if s == 0 and t == 3 and done:
                            pe.wait_ge(mod_ready, done[-1] + 1)
                        if kind == "k":
                            mm = unit_k(s, t, b)
                        elif kind == "v":
                            mm = moving_weights(s, (b + t,), lambda kc, _: tok(0)(kc, t),
                                                lambda kc, _: tok(1)(kc, t), (2 * s, 2 * s + 1), KC - 1)
                        else:
                            mm = unit_paired(s, t, b, lambda kc: hT[:, 0, :, kc, :], lambda kc: hT[:, 0, 0, kc, :])
                    mm.then_inc(used[s], 1)
                    if s == 5 and len(ada_groups(j)) == 2:
                        pe.wait_ge(*results_read(j - 1))
                        sum_mod(ada_groups(j)[0], j + 1)
                    if s == 1 and j == JOB_MERGE - 2:
                        pe.wait_ge(*results_read(j - 1))
                        for n in range(4):
                            rotate(n)
                    if s == 2 and j == JOB_MERGE - 1:
                        pe.wait_ge(*results_read(j - 1))
                        for n in range(4, 6):
                            rotate(n)

            def rotate(n):
                t, h, b = rotation(n)
                for i in range(2):
                    mm = pe.matmul(ps[:, b, i * SEQ:(i + 1) * SEQ], consts[:, C_ROT:C_ROT + P], t[:, h + i, 0:SEQ],
                                   start=True, stop=True)
                mm.then_inc(rotated, 1)

            pe.wait_ge(mod1_ready, 1)
            for j in range(JOB_NA, JOB_DIFF):
                projection(j)

            pe.wait_ge(*results_read(JOB_DIFF - 2))
            N = HEADS * TOK

            def na_scores(n):
                h, t = divmod(n, TOK)
                if n >= 2:
                    pe.wait_ge(na_biased, n - 1)
                    pe.wait_ge(na_ctx_scaled, n - 1)
                for b, keys in ((0, slice(0, SEQ)), (2, slice(SEQ, 2 * SEQ))):
                    mm = pe.matmul(ps[:, b + n % 2, 0:SEQ], qT[:, h, t * P:(t + 1) * P], kT[:, h, keys],
                                   start=True, stop=True)
                mm.then_inc(na_scored, 1)

            def na_turn(n):
                pe.wait_ge(na_probs, n + 1)
                if n >= 2:
                    pe.wait_ge(na_pT_ready, n - 1)
                for k in range(2 * TOK):
                    mm = pe.transpose(ps[:, 6 + n % 2, k * P:(k + 1) * P], scores[:, n % 3, k * P:(k + 1) * P], ident)
                mm.then_inc(na_turned, 1)

            def na_values(n):
                h = n // TOK
                pe.wait_ge(na_pT_ready, n + 1)
                if n >= 2:
                    pe.wait_ge(na_out, n - 1)
                for k in range(2 * TOK):
                    mm = pe.matmul(ps[:, 4 + n % 2, 0:P], v_sb[:, k, h * HD:(h + 1) * HD], na_pT[:, k, :],
                                   start=(k == 0), stop=(k == 2 * TOK - 1))
                mm.then_inc(na_summed, 1)

            na_scores(0)
            na_scores(1)
            pe.wait_ge(*results_read(JOB_DIFF - 1))
            for n in range(N):
                if n + 2 < N:
                    na_scores(n + 2)
                if n:
                    na_values(n - 1)
                na_turn(n)
            na_values(N - 1)
            pe.wait_ge(na_out, N)
            pe.wait_ge(na_pT_ready, N)

            for j in range(JOB_DIFF, JOB_MERGE):
                projection(j)

            def df_scores(n):
                h, t = divmod(n, TOK)
                pe.wait_ge(roped, max(6, 5 + h // 2))
                if n >= 2:
                    pe.wait_ge(df_exp, 2 * n - 2)
                for m in range(2):
                    half = slice(m * MAP_DIM, (m + 1) * MAP_DIM)
                    pe.matmul(ps[:, 2 * (n % 2) + m, :], qT[half, h, t * P:(t + 1) * P], kT[half, h, :],
                              start=True, stop=True).then_inc(df_scored, 1)

            def df_turn(n):
                pe.wait_ge(df_probs, n + 1)
                if n >= 1:
                    pe.wait_ge(df_pT_ready, n)
                for k in range(2 * TOK):
                    mm = pe.transpose(ps[:, 4, k * P:(k + 1) * P], diff_e[:, n % 2, 0, k * P:(k + 1) * P],
                                      ident)
                mm.then_inc(df_turned, 1)

            def df_values(n):
                h = n // TOK
                pe.wait_ge(df_pT_ready, n + 1)
                if n >= 2:
                    pe.wait_ge(df_out, n - 1)
                for k in range(2 * TOK):
                    mm = pe.matmul(ps[:, 6 + n % 2, 0:P], diff_pT[:, n % 2, k, :],
                                   v_sb[:, k, h * HD:(h + 1) * HD], start=(k == 0), stop=(k == 2 * TOK - 1))
                mm.then_inc(df_summed, 1)

            df_scores(0)
            df_scores(1)
            pe.wait_ge(*results_read(JOB_MERGE - 1))
            for n in range(N):
                if n + 2 < N:
                    df_scores(n + 2)
                if n in LATE_ROTATIONS:
                    if LATE_ROTATIONS[n] == 7:
                        pe.wait_ge(rope_sin, 7)
                    rotate(LATE_ROTATIONS[n])
                if n:
                    df_values(n - 1)
                df_turn(n)
            df_values(N - 1)

            def part(t):
                return lambda kc, n: t[:, kc, n * P:(n + 1) * P]

            def spread(n, col, b):
                for kc in range(KC):
                    mm = pe.matmul(ps[:, b + kc // 4, (kc % 4) * P:(kc % 4 + 1) * P],
                                   mod[:, col + kc:col + kc + 1].to_broadcast([P, P]), ident,
                                   start=True, stop=True)
                mm.then_inc(n, 1)

            def turn_y(g):
                pe.wait_ge(y_ready, g + 1)
                for n in range(TILES):
                    for t in range(TOK):
                        at = ((n % 2) * TOK + t) * P
                        mm = pe.transpose(ps[:, 4 + n // 2, at:at + P], y[:, t, n * P:(n + 1) * P], ident)
                mm.then_inc(y_turned, 1)

            def merge_group(g, first):
                j = 3 * g + JOB_MERGE
                if not first:
                    pe.wait_ge(sig_a_ready, g)
                for s in range(SLOTS):
                    take(j, s)
                    moving_weights(s, (0, 1), tok(0), tok(1), (2 * s, 2 * s + 1), KC - 1).then_inc(used[s], 1)
                    if s == 5 and first:
                        pe.wait_ge(o_normed, 1)
                        for n in range(HEADS * TOK):
                            mm = pe.transpose(ps[:, 4 + n // 4, (n % 4) * P:(n % 4 + 1) * P], diff_o[:, n, :],
                                              ident)
                        mm.then_inc(o_turned, 1)
                    if s == 3 and not first:
                        turn_y(g - 1)
                if not first:
                    pe.wait_ge(sig_b_ready, g)
                for s in range(SLOTS):
                    take(j + 1, s)
                    moving_weights(s, (2, 3), tok(0), tok(1), (2 * s, 2 * s + 1), KC - 1).then_inc(used[s], 1)
                    if s == 3 and first:
                        pe.wait_ge(bT_scaled, 1)
                        pe.wait_ge(mod_ready, ADA_GROUPS)
                        spread(g1_spread, 0, 4)
                if first:
                    pe.wait_ge(g1_ready, 1)
                    pe.wait_ge(bT_ready, 1)
                    pe.wait_ge(aT_ready, 1)
                else:
                    pe.wait_ge(yT_ready, g)
                for s in range(SLOTS):
                    take(j + 2, s)
                    kcs = (2 * (s % 4), 2 * (s % 4) + 1)
                    if s < 4:
                        mm = moving_weights(s, (4, 5), part(aT_hi), part(aT_lo), kcs, HEADS - 1)
                    else:
                        mm = moving_weights(s, (6, 7), part(bT_hi), part(bT_lo), kcs, HEADS - 1)
                    mm.then_inc(used[s], 1)

            merge_group(0, True)
            with pe.Fori(1, D // GROUP) as g:
                merge_group(g, False)

            for g in range(4):
                if g == 0:
                    pe.wait_ge(sig_a_ready, 4)
                if g == 1:
                    pe.wait_ge(sig_b_ready, 4)
                if g == 2:
                    pe.wait_ge(yT_ready, 4)
                for s in range(SLOTS):
                    if g == 0 and s == 6:
                        pe.wait_ge(yT_ready, 4)
                    elif g == 0 and s == 0:
                        pe.wait_ge(yT_ready, 3)
                    take(JOB_OUT + g, s)
                    moving_weights(s, (2 * g, 2 * g + 1), part(yT_hi), part(yT_lo), (2 * s, 2 * s + 1), KC - 1)\
                        .then_inc(used[s], 1)
                    if g == 0 and s == 3:
                        turn_y(3)
            pe.wait_ge(x2_added, 2)
            spread(g2_spread, 3 * KC, 0)

            def turn_x2(m):
                for h in range(2):
                    kc = 2 * m + h
                    for t in range(TOK):
                        at = (h * TOK + t) * P
                        mm = pe.transpose(ps[:, 4 + m % 4, at:at + P], x2_normed[:, t, kc * P:(kc + 1) * P], ident)
                mm.then_inc(x2_turned, 1)

            for m in range(4):
                pe.wait_ge(x2_norm_ready, TOK * (m // 2 + 1))
                turn_x2(m)
            pe.wait_ge(g2_ready, 1)

            def both(kc):
                return h2T[:, kc, :, :]

            def high(kc):
                return h2T[:, kc, 0, :]

            def up_job(n, b, ready):
                for s in range(SLOTS):
                    if ready:
                        pe.wait_ge(h2T_ready, s + 1)
                    take(n + JOB_UP, s)
                    for t in range(TILES):
                        mm = unit_paired(s, t, b, both, high)
                    mm.then_inc(used[s], 1)
                    if ready and s + 4 < KC // 2:
                        pe.wait_ge(modulated2_ready, 2 * s + 2)
                        pe.wait_ge(x2_norm_ready, TOK * ((s + 4) // 2 + 1))
                        turn_x2(s + 4)

            up_job(0, 0, True)
            pe.wait_ge(modulated2_ready, KC)
            up_job(1, 4, False)
            with pe.Fori(1, FF_GROUPS) as i:
                for half in range(2):
                    pe.wait_ge(up_read, 2 * i + half - 1)
                    up_job(2 * i + half, 4 * half, False)

            def down_job(i, first, last):
                for s in range(SLOTS):
                    take(i + JOB_DOWN, s)
                    half, t = divmod(s, TILES) if last else (s % 2, s // 2)
                    if half == 0:
                        pe.wait_ge(f_lo_ready, TILES * i + t + 1)
                    if first and s < 2:
                        pe.wait_ge(up_read, 2 * FF_GROUPS - 1 + s)
                    for n in range(TOK):
                        for q in range(2):
                            b = 4 * half + 2 * n + q
                            at = slice(q * GROUP, (q + 1) * GROUP)
                            hi, lo = f_hi[:, t, n * P:(n + 1) * P], f_lo[:, t, n * P:(n + 1) * P]
                            pe.matmul(ps[:, b, :], hi, w_hi[:, row4(s), at], start=(first and t == 0), stop=False)
                            pe.matmul(ps[:, b, :], hi, w_lo[:, row4(s), at], start=False, stop=False)
                            mm = pe.matmul(ps[:, b, :], lo, w_hi[:, row4(s), at], start=False,
                                           stop=(last and t == 3))
                    mm.then_inc(used[s], 1)

            down_job(0, True, False)
            with pe.Fori(1, FF_GROUPS - 1) as i:
                down_job(i, False, False)
            down_job(FF_GROUPS - 1, False, True)


_INS = ["x", "c", "ctx", "c_ctx", "ada_w", "ada_b", "norm1_g", "w_in", "na_rpb", "diff_lambda", "diff_norm_g",
        "w_branch_a", "w_branch_b", "w_out", "norm2_g", "ffn_w_up", "ffn_conv_w", "ffn_conv_b", "ffn_w_down",
        "final_norm_g"]


def kernel(**inputs):
    import concourse.bacc as bacc
    from concourse.bass_utils import run_bass_kernel_spmd

    nc = bacc.Bacc("TRN2", target_bir_lowering=False, num_devices=1)
    arrays, args = {}, []
    for name in _INS:
        a = np.ascontiguousarray(inputs[name])
        arrays[f"in_{name}"] = a
        args.append(nc.dram_tensor(f"in_{name}", a.shape, F32, kind="ExternalInput").ap())
    arrays["in_constants"] = shape_constants()
    args.append(nc.dram_tensor("in_constants", (P, C_ALL), F32, kind="ExternalInput").ap())
    result = nc.dram_tensor("out_0", (1, SEQ, D), F32, kind="ExternalOutput").ap()
    block_program(nc, *args, result)
    r = run_bass_kernel_spmd(nc, [arrays], core_ids=[0])
    return r.results[0]["out_0"]
```

```python
import math
from contextlib import ExitStack

import numpy as np

import concourse.bass as bass
from concourse import mybir

F32 = mybir.dt.float32
F32R = mybir.dt.float32r
ACT = mybir.ActivationFunctionType
ALU = mybir.AluOpType
AX = mybir.AxisListType

P = 128
D = 2048
SEQ = 256
GRID_W = 64
ROWS = SEQ // GRID_W
HEADS = 8
HD = 128
WIDTH = HEADS * HD
WIN_ROWS = 8
WIN_COLS = 16
RPB_ROWS = 2 * WIN_ROWS - 1
RPB_COLS = 2 * WIN_COLS - 1
RPB_MARGIN = WIN_COLS
RPB_BLOCK = GRID_W * GRID_W + 2 * RPB_MARGIN
ZERO_PARTS = 8
MAP_DIM = 64
D_FF = 5632
TAPS = 3
EPS = 1e-6
LAMBDA_INIT = 0.8 - 0.6 * math.exp(0.0)
NA_SCALE = HD ** -0.5
DIFF_SCALE = MAP_DIM ** -0.5
MASKED = -1e30

KC = D // P
TOK = SEQ // P
UNIT = 1024
GROUP = 512
TILES = GROUP // P
SLOTS = 8
SPLIT_SLOTS = 4
ADA_SLOTS = 4
FF_TILES = D_FF // P
FF_GROUPS = D_FF // GROUP

QA, KA, VA, QB, KB, VB = (n * WIDTH for n in range(6))
GATE_A = 6 * WIDTH
GATE_B = GATE_A + D

JOB_NA = 8
JOB_DIFF = 14
JOB_MERGE = 20
JOB_OUT = 32
JOB_UP = 36
JOB_DOWN = JOB_UP + 2 * FF_GROUPS
PROJECTIONS = [("k", KA), ("k", KA + GROUP), ("v", VA), ("v", VA + GROUP), ("q", QA), ("q", QA + GROUP),
               ("k", KB), ("k", KB + GROUP), ("v", VB), ("v", VB + GROUP), ("q", QB), ("q", QB + GROUP)]
FIRST_HALF = [("ada", block, kc) for block in (0, 2) for kc in range(KC)]
SECOND_HALF = [("ada", block, kc) for block in (1, 3) for kc in range(KC)]
HEAD = (FIRST_HALF + SECOND_HALF[0:10] + [("k", 0)] + SECOND_HALF[10:17] + [("k", 1)] + SECOND_HALF[17:24]
        + [("k", 2)] + SECOND_HALF[24:32] + [("k", s) for s in range(3, SLOTS)])
K_UNITS = [HEAD.index(("k", s)) for s in range(SLOTS)]
ADA_BLOCKS = (0, 2, 1, 3)
BLOCK_ENDS = [HEAD.index(("ada", block, KC - 1)) for block in ADA_BLOCKS]
MID = len(FIRST_HALF) - 1
TURN_AFTER = {-1: (0,), 0: (1,), 1: (2,), 4: (3,), 5: (4,), 12: (5, 6), 21: (7,)}
MODULATE_AFTER = {8: (0, 1), 9: (2,), 10: (3, 4), 16: (5, 6), 25: (7,)}
SPLIT_AFTER = {8: (0,), 9: (1,), 10: (2,), 11: (3,), 12: (4,), 16: (5,), 17: (6,), 25: (7,)}
TURN_BANKS = [0, 1, 2, 6, 7, 6, 7, 4, 4, 6, 7, 5, 4, 6, 7, 5]
ADA_JOBS = [9, 9, 10, 10, 11, 11, 12, 13, 14, 14, 15, 15, 16, 16, 17, 17]
ADA_GROUPS = len(ADA_JOBS)
ADA_BEFORE_NA = sum(j < JOB_DIFF for j in ADA_JOBS)
ADA_FIRST_COL = 2 * D

C_IDENT, C_ROT, C_COS, C_SIN, C_MASK, C_SEL = 0, 128, 256, 512, 768, 832
C_ALL = 834
V_C, V_CC, V_ADAB, V_N1, V_N2, V_CONV, V_CONVB, V_DNG = 0, 16, 32, 128, 144, 160, 424, 512
V_ALL = 513


def shape_constants():
    k = np.zeros((P, C_ALL), np.float32)
    k[:, C_IDENT:C_IDENT + P] = np.eye(P)
    quarter = MAP_DIM // 4
    for m in range(P // MAP_DIM):
        for pair in range(2):
            a = m * MAP_DIM + 2 * pair * quarter
            for j in range(quarter):
                k[a + quarter + j, C_ROT + a + j] = -1.0
                k[a + j, C_ROT + a + quarter + j] = 1.0
    t = np.arange(SEQ)
    inv = (np.float32(10000.0) ** (-np.arange(quarter, dtype=np.float32) / np.float32(quarter))).astype(np.float32)
    ang_r = (t // GRID_W).astype(np.float32)[:, None] * inv[None]
    ang_c = (t % GRID_W).astype(np.float32)[:, None] * inv[None]
    ang = np.concatenate([ang_r, ang_r, ang_c, ang_c], axis=1).T
    k[:, C_COS:C_COS + SEQ] = np.tile(np.cos(ang), (2, 1))
    k[:, C_SIN:C_SIN + SEQ] = np.tile(np.sin(ang), (2, 1))
    col = np.arange(P) % GRID_W
    start = np.clip(col - WIN_COLS // 2, 0, GRID_W - WIN_COLS)[:, None]
    key = np.arange(GRID_W)[None]
    k[:, C_MASK:C_MASK + GRID_W] = np.where((key >= start) & (key < start + WIN_COLS), 0.0, MASKED)
    k[0:2, C_SEL] = 1.0
    k[2:4, C_SEL + 1] = 1.0
    return k


def block_program(nc, x, c, ctx, c_ctx, ada_w, ada_b, norm1_g, w_in, na_rpb, diff_lambda, diff_norm_g,
                  w_branch_a, w_branch_b, w_out, norm2_g, ffn_w_up, ffn_conv_w, ffn_conv_b, ffn_w_down,
                  final_norm_g, constants, out):
    base = nc.sbuf_base + (-nc.sbuf_base) % 64
    kb = 1024

    def place(name, at, shape, dtype=F32):
        return nc.alloc_sbuf_tensor_at(name, shape, dtype, offset=base + at)

    raw = place("raw", 0, [P, SLOTS, UNIT])
    w_hi = place("w_hi", 32 * kb, [P, SPLIT_SLOTS, UNIT], F32R)
    w_lo = place("w_lo", 48 * kb, [P, SPLIT_SLOTS, UNIT], F32R)
    lat, con = 64 * kb, 96 * kb
    hT = place("hT", lat, [P, 2, 2, KC, SEQ], F32R)
    junk = place("junk", lat, [P, D])
    h2T = place("h2T", lat, [P, KC, 2, SEQ], F32R)
    aT_hi = place("aT_hi", con, [P, HEADS, SEQ], F32R)
    aT_lo = place("aT_lo", con + 8 * kb, [P, HEADS, SEQ], F32R)
    bT_hi = place("bT_hi", con + 16 * kb, [P, HEADS, SEQ], F32R)
    bT_lo = place("bT_lo", con + 24 * kb, [P, HEADS, SEQ], F32R)
    rope_tmp = place("rope_tmp", con + 16 * kb, [P, 2, 2, SEQ])
    g2_rows = place("g2_rows", con, [P, D])
    final_rows = place("final_rows", con + 8 * kb, [P, D])
    conv_in = place("conv_in", con + 16 * kb, [P, TILES, SEQ])
    conv_gate = place("conv_gate", con + 20 * kb, [P, TILES, SEQ])
    conv_up = place("conv_up", con + 24 * kb, [P, TILES, SEQ])
    arena = 128 * kb
    tokens = place("tokens", arena, [P, 2 * TOK, D])
    modulated = place("modulated", arena + 32 * kb, [P, 4, 2, SEQ])
    kT = place("kT", arena, [P, HEADS, 2 * SEQ])
    v_sb = place("v_sb", arena + 16 * kb, [P, 2 * TOK, WIDTH])
    qT = place("qT", arena + 32 * kb, [P, HEADS, SEQ])
    bias = place("bias", arena + 40 * kb, [P, 2, TOK * SEQ])
    diff_pT = place("diff_pT", arena + 40 * kb, [P, 2, 2 * TOK, P])
    yT_hi = place("yT_hi", arena, [P, KC, SEQ], F32R)
    yT_lo = place("yT_lo", arena + 16 * kb, [P, KC, SEQ], F32R)
    g1_rows = place("g1_rows", arena + 32 * kb, [P, D])
    y = place("y", arena + 40 * kb, [P, TOK, GROUP])
    x2_normed = place("x2_normed", arena, [P, TOK, D])
    modulated2 = place("modulated2", arena + 16 * kb, [P, 4, 2, SEQ])
    hidden = place("hidden", arena, [P, FF_TILES, SEQ])
    att = 172 * kb
    aT = place("aT", att, [P, HEADS, SEQ])
    diff_o = place("diff_o", att, [P, HEADS * TOK, HD])
    ada_acc = place("ada_acc", att + 8 * kb, [P, 2, GROUP])
    ada_raw = place("ada_raw", att + 12 * kb, [P, ADA_SLOTS, 2, GROUP])
    mod_rows = place("mod_rows", att, [4, 2 * D])
    x2 = place("x2", att, [P, TOK, D])
    tmp = 192 * kb
    param_rows = place("param_rows", tmp, [P, 6, P])
    scores = place("scores", tmp, [P, 3, 2 * SEQ])
    na_pT = place("na_pT", tmp + 6 * kb, [P, 2 * TOK, P])
    diff_e = place("diff_e", tmp, [P, 2, 2, 2 * SEQ])
    diff_sq = place("diff_sq", tmp, [P, HEADS * TOK, HD])
    bT = place("bT", tmp, [P, HEADS, SEQ])
    sig_a = place("sig_a", tmp, [P, TOK, GROUP])
    sig_b = place("sig_b", tmp + 4 * kb, [P, TOK, GROUP])
    f_hi = place("f_hi", tmp, [P, SPLIT_SLOTS, SEQ], F32R)
    f_lo = place("f_lo", tmp + 4 * kb, [P, SPLIT_SLOTS, SEQ], F32R)
    squares_out = place("squares_out", lat, [P, UNIT])
    final_tmp = place("final_tmp", con + 16 * kb, [P, TOK, D])
    at = 200 * kb

    def keep(name, shape, dtype=F32):
        nonlocal at
        t = place(name, at, shape, dtype)
        at += (4 * int(np.prod(shape[1:])) + 31) // 32 * 32
        return t

    consts = keep("consts", [P, C_ALL])
    vecs = keep("vecs", [P, V_ALL])
    c_parts = keep("c_parts", [P, 4 * KC + P], F32R)
    silu_c = keep("silu_c", [P, 2 * KC])
    exp_c = keep("exp_c", [P, 2 * KC])
    gain1 = keep("gain1", [P, 2, KC])
    shift1 = keep("shift1", [P, 2, KC])
    mod = keep("mod", [P, 4 * ADA_GROUPS])
    gain2 = keep("gain2", [P, KC])
    ones = keep("ones", [P, 1])
    rms1 = keep("rms1", [P, 2 * TOK])
    row_max = keep("row_max", [P, 3, 2])
    row_sum = keep("row_sum", [P, 3, 2])
    lam = keep("lam", [P, 2])
    warm = keep("warm", [P, 1])
    rms_o = keep("rms_o", [P, HEADS * TOK])
    dng = keep("dng", [P, 1])
    ssq2 = keep("ssq2", [P, TOK, 4])
    rms2 = keep("rms2", [P, TOK])
    ssq3 = keep("ssq3", [P, TOK, 2])
    rms3 = keep("rms3", [P, TOK])
    lam_in = place("lam_in", lat + 8 * kb, [P, 4 * MAP_DIM])
    lam_prod = place("lam_prod", lat + 9 * kb, [P, 2, MAP_DIM])
    zeros = place("zeros", arena + 40 * kb, [HEADS * RPB_ROWS, RPB_BLOCK // ZERO_PARTS])
    ident = consts[:, C_IDENT:C_IDENT + P]

    rpb_grid = nc.dram_tensor("rpb_grid", [HEADS * RPB_ROWS, RPB_BLOCK], F32)

    ps = nc.alloc_psum_tensor("ps", [P, 8, GROUP], F32)

    with ExitStack() as es:
        def sem(name):
            return es.enter_context(nc.semaphore(name))

        def sems(name, n):
            return [sem(f"{name}{i}") for i in range(n)]

        raw_landed = sems("raw_landed", SLOTS)
        hi_ready = sems("hi_ready", SLOTS)
        lo_ready = sems("lo_ready", SLOTS)
        used = sems("used", SLOTS)
        ident_landed = sem("ident_landed")
        consts_landed = sem("consts_landed")
        rows_landed = sem("rows_landed")
        rows2_landed = sem("rows2_landed")
        tokens_landed = sem("tokens_landed")
        vecs_turned = sem("vecs_turned")
        vecs_ready = sem("vecs_ready")
        exp_c_ready = sem("exp_c_ready")
        start_dve = sem("start_dve")
        ones_ready = sem("ones_ready")
        c_ready = sem("c_ready")
        lam_landed = sem("lam_landed")
        lam_step = sem("lam_step")
        lam_exp = sem("lam_exp")
        lam_ready = sem("lam_ready")
        squares1 = sem("squares1")
        rms1_step = sem("rms1_step")
        normed1 = sem("normed1")
        mod_rows_ready = sem("mod_rows_ready")
        mod_cols_ready = sem("mod_cols_ready")
        mod1_step = sem("mod1_step")
        mod1_ready = sem("mod1_ready")
        tokens_turned = sem("tokens_turned")
        modulated_ready = sem("modulated_ready")
        hT_hi_ready = sem("hT_hi_ready")
        hT_ready = sem("hT_ready")
        ada_landed = sems("ada_landed", ADA_SLOTS)
        ada_summed = sem("ada_summed")
        mod_summed = sem("mod_summed")
        mod_ready = sem("mod_ready")
        half_read = sem("half_read")
        kv_read = sem("kv_read")
        q_read = sem("q_read")
        zeros_ready = sem("zeros_ready")
        padded = sem("padded")
        bias_landed = sems("bias_landed", 2)
        bias_ready = sem("bias_ready")
        na_scored = sem("na_scored")
        na_ctx_scaled = sem("na_ctx_scaled")
        na_biased = sem("na_biased")
        na_max = sem("na_max")
        na_exp = sem("na_exp")
        na_recip = sem("na_recip")
        na_probs = sem("na_probs")
        na_turned = sem("na_turned")
        na_pT_ready = sem("na_pT_ready")
        na_summed = sem("na_summed")
        na_out = sem("na_out")
        aT_hi_ready = sem("aT_hi_ready")
        aT_ready = sem("aT_ready")
        rotated = sem("rotated")
        rope_cos = sem("rope_cos")
        rope_sin = sem("rope_sin")
        roped = sem("roped")
        df_scored = sem("df_scored")
        df_max = sem("df_max")
        df_bias = sem("df_bias")
        df_exp = sem("df_exp")
        df_recip = sem("df_recip")
        df_lam = sem("df_lam")
        df_first = sem("df_first")
        df_probs = sem("df_probs")
        df_turned = sem("df_turned")
        df_pT_ready = sem("df_pT_ready")
        df_summed = sem("df_summed")
        df_out = sem("df_out")
        o_step = sem("o_step")
        o_normed = sem("o_normed")
        o_turned = sem("o_turned")
        bT_scaled = sem("bT_scaled")
        bT_hi_ready = sem("bT_hi_ready")
        bT_ready = sem("bT_ready")
        g1_spread = sem("g1_spread")
        g1_ready = sem("g1_ready")
        sig_a_ready = sem("sig_a_ready")
        sig_b_ready = sem("sig_b_ready")
        y_a = sem("y_a")
        y_b = sem("y_b")
        y_ready = sem("y_ready")
        y_turned = sem("y_turned")
        yT_hi_ready = sem("yT_hi_ready")
        yT_ready = sem("yT_ready")
        x2_landed = sem("x2_landed")
        out_tile = sem("out_tile")
        out_gated = sem("out_gated")
        x2_added = sem("x2_added")
        squares2 = sem("squares2")
        rms2_step = sem("rms2_step")
        x2_norm_ready = sem("x2_norm_ready")
        gain2_ready = sem("gain2_ready")
        g2_spread = sem("g2_spread")
        g2_ready = sem("g2_ready")
        x2_turned = sem("x2_turned")
        modulated2_ready = sem("modulated2_ready")
        h2T_hi_ready = sem("h2T_hi_ready")
        h2T_ready = sem("h2T_ready")
        up_half_read = sem("up_half_read")
        up_read = sem("up_read")
        conv_mid = sem("conv_mid")
        conv_left = sem("conv_left")
        conv_done = sem("conv_done")
        gate_done = sem("gate_done")
        hidden_ready = sem("hidden_ready")
        f_hi_ready = sem("f_hi_ready")
        f_lo_ready = sem("f_lo_ready")
        final_landed = sem("final_landed")
        down_tile = sem("down_tile")
        out3_gated = sem("out3_gated")
        x3_ready = sem("x3_ready")
        squares3 = sem("squares3")
        rms3_step = sem("rms3_step")
        x3_weighted = sem("x3_weighted")
        out_ready = sem("out_ready")
        out1_ready = sem("out1_ready")
        out_stored = sem("out_stored")

        block = es.enter_context(nc.Block())

        w_in_v = w_in[0].rearrange("(k p) n -> p k n", p=P)
        ada_v = ada_w[0].rearrange("(k p) n -> p k n", p=P)
        pa_v = w_branch_a[0].rearrange("(k p) n -> p k n", p=P)
        pb_v = w_branch_b[0].rearrange("(k p) n -> p k n", p=P)
        out_v = w_out[0].rearrange("(k p) n -> p k n", p=P)
        up_v = ffn_w_up[0].rearrange("(k p) n -> p k n", p=P)
        down_v = ffn_w_down[0].rearrange("(k p) n -> p k n", p=P)

        def results_read(j):
            mine = PROJECTIONS[j - JOB_NA][0] == "q"
            n = sum((kind == "q") == mine for kind, _ in PROJECTIONS[:j - JOB_NA + 1])
            return (q_read if mine else kv_read), n

        def ada_groups(j):
            return [g for g, job in enumerate(ADA_JOBS) if job == j]

        def ada_bank(j):
            return 4 * (j % 2) + 3

        def rotation(n):
            if n < 4:
                return kT, 2 * n, 4 + n
            return qT, 2 * (n - 4), (n - 4 if n < 6 else 5)

        LATE_ROTATIONS = {1: 6, 3: 7}

        def is_first(j):
            return isinstance(j, int) and j == 0

        @block.sync
        def _(sp):
            def load(j, s, src, parts=2):
                if not is_first(j):
                    sp.wait_ge(lo_ready[s], j)
                dst = raw[:, s, :].rearrange("p (a n) -> p a n", a=parts)
                sp.dma_start(dst, src).then_inc(raw_landed[s], 16)

            sp.dma_start(ident, constants[:, C_IDENT:C_IDENT + P]).then_inc(ident_landed, 16)
            sp.dma_start(param_rows[0:16, 0, :], c.rearrange("a (k p) -> (a k) p", p=P)).then_inc(rows_landed, 16)
            sp.dma_start(param_rows[16:32, 0, :], c_ctx.rearrange("(k p) -> k p", p=P)).then_inc(rows_landed, 16)
            for u, (kind, *unit) in enumerate(HEAD):
                if kind == "ada":
                    block, kc = unit
                    load(u // SLOTS, u % SLOTS, ada_v[:, kc:kc + 1, UNIT * block:UNIT * (block + 1)], parts=1)
                else:
                    s, = unit
                    load(u // SLOTS, u % SLOTS, w_in_v[:, 2 * s:2 * s + 2, KA:KA + GROUP])
                if u == SLOTS:
                    sp.dma_start(consts[:, P:C_ALL], constants[:, P:C_ALL]).then_inc(consts_landed, 16)
                if u == BLOCK_ENDS[0]:
                    sp.dma_start(tokens[:, 0:TOK, :],
                                 x[0].rearrange("(t p) n -> p t n", p=P)).then_inc(tokens_landed, 16)
                    sp.dma_start(tokens[:, TOK:2 * TOK, :],
                                 ctx[0].rearrange("(t p) n -> p t n", p=P)).then_inc(tokens_landed, 16)
            for n, (_, col) in list(enumerate(PROJECTIONS))[1:]:
                for s in range(SLOTS):
                    load(JOB_NA + n, s, w_in_v[:, 2 * s:2 * s + 2, col:col + GROUP])
            with sp.Fori(1, D // GROUP + 1) as g:
                jobs = [sp.snap(3 * g + (JOB_MERGE - 3 + n)) for n in range(3)]
                cols = [g * GROUP + (col - GROUP) for col in (GATE_A, GATE_B, 0)]
                for n in range(2):
                    for s in range(SLOTS):
                        load(jobs[n], s, w_in_v[:, 2 * s:2 * s + 2, bass.ds(cols[n], GROUP)])
                col = cols[2]
                for s in range(SLOTS):
                    src = (pa_v, pb_v)[s // 4]
                    load(jobs[2], s, src[:, 2 * (s % 4):2 * (s % 4) + 2, bass.ds(col, GROUP)])
            with sp.Fori(1, D // GROUP + 1) as g:
                job, col = sp.snap(g + (JOB_OUT - 1)), g * GROUP - GROUP
                for s in range(SLOTS):
                    load(job, s, out_v[:, 2 * s:2 * s + 2, bass.ds(col, GROUP)])
            with sp.Fori(1, FF_GROUPS + 1) as g:
                jobs = [sp.snap(2 * g + (JOB_UP - 2 + half)) for half in range(2)]
                cols = [g * GROUP + (half * D_FF - GROUP) for half in range(2)]
                for half in range(2):
                    for s in range(SLOTS):
                        load(jobs[half], s, up_v[:, 2 * s:2 * s + 2, bass.ds(cols[half], GROUP)])
            with sp.Fori(1, FF_GROUPS) as g:
                job = sp.snap(g + (JOB_DOWN - 1))
                rows = [TILES * g + (t - TILES) for t in range(TILES)]
                for s in range(SLOTS):
                    load(job, s, down_v[:, bass.ds(rows[s // 2], 1), UNIT * (s % 2):UNIT * (s % 2) + UNIT],
                         parts=1)
            for s in range(SLOTS):
                row, half = FF_TILES - TILES + s % TILES, s // TILES
                load(JOB_DOWN + FF_GROUPS - 1, s, down_v[:, row:row + 1, UNIT * half:UNIT * (half + 1)], parts=1)
            for t, half, ready, count in ((0, 0, out_ready, 1), (0, 1, out_ready, 2), (1, 0, out1_ready, 1),
                                          (1, 1, out_ready, 3)):
                at = slice(half * UNIT, (half + 1) * UNIT)
                sp.wait_ge(ready, count)
                sp.dma_start(out[0, t * P:(t + 1) * P, at], final_tmp[:, t, at]).then_inc(out_stored, 16)
            sp.wait_ge(out_stored, 16 * 2 * TOK)

        @block.gpsimd
        def _(pool):
            pool.memset(zeros[:], 0.0).then_inc(zeros_ready, 1)
            pool.dma_start(lam_in[:], diff_lambda.rearrange("a m d -> a (m d)").to_broadcast([P, 4 * MAP_DIM]))\
                .then_inc(lam_landed, 16)

            def load_ada(g, skip_wait=False, between=lambda pair: None):
                for pair in range(KC // 2):
                    if not (skip_wait and pair < ADA_SLOTS):
                        pool.wait_ge(ada_summed, KC * g + 2 * (pair - ADA_SLOTS + 1))
                    pool.dma_start(ada_raw[:, pair % ADA_SLOTS, :, :],
                                   ada_v[:, 2 * pair:2 * pair + 2, bass.ds(g * GROUP + ADA_FIRST_COL, GROUP)])\
                        .then_inc(ada_landed[pair % ADA_SLOTS], 16)
                    between(pair)

            pool.wait_ge(mod_cols_ready, 2)
            pool.wait_ge(zeros_ready, 1)
            pool.dma_start(rpb_grid.ap().rearrange("p (a n) -> p a n", a=ZERO_PARTS),
                           zeros[:].unsqueeze(1)
                           .to_broadcast([HEADS * RPB_ROWS, ZERO_PARTS, RPB_BLOCK // ZERO_PARTS]))\
                .then_inc(padded, 16)

            def scatter_bias(pair):
                if pair == ADA_SLOTS - 1:
                    pool.wait_ge(padded, 16)
                    pool.dma_start(bass.AP(rpb_grid, RPB_MARGIN - (WIN_COLS - 1),
                                           [[RPB_BLOCK, HEADS * RPB_ROWS], [GRID_W + 1, GRID_W], [1, RPB_COLS]]),
                                   na_rpb[0].rearrange("h r w -> (h r) w").unsqueeze(1)
                                   .to_broadcast([HEADS * RPB_ROWS, GRID_W, RPB_COLS])).then_inc(padded, 16)

            load_ada(0, skip_wait=True, between=scatter_bias)
            pool.wait_ge(padded, 32)

            def load_bias(h, r):
                src = bass.AP(rpb_grid, (h * RPB_ROWS + WIN_ROWS - 1 - r) * RPB_BLOCK + RPB_MARGIN,
                              [[GRID_W, GRID_W], [RPB_BLOCK, ROWS], [1, GRID_W]])
                dst = bias[(r % 2) * GRID_W:(r % 2 + 1) * GRID_W, h % 2,
                           (r // 2) * SEQ:(r // 2 + 1) * SEQ].rearrange("p (a b) -> p a b", a=ROWS)
                pool.dma_start(dst, src).then_inc(bias_landed[h % 2], 16)

            def load_first_biases(pair):
                load_bias(pair // ROWS, pair % ROWS)

            pool.wait_ge(hT_ready, KC)
            load_ada(1, between=load_first_biases)
            with pool.Fori(2, ADA_BEFORE_NA) as g:
                load_ada(g)
            for h in range(2, HEADS):
                pool.wait_ge(na_biased, TOK * (h - 1))
                for r in range(ROWS):
                    load_bias(h, r)
            pool.wait_ge(na_out, HEADS * TOK)
            with pool.Fori(ADA_BEFORE_NA, ADA_GROUPS) as g:
                load_ada(g)
            pool.wait_ge(mod_ready, ADA_GROUPS)
            pool.wait_ge(bT_ready, 1)
            pool.dma_start(x2[:], x[0].rearrange("(t p) n -> p t n", p=P)).then_inc(x2_landed, 16)
            pool.wait_ge(used[7], JOB_OUT)
            pool.dma_start(final_rows[:], final_norm_g.rearrange("(a n) -> a n", a=1).to_broadcast([P, D]))\
                .then_inc(final_landed, 16)

        @block.scalar
        def _(act):
            def round_hi(j, s):
                act.wait_ge(raw_landed[s], 16 * j + 16)
                if s >= SPLIT_SLOTS:
                    act.wait_ge(used[s - SPLIT_SLOTS], j + 1)
                elif not is_first(j):
                    act.wait_ge(used[s + SPLIT_SLOTS], j)
                act.copy(w_hi[:, s % SPLIT_SLOTS, :], raw[:, s, :]).then_inc(hi_ready[s], 1)

            def warm_up(func):
                act.activation(warm[:], ones[:], func)

            act.wait_ge(ones_ready, 1)
            warm_up(ACT.Exp)
            act.wait_ge(vecs_ready, 1)
            act.activation(exp_c[:], vecs[:, V_C:V_C + 2 * KC], ACT.Exp, scale=-1.0).then_inc(exp_c_ready, 1)
            def read_mod_rows(i):
                u, block, b = BLOCK_ENDS[i], ADA_BLOCKS[i], 4 + 2 * (i % 2)
                act.wait_ge(used[u % SLOTS], u // SLOTS + 1)
                act.copy(mod_rows[:, block * UNIT:(block + 1) * UNIT].rearrange("p (a n) -> p a n", a=2),
                         ps[0:4, b:b + 2, :]).then_inc(mod_rows_ready, 1)

            def modulate(kc):
                act.wait_ge(mod1_ready, kc // 8 + 1)
                act.wait_ge(tokens_turned, kc + 1)
                if kc >= 4:
                    act.wait_ge(hT_ready, kc - 3)
                for st in range(2):
                    act.activation(modulated[:, kc % 4, st, :], ps[:, TURN_BANKS[kc], st * SEQ:(st + 1) * SEQ],
                                   ACT.Identity, bias=shift1[:, st, kc:kc + 1],
                                   scale=gain1[:, st, kc:kc + 1]).then_inc(modulated_ready, 1)

            def read_result(j):
                kind, col = PROJECTIONS[j - JOB_NA]
                g = (col // GROUP) % 2
                b = 4 * (j % 2)
                act.wait_ge(used[7], j + 1)
                if kind == "k":
                    act.copy(kT[:, TILES * g:TILES * (g + 1), :], ps[:, b:b + 4, :]).then_inc(kv_read, 1)
                elif kind == "v":
                    act.copy(v_sb[:, :, g * GROUP:(g + 1) * GROUP], ps[:, b:b + 4, :])\
                        .then_inc(kv_read, 1)
                else:
                    act.copy(qT[:, TILES * g:TILES * (g + 1), :], ps[:, b:b + 4, 0:SEQ]).then_inc(half_read, 1)

            squares_after = {BLOCK_ENDS[0] + 3 + 2 * t: t for t in range(2 * TOK)}

            def by_row(vector):
                return vector.rearrange("a (k p) -> (a k) p", p=P)

            other_rows = [(param_rows[0:96, 1, :], by_row(ada_b)),
                          (param_rows[96:96 + KC, 1, :], by_row(norm1_g)),
                          (param_rows[96 + KC:P, 1, :], by_row(norm2_g))]
            other_rows += [(param_rows[0:2 * FF_TILES, 2 + tap, :], by_row(ffn_conv_w[0, tap:tap + 1, :]))
                           for tap in range(TAPS)]
            other_rows += [(param_rows[0:2 * FF_TILES, 5, :], by_row(ffn_conv_b)),
                           (param_rows[2 * FF_TILES:2 * FF_TILES + 1, 5, :], diff_norm_g)]
            for u in range(len(HEAD)):
                round_hi(u // SLOTS, u % SLOTS)
                if 3 <= u < 3 + len(other_rows):
                    dst, src = other_rows[u - 3]
                    act.dma_start(dst, src).then_inc(rows2_landed, 16)
                if u == 5:
                    act.wait_ge(lam_step, 2)
                    act.activation(lam[:], lam[:], ACT.Exp).then_inc(lam_exp, 1)
                if u in squares_after:
                    t = squares_after[u]
                    if t == 0:
                        act.wait_ge(tokens_landed, 32)
                        act.wait_ge(lam_step, 2)
                    else:
                        act.wait_ge(squares1, t)
                    act.activation(junk[:], tokens[:, t, :], ACT.Square,
                                   accum_out=rms1[:, t:t + 1]).then_inc(squares1, 1)
                if u == BLOCK_ENDS[0] + 11:
                    act.wait_ge(rms1_step, 1)
                    act.activation(rms1[:], rms1[:], ACT.Sqrt).then_inc(rms1_step, 1)
                if u - 3 in BLOCK_ENDS[:3]:
                    read_mod_rows(BLOCK_ENDS.index(u - 3))
                for kc in MODULATE_AFTER.get(u - MID, ()):
                    modulate(kc)
                if u == K_UNITS[6]:
                    read_mod_rows(3)
                    for kc in range(8, 11):
                        modulate(kc)
            modulate(11)
            modulate(12)
            round_hi(JOB_NA + 1, 0)
            modulate(13)
            modulate(14)
            round_hi(JOB_NA + 1, 1)
            modulate(15)

            for j in range(JOB_NA + 1, JOB_DIFF):
                for s in range(SLOTS):
                    if j > JOB_NA + 1 or s >= 2:
                        round_hi(j, s)
                    if s == 3:
                        read_result(j - 1)
            for s in range(SPLIT_SLOTS - 1):
                round_hi(JOB_DIFF, s)

            def scale_ctx(n):
                act.wait_ge(na_scored, n + 1)
                if n >= 3:
                    act.wait_ge(na_turned, n - 2)
                act.mul(scores[:, n % 3, SEQ:2 * SEQ], ps[:, 2 + n % 2, 0:SEQ], NA_SCALE)\
                    .then_inc(na_ctx_scaled, 1)

            def na_exponent(n):
                act.wait_ge(na_max, n + 1)
                act.activation(scores[:, n % 3, :], scores[:, n % 3, :], ACT.Exp, bias=row_max[:, n % 3, 0:1],
                               accum_out=row_sum[:, n % 3, 0:1]).then_inc(na_exp, 1)

            N = HEADS * TOK
            warm_up(ACT.Exp)
            act.wait_ge(ada_summed, KC * ADA_BEFORE_NA)
            scale_ctx(0)
            scale_ctx(1)
            na_exponent(0)
            read_result(JOB_DIFF - 1)
            for n in range(N):
                if n + 2 < N:
                    scale_ctx(n + 2)
                if n + 1 < N:
                    na_exponent(n + 1)
                act.wait_ge(na_turned, n + 1)
                if n >= 1:
                    act.wait_ge(na_summed, n)
                act.copy(na_pT[:], ps[:, 6 + n % 2, :].rearrange("p (a b) -> p a b", a=4)).then_inc(na_pT_ready, 1)

            for j in range(JOB_DIFF, JOB_MERGE):
                for s in range(SLOTS):
                    if j > JOB_DIFF or s >= SPLIT_SLOTS - 1:
                        round_hi(j, s)
                    if s == 3 and j > JOB_DIFF:
                        read_result(j - 1)
                    if s == 4 and j == JOB_MERGE - 1:
                        act.wait_ge(na_out, HEADS * TOK)
                        act.copy(aT_hi[:], aT[:]).then_inc(aT_hi_ready, 1)
            for s in range(SPLIT_SLOTS - 1):
                round_hi(JOB_MERGE, s)

            def df_exponents(n):
                act.wait_ge(df_bias, n + 1)
                if n >= 2:
                    act.wait_ge(df_turned, n - 1)
                for m in range(2):
                    act.activation(diff_e[:, n % 2, m, :], ps[:, 2 * (n % 2) + m, :], ACT.Exp,
                                   bias=row_max[:, n % 3, m:m + 1], scale=DIFF_SCALE,
                                   accum_out=row_sum[:, n % 3, m:m + 1]).then_inc(df_exp, 1)

            warm_up(ACT.Exp)
            act.wait_ge(ada_summed, KC * ADA_GROUPS)
            df_exponents(0)
            read_result(JOB_MERGE - 1)
            for n in range(N):
                if n + 1 < N:
                    df_exponents(n + 1)
                act.wait_ge(df_turned, n + 1)
                if n >= 2:
                    act.wait_ge(df_summed, n - 1)
                act.copy(diff_pT[:, n % 2, :, :], ps[:, 4, :].rearrange("p (a b) -> p a b", a=4))\
                    .then_inc(df_pT_ready, 1)
                if n >= 1:
                    act.wait_ge(df_summed, n)
                    act.copy(diff_o[:, n - 1, :], ps[:, 6 + (n - 1) % 2, 0:P]).then_inc(df_out, 1)
            act.wait_ge(df_summed, N)
            act.copy(diff_o[:, N - 1, :], ps[:, 6 + (N - 1) % 2, 0:P]).then_inc(df_out, 1)
            for s in (SPLIT_SLOTS - 1, SPLIT_SLOTS):
                round_hi(JOB_MERGE, s)
            act.wait_ge(o_step, 3)
            act.activation(rms_o[:], rms_o[:], ACT.Sqrt).then_inc(o_step, 1)

            for s in range(SPLIT_SLOTS + 1, SLOTS):
                round_hi(JOB_MERGE, s)
            for s in range(2):
                round_hi(JOB_MERGE + 1, s)
            act.wait_ge(o_turned, 1)
            act.mul(bT[:].rearrange("p h q -> p (h q)"), ps[:, 4:8, :].rearrange("p a n -> p (a n)"), dng[:])\
                .then_inc(bT_scaled, 1)
            act.wait_ge(bT_scaled, 1)
            act.copy(bT_hi[:], bT[:]).then_inc(bT_hi_ready, 1)

            def turn_hi(g):
                act.wait_ge(y_turned, g + 1)
                act.copy(yT_hi[:, bass.ds(g * TILES, TILES), :],
                         ps[:, 4:6, :].rearrange("p a (b q) -> p (a b) q", b=2)).then_inc(yT_hi_ready, 1)

            def merge_group(g, first):
                j = 3 * g + JOB_MERGE
                if not first:
                    for s in range(SLOTS):
                        round_hi(j, s)
                    turn_hi(g - 1)
                for s in range(SLOTS):
                    if not first or s >= 2:
                        round_hi(j + 1, s)
                    if s == 3:
                        act.wait_ge(used[7], j + 1)
                        if not first:
                            act.wait_ge(y_a, g)
                        else:
                            act.wait_ge(bT_ready, 1)
                        act.activation(sig_a[:], ps[:, 0:2, :], ACT.Sigmoid).then_inc(sig_a_ready, 1)
                if first:
                    act.wait_ge(g1_spread, 1)
                    act.copy(g1_rows[:], ps[:, 4:8, :].rearrange("p a n -> p (a n)")).then_inc(g1_ready, 1)
                for s in range(SLOTS):
                    round_hi(j + 2, s)
                    if s == 3:
                        act.wait_ge(used[7], j + 2)
                        if not first:
                            act.wait_ge(y_ready, g)
                        act.activation(sig_b[:], ps[:, 2:4, :], ACT.Sigmoid).then_inc(sig_b_ready, 1)

            merge_group(0, True)
            with act.Fori(1, D // GROUP) as g:
                merge_group(g, False)

            def square_group(g):
                for t in range(TOK):
                    act.wait_ge(x2_added, TOK * g + t + 1)
                    if g or t:
                        act.wait_ge(squares2, TOK * g + t)
                    act.activation(sig_b[:, t, :], x2[:, t, g * GROUP:(g + 1) * GROUP], ACT.Square,
                                   accum_out=ssq2[:, t, g:g + 1]).then_inc(squares2, 1)

            for g in range(4):
                for s in range(SLOTS):
                    round_hi(JOB_OUT + g, s)
                    if s == 4 and g:
                        square_group(g - 1)
                if g == 0:
                    turn_hi(3)
            for s in range(SPLIT_SLOTS):
                round_hi(JOB_UP, s)
            warm_up(ACT.Sqrt)
            square_group(3)
            act.wait_ge(rms2_step, 2)
            act.activation(rms2[:], rms2[:], ACT.Sqrt).then_inc(rms2_step, 1)
            act.wait_ge(g2_spread, 1)
            act.copy(g2_rows[:], ps[:, 0:4, :].rearrange("p a n -> p (a n)")).then_inc(g2_ready, 1)
            act.wait_ge(gain2_ready, 2)

            def modulate2(m):
                act.wait_ge(x2_turned, m + 1)
                if m >= 4:
                    act.wait_ge(h2T_ready, m - 3)
                for h in range(2):
                    kc = 2 * m + h
                    act.activation(modulated2[:, m % 4, h, :], ps[:, 4 + m % 4, h * SEQ:(h + 1) * SEQ],
                                   ACT.Identity, bias=mod[:, KC + kc:KC + kc + 1],
                                   scale=gain2[:, kc:kc + 1]).then_inc(modulated2_ready, 1)

            for m in range(4):
                modulate2(m)
            for s in range(SPLIT_SLOTS):
                modulate2(s + 4)
                round_hi(JOB_UP, s + SPLIT_SLOTS)

            def conv_begin(n, b):
                act.wait_ge(used[7], n + JOB_UP + 1)
                if not is_first(n):
                    act.wait_ge(conv_done, n)
                act.copy(conv_in[:], ps[:, b:b + 4, 0:SEQ]).then_inc(up_half_read, 1)

            def conv_middle(n, tile, dst):
                act.wait_ge(up_read, n + 1)
                for t in range(TILES):
                    act.activation(dst[:, t, :], conv_in[:, t, :], ACT.Identity,
                                   bias=vecs[:, bass.ds(tile + (V_CONVB + t), 1)],
                                   scale=vecs[:, bass.ds(tile + (V_CONV + 88 + t), 1)]).then_inc(conv_mid, 1)

            def gate_steps(i, s):
                n = 2 * i
                if s == 3:
                    conv_begin(n, 0)
                if s == 4:
                    if not is_first(i):
                        act.wait_ge(hidden_ready, i)
                    conv_middle(n, TILES * i, conv_gate)
                if s == 6:
                    act.wait_ge(conv_done, n + 1)
                    act.activation(conv_gate[:], conv_gate[:], ACT.Silu).then_inc(gate_done, 1)

            def up_steps(i, s):
                n = 2 * i + 1
                if s == 3:
                    conv_begin(n, 4)
                if s == 4:
                    conv_middle(n, TILES * i + FF_TILES, conv_up)

            def ffn_pair(i, first):
                for s in range(SLOTS):
                    if not first:
                        round_hi(2 * i + JOB_UP, s)
                        up_steps(i - 1, s)
                for s in range(SLOTS):
                    round_hi(2 * i + JOB_UP + 1, s)
                    gate_steps(i, s)

            ffn_pair(0, True)
            with act.Fori(1, FF_GROUPS) as i:
                ffn_pair(i, False)

            def f_high(i, t, first):
                if not first:
                    act.wait_ge(used[2 * t + 1], i + JOB_DOWN)
                act.copy(f_hi[:, t:t + 1, :], hidden[:, bass.ds(TILES * i + t, 1), :])\
                    .then_inc(f_hi_ready, 1)

            def down_job(i, first, last=False):
                for s in range(SLOTS):
                    round_hi(i + JOB_DOWN, s)
                    if last and s < TILES:
                        f_high(i, s, first)
                    if not last and s % 2 == 0:
                        f_high(i, s // 2, first)
                    if first:
                        up_steps(FF_GROUPS - 1, s)
                        if s == 6:
                            act.wait_ge(hidden_ready, FF_GROUPS)

            down_job(0, True)
            with act.Fori(1, FF_GROUPS - 1) as i:
                down_job(i, False)
            down_job(FF_GROUPS - 1, False, last=True)

            warm_up(ACT.Sqrt)
            for half in range(2):
                for t in range(TOK):
                    if half or t:
                        act.wait_ge(squares3, TOK * half + t)
                    act.wait_ge(x3_ready, TOK * half + t + 1)
                    act.activation(squares_out[:], x2[:, t, half * UNIT:(half + 1) * UNIT], ACT.Square,
                                   accum_out=ssq3[:, t, half:half + 1]).then_inc(squares3, 1)
                    if half == 1:
                        act.wait_ge(rms3_step, 4 * t + 2)
                        act.activation(rms3[:, t:t + 1], rms3[:, t:t + 1], ACT.Sqrt).then_inc(rms3_step, 1)
            act.wait_ge(rms3_step, 8)
            act.wait_ge(x3_weighted, TOK)
            part = final_tmp[:, 1, 0:UNIT]
            act.mul(part, part, rms3[:, 1:2]).then_inc(out1_ready, 1)

        @block.vector
        def _(dve):
            def split_lo(j, s):
                dve.wait_ge(hi_ready[s], j + 1)
                dve.tensor_tensor(w_lo[:, s % SPLIT_SLOTS, :], raw[:, s, :], w_hi[:, s % SPLIT_SLOTS, :],
                                  ALU.subtract).then_inc(lo_ready[s], 1)

            steps = 0

            def step(ins):
                nonlocal steps
                steps += 1
                ins.then_inc(start_dve, 1)
                dve.wait_ge(start_dve, steps)

            dve.memset(ones[:], 1.0).then_inc(ones_ready, 1)
            step(dve.memset(c_parts[:].bitcast(F32), 0.0))
            dve.wait_ge(vecs_turned, 1)
            dve.tensor_copy(vecs[:, 0:2 * KC], ps[:, 5, 0:2 * KC]).then_inc(vecs_ready, 1)
            dve.wait_ge(vecs_ready, 1)
            dve.wait_ge(exp_c_ready, 1)
            step(dve.tensor_scalar(exp_c[:], exp_c[:], 1.0, None, ALU.add))
            step(dve.reciprocal(exp_c[:], exp_c[:]))
            step(dve.tensor_tensor(silu_c[:], vecs[:, V_C:V_C + 2 * KC], exp_c[:], ALU.mult))
            for st in range(2):
                part = c_parts[:, 0:4 * KC].rearrange("p (k f) -> p f k", f=4)
                step(dve.tensor_copy(part[:, 2 * st, :], silu_c[:, st * KC:(st + 1) * KC]))
                dve.tensor_tensor(part[:, 2 * st + 1, :], silu_c[:, st * KC:(st + 1) * KC], part[:, 2 * st, :],
                                  ALU.subtract).then_inc(c_ready, 1)
            def modulation1(half):
                n = KC // 2
                at = slice(half * n, (half + 1) * n)
                sums = ps[:, (3, 5)[half], 0:4 * KC].rearrange("p (m k s) -> p m s k", m=2, s=2)[:, :, :, at]

                def spread(v):
                    return vecs[:, v + half * n:v + (half + 1) * n].unsqueeze(1).to_broadcast([P, 2, n])

                dve.wait_ge(mod_cols_ready, half + 1)
                dve.wait_ge(vecs_ready, 4)
                dve.tensor_tensor(shift1[:, :, at], sums[:, 0], spread(V_ADAB), ALU.add).then_inc(mod1_step, 1)
                dve.tensor_tensor(gain1[:, :, at], sums[:, 1], spread(V_ADAB + KC), ALU.add)\
                    .then_inc(mod1_step, 1)
                dve.wait_ge(mod1_step, 2 * half + 2)
                dve.scalar_tensor_tensor(gain1[:, :, at], gain1[:, :, at], 1.0, spread(V_N1), ALU.add, ALU.mult)\
                    .then_inc(mod1_ready, 1)

            def split_modulated(kc):
                dve.wait_ge(modulated_ready, 2 * kc + 2)
                dve.tensor_copy(hT[:, :, 0, kc, :], modulated[:, kc % 4, :, :]).then_inc(hT_hi_ready, 1)
                dve.wait_ge(hT_hi_ready, kc + 1)
                dve.tensor_tensor(hT[:, :, 1, kc, :], modulated[:, kc % 4, :, :], hT[:, :, 0, kc, :],
                                  ALU.subtract).then_inc(hT_ready, 1)

            def ada_step(g, kc):
                slot, turns = kc // 2 % ADA_SLOTS, KC // 2 // ADA_SLOTS
                dve.wait_ge(ada_landed[slot], 16 * (turns * g + kc // 2 // ADA_SLOTS + 1))
                raw_columns = ada_raw[:, slot, kc % 2, :]
                acc = ada_acc[:, g % 2, :]
                if kc == 0:
                    if g >= 2:
                        dve.wait_ge(mod_summed, g - 1)
                    dve.tensor_scalar(acc, raw_columns, silu_c[:, 0:1], None, ALU.mult)\
                        .then_inc(ada_summed, 1)
                else:
                    dve.wait_ge(ada_summed, KC * g + kc)
                    dve.scalar_tensor_tensor(acc, raw_columns, silu_c[:, kc:kc + 1], acc,
                                             ALU.mult, ALU.add).then_inc(ada_summed, 1)

            def read_mod(j):
                groups = ada_groups(j - 1)
                if groups:
                    first, n = 4 * groups[0], 4 * len(groups)
                    dve.wait_ge(mod_summed, groups[-1] + 1)
                    dve.tensor_tensor(mod[:, first:first + n], ps[:, ada_bank(j), 0:n],
                                      vecs[:, V_ADAB + 2 * KC + first:V_ADAB + 2 * KC + first + n],
                                      ALU.add).then_inc(mod_ready, len(groups))

            def read_result(j):
                kind, col = PROJECTIONS[j - JOB_NA]
                if kind != "q":
                    return
                g = (col // GROUP) % 2
                b = 4 * (j % 2)
                q = qT[:, TILES * g:TILES * (g + 1), :]
                dve.wait_ge(half_read, g + 1 + (2 if j >= JOB_DIFF else 0))
                dve.tensor_tensor(q, q, ps[:, b:b + 4, SEQ:2 * SEQ], ALU.add).then_inc(q_read, 1)

            def ada_steps(j, s):
                steps = [(g, kc) for g in ada_groups(j) for kc in range(KC)]
                n = len(steps) // SLOTS
                for g, kc in steps[s * n:(s + 1) * n]:
                    ada_step(g, kc)

            for u in range(len(HEAD)):
                split_lo(u // SLOTS, u % SLOTS)
                if u == 5:
                    dve.wait_ge(lam_landed, 16)
                    for m in range(2):
                        dve.tensor_tensor_reduce(lam_prod[:, m, :], lam_in[:, 2 * m * MAP_DIM:(2 * m + 1) * MAP_DIM],
                                                 lam_in[:, (2 * m + 1) * MAP_DIM:(2 * m + 2) * MAP_DIM], 1.0, 0.0,
                                                 ALU.mult, ALU.add, lam[:, m:m + 1]).then_inc(lam_step, 1)
                    dve.wait_ge(lam_exp, 1)
                    step(dve.tensor_tensor(lam[:, 0:1], lam[:, 1:2], lam[:, 0:1], ALU.subtract))
                    dve.tensor_scalar(lam[:, 0:1], lam[:, 0:1], -LAMBDA_INIT, None, ALU.add).then_inc(lam_ready, 1)
                if u == BLOCK_ENDS[0] + 1:
                    dve.wait_ge(vecs_turned, 2)
                    dve.tensor_copy(vecs[:, 2 * KC:512], ps[:, 6, 2 * KC:512]).then_inc(vecs_ready, 1)
                    dve.tensor_copy(vecs[:, 512:513], ps[:, 7, 88:89]).then_inc(vecs_ready, 1)
                    dve.wait_ge(vecs_ready, 3)
                    dve.tensor_scalar(dng[:], vecs[:, V_DNG:V_DNG + 1], 1.0 - LAMBDA_INIT, None, ALU.mult)\
                        .then_inc(vecs_ready, 1)
                if u == BLOCK_ENDS[0] + 10:
                    dve.wait_ge(squares1, 4)
                    dve.tensor_scalar(rms1[:], rms1[:], 1.0 / D, EPS, ALU.mult, ALU.add).then_inc(rms1_step, 1)
                if u == BLOCK_ENDS[0] + 11:
                    dve.wait_ge(rms1_step, 2)
                    dve.reciprocal(rms1[:], rms1[:]).then_inc(rms1_step, 1)
                    dve.wait_ge(rms1_step, 3)
                if BLOCK_ENDS[0] + 11 <= u <= BLOCK_ENDS[0] + 14:
                    t = u - (BLOCK_ENDS[0] + 11)
                    dve.tensor_scalar(tokens[:, t, :], tokens[:, t, :], rms1[:, t:t + 1], None, ALU.mult)\
                        .then_inc(normed1, 1)
                if u == MID + 7:
                    modulation1(0)
                for kc in SPLIT_AFTER.get(u - MID, ()):
                    split_modulated(kc)
                if u == K_UNITS[6]:
                    modulation1(1)
                    for kc in range(8, 11):
                        split_modulated(kc)
            split_modulated(11)
            split_modulated(12)
            split_lo(JOB_NA + 1, 0)
            split_modulated(13)
            split_modulated(14)
            split_lo(JOB_NA + 1, 1)
            split_modulated(15)

            for j in range(JOB_NA + 1, JOB_DIFF):
                for s in range(SLOTS):
                    if s == 3:
                        read_mod(j)
                    if j > JOB_NA + 1 or s >= 2:
                        split_lo(j, s)
                    if s == 3:
                        read_result(j - 1)
                    ada_steps(j, s)
            for s in range(SPLIT_SLOTS - 1):
                split_lo(JOB_DIFF, s)

            mask = consts[:, C_MASK:C_MASK + GRID_W].unsqueeze(1).to_broadcast([P, TOK * ROWS, GRID_W])

            def na_bias(n):
                h, t = divmod(n, TOK)
                if t == 0:
                    dve.wait_ge(bias_landed[h % 2], 64 * (h // 2 + 1))
                    b = bias[:, h % 2, :].rearrange("p (a b) -> p a b", b=GRID_W)
                    dve.tensor_tensor(b, b, mask, ALU.add).then_inc(bias_ready, 1)
                    dve.wait_ge(bias_ready, h + 1)
                dve.wait_ge(na_scored, n + 1)
                if n >= 3:
                    dve.wait_ge(na_turned, n - 2)
                dve.scalar_tensor_tensor(scores[:, n % 3, 0:SEQ], ps[:, n % 2, 0:SEQ], NA_SCALE,
                                         bias[:, h % 2, t * SEQ:(t + 1) * SEQ], ALU.mult, ALU.add)\
                    .then_inc(na_biased, 1)
                dve.wait_ge(na_biased, n + 1)
                dve.wait_ge(na_ctx_scaled, n + 1)
                dve.tensor_reduce(row_max[:, n % 3, 0:1], scores[:, n % 3, :], AX.X, ALU.max, negate=True)\
                    .then_inc(na_max, 1)

            def na_result(n):
                h, t = divmod(n, TOK)
                dve.wait_ge(na_summed, n + 1)
                dve.tensor_copy(aT[:, h, t * P:(t + 1) * P], ps[:, 4 + n % 2, 0:P]).then_inc(na_out, 1)

            N = HEADS * TOK
            dve.wait_ge(ada_summed, KC * ADA_BEFORE_NA)
            na_bias(0)
            na_bias(1)
            read_result(JOB_DIFF - 1)
            for n in range(N):
                dve.wait_ge(na_exp, n + 1)
                dve.reciprocal(row_sum[:, n % 3, 0:1], row_sum[:, n % 3, 0:1]).then_inc(na_recip, 1)
                dve.wait_ge(na_recip, n + 1)
                dve.tensor_scalar(scores[:, n % 3, :], scores[:, n % 3, :], row_sum[:, n % 3, 0:1], None, ALU.mult)\
                    .then_inc(na_probs, 1)
                if n + 2 < N:
                    na_bias(n + 2)
                if n >= 1:
                    na_result(n - 1)
            na_result(N - 1)

            cos = consts[:, C_COS:C_COS + SEQ].unsqueeze(1).to_broadcast([P, 2, SEQ])
            sin = consts[:, C_SIN:C_SIN + SEQ].unsqueeze(1).to_broadcast([P, 2, SEQ])

            def rope(n):
                t, h, b = rotation(n)
                x = t[:, h:h + 2, 0:SEQ]
                dve.wait_ge(rotated, n + 1)
                if n >= 2:
                    dve.wait_ge(roped, n - 1)
                dve.tensor_tensor(rope_tmp[:, n % 2, :, :], ps[:, b, :].rearrange("p (a q) -> p a q", a=2), sin,
                                  ALU.mult).then_inc(rope_sin, 1)
                dve.tensor_tensor(x, x, cos, ALU.mult).then_inc(rope_cos, 1)
                dve.wait_ge(rope_sin, n + 1)
                dve.wait_ge(rope_cos, n + 1)
                dve.tensor_tensor(x, x, rope_tmp[:, n % 2, :, :], ALU.add).then_inc(roped, 1)

            for j in range(JOB_DIFF, JOB_MERGE):
                for s in range(SLOTS):
                    if s == (3 if j > JOB_DIFF else 0):
                        read_mod(j)
                    if j > JOB_DIFF or s >= SPLIT_SLOTS - 1:
                        split_lo(j, s)
                    if s == 3 and j > JOB_DIFF:
                        read_result(j - 1)
                    ada_steps(j, s)
                    if j == JOB_MERGE - 2 and s >= 4:
                        rope(s - 4)
                    if j == JOB_MERGE - 1:
                        if s == 7:
                            dve.wait_ge(aT_hi_ready, 1)
                            dve.tensor_tensor(aT_lo[:], aT[:], aT_hi[:], ALU.subtract).then_inc(aT_ready, 1)
                        if s in (4, 5):
                            rope(s)
            for s in range(SPLIT_SLOTS - 1):
                split_lo(JOB_MERGE, s)

            def df_maxima(n):
                dve.wait_ge(df_scored, 2 * n + 2)
                dve.tensor_reduce(row_max[:, n % 3, :], ps[:, 2 * (n % 2):2 * (n % 2) + 2, :], AX.X, ALU.max,
                                  negate=True).then_inc(df_max, 1)
                dve.wait_ge(df_max, n + 1)
                dve.tensor_scalar(row_max[:, n % 3, :], row_max[:, n % 3, :], DIFF_SCALE, None, ALU.mult)\
                    .then_inc(df_bias, 1)

            dve.wait_ge(lam_ready, 1)
            df_maxima(0)
            df_maxima(1)
            read_result(JOB_MERGE - 1)
            for n in range(N):
                dve.wait_ge(df_exp, 2 * n + 2)
                dve.reciprocal(row_sum[:, n % 3, :], row_sum[:, n % 3, :]).then_inc(df_recip, 1)
                dve.wait_ge(df_recip, n + 1)
                dve.tensor_scalar(row_sum[:, n % 3, 1:2], row_sum[:, n % 3, 1:2], lam[:, 0:1], None, ALU.mult)\
                    .then_inc(df_lam, 1)
                dve.tensor_scalar(diff_e[:, n % 2, 0, :], diff_e[:, n % 2, 0, :], row_sum[:, n % 3, 0:1], None,
                                  ALU.mult).then_inc(df_first, 1)
                dve.wait_ge(df_lam, n + 1)
                dve.wait_ge(df_first, n + 1)
                dve.scalar_tensor_tensor(diff_e[:, n % 2, 0, :], diff_e[:, n % 2, 1, :], row_sum[:, n % 3, 1:2],
                                         diff_e[:, n % 2, 0, :], ALU.mult, ALU.add).then_inc(df_probs, 1)
                if n + 2 < N:
                    df_maxima(n + 2)
                if n in LATE_ROTATIONS:
                    rope(LATE_ROTATIONS[n])
            dve.wait_ge(df_out, N)
            dve.tensor_tensor(diff_sq[:], diff_o[:], diff_o[:], ALU.mult).then_inc(o_step, 1)
            dve.wait_ge(o_step, 1)
            dve.tensor_reduce(rms_o[:], diff_sq[:], AX.X, ALU.add).then_inc(o_step, 1)
            dve.wait_ge(o_step, 2)
            dve.tensor_scalar(rms_o[:], rms_o[:], 1.0 / HD, EPS, ALU.mult, ALU.add).then_inc(o_step, 1)
            for s in (SPLIT_SLOTS - 1, SPLIT_SLOTS):
                split_lo(JOB_MERGE, s)
            dve.wait_ge(o_step, 4)
            dve.reciprocal(rms_o[:], rms_o[:]).then_inc(o_step, 1)
            dve.wait_ge(o_step, 5)
            dve.tensor_tensor(diff_o[:], diff_o[:], rms_o[:].unsqueeze(2).to_broadcast([P, HEADS * TOK, HD]),
                              ALU.mult).then_inc(o_normed, 1)
            for s in range(SPLIT_SLOTS + 1, SLOTS):
                split_lo(JOB_MERGE, s)
            for s in range(2):
                split_lo(JOB_MERGE + 1, s)
            dve.wait_ge(bT_hi_ready, 1)
            dve.tensor_tensor(bT_lo[:], bT[:], bT_hi[:], ALU.subtract).then_inc(bT_ready, 1)

            def merge_y(g, n):
                dve.wait_ge(used[7], 3 * g + JOB_MERGE + 3)
                dve.wait_ge(sig_a_ready, n)
                dve.wait_ge(sig_b_ready, n)
                if not (isinstance(g, int) and g == 0):
                    dve.wait_ge(y_turned, g)
                dve.tensor_tensor(y[:], ps[:, 4:6, :], sig_a[:], ALU.mult).then_inc(y_a, 1)
                dve.tensor_tensor(sig_b[:], ps[:, 6:8, :], sig_b[:], ALU.mult).then_inc(y_b, 1)
                dve.wait_ge(y_a, n)
                dve.wait_ge(y_b, n)
                dve.tensor_tensor(y[:], y[:], sig_b[:], ALU.add).then_inc(y_ready, 1)

            def turn_lo(g):
                dve.wait_ge(yT_hi_ready, g + 1)
                dve.tensor_tensor(yT_lo[:, bass.ds(g * TILES, TILES), :],
                                  ps[:, 4:6, :].rearrange("p a (b q) -> p (a b) q", b=2),
                                  yT_hi[:, bass.ds(g * TILES, TILES), :], ALU.subtract).then_inc(yT_ready, 1)

            def merge_group(g, first):
                j = 3 * g + JOB_MERGE
                if not first:
                    for s in range(SLOTS):
                        split_lo(j, s)
                        if s == 3:
                            merge_y(g - 1, g)
                    turn_lo(g - 1)
                for s in range(SLOTS):
                    if not first or s >= 2:
                        split_lo(j + 1, s)
                for s in range(SLOTS):
                    split_lo(j + 2, s)

            merge_group(0, True)
            with dve.Fori(1, D // GROUP) as g:
                merge_group(g, False)

            def add_out(g):
                if g:
                    dve.wait_ge(x2_added, TOK * g)
                else:
                    dve.wait_ge(g1_ready, 1)
                    dve.wait_ge(x2_landed, 16)
                at = slice(g * GROUP, (g + 1) * GROUP)
                for t in range(TOK):
                    if g == 3 and t == 0:
                        dve.wait_ge(out_tile, 1)
                    else:
                        dve.wait_ge(used[7], JOB_OUT + g + 1)
                    dve.tensor_tensor(sig_a[:, t, :], ps[:, 2 * g + t, :], g1_rows[:, at], ALU.mult)\
                        .then_inc(out_gated, 1)
                    dve.wait_ge(out_gated, TOK * g + t + 1)
                    dve.tensor_tensor(x2[:, t, at], x2[:, t, at], sig_a[:, t, :], ALU.add).then_inc(x2_added, 1)

            for g in range(4):
                for s in range(SLOTS):
                    split_lo(JOB_OUT + g, s)
                    if s == 3:
                        if g == 0:
                            merge_y(3, 4)
                        else:
                            add_out(g - 1)
                if g == 0:
                    turn_lo(3)
            for s in range(SPLIT_SLOTS - 1):
                split_lo(JOB_UP, s)
            add_out(3)
            split_lo(JOB_UP, SPLIT_SLOTS - 1)
            dve.tensor_scalar(gain2[:], mod[:, 2 * KC:3 * KC], 1.0, None, ALU.add).then_inc(gain2_ready, 1)
            dve.wait_ge(gain2_ready, 1)
            dve.tensor_tensor(gain2[:], gain2[:], vecs[:, V_N2:V_N2 + KC], ALU.mult).then_inc(gain2_ready, 1)
            dve.wait_ge(squares2, 4 * TOK)
            dve.tensor_reduce(rms2[:], ssq2[:], AX.X, ALU.add).then_inc(rms2_step, 1)
            dve.wait_ge(rms2_step, 1)
            dve.tensor_scalar(rms2[:], rms2[:], 1.0 / D, EPS, ALU.mult, ALU.add).then_inc(rms2_step, 1)
            dve.wait_ge(rms2_step, 3)
            dve.reciprocal(rms2[:], rms2[:]).then_inc(rms2_step, 1)
            dve.wait_ge(rms2_step, 4)
            for g in range(4):
                for t in range(TOK):
                    dve.tensor_scalar(x2_normed[:, t, g * GROUP:(g + 1) * GROUP],
                                      x2[:, t, g * GROUP:(g + 1) * GROUP], rms2[:, t:t + 1], None, ALU.mult)\
                        .then_inc(x2_norm_ready, 1)

            def split_modulated2(m):
                dve.wait_ge(modulated2_ready, 2 * m + 2)
                dve.tensor_copy(h2T[:, 2 * m:2 * m + 2, 0, :], modulated2[:, m % 4, :, :])\
                    .then_inc(h2T_hi_ready, 1)
                dve.wait_ge(h2T_hi_ready, m + 1)
                dve.tensor_tensor(h2T[:, 2 * m:2 * m + 2, 1, :], modulated2[:, m % 4, :, :],
                                  h2T[:, 2 * m:2 * m + 2, 0, :], ALU.subtract).then_inc(h2T_ready, 1)

            for m in range(4):
                split_modulated2(m)
            for s in range(SPLIT_SLOTS):
                split_modulated2(s + 4)
                split_lo(JOB_UP, s + SPLIT_SLOTS)

            def conv_sum(n, b):
                dve.wait_ge(up_half_read, n + 1)
                dve.tensor_tensor(conv_in[:], conv_in[:], ps[:, b:b + 4, SEQ:2 * SEQ], ALU.add)\
                    .then_inc(up_read, 1)

            def conv_sides(n, tile, dst):
                dve.wait_ge(conv_mid, TILES * n + TILES)
                for t in range(TILES):
                    dve.scalar_tensor_tensor(dst[:, t, 1:SEQ], conv_in[:, t, 0:SEQ - 1],
                                             vecs[:, bass.ds(tile + (V_CONV + t), 1)],
                                             dst[:, t, 1:SEQ], ALU.mult, ALU.add).then_inc(conv_left, 1)
                dve.wait_ge(conv_left, TILES * n + TILES)
                for t in range(TILES):
                    ins = dve.scalar_tensor_tensor(dst[:, t, 0:SEQ - 1], conv_in[:, t, 1:SEQ],
                                                   vecs[:, bass.ds(tile + (V_CONV + 176 + t), 1)],
                                                   dst[:, t, 0:SEQ - 1], ALU.mult, ALU.add)
                ins.then_inc(conv_done, 1)

            def gate_steps(i, s):
                n = 2 * i
                if s == 3:
                    conv_sum(n, 0)
                if s == 4:
                    conv_sides(n, TILES * i, conv_gate)

            def up_steps(i, s):
                n = 2 * i + 1
                if s == 3:
                    conv_sum(n, 4)
                if s == 4:
                    conv_sides(n, TILES * i + FF_TILES, conv_up)
                if s == 5:
                    dve.wait_ge(conv_done, n + 1)
                    dve.wait_ge(gate_done, i + 1)
                    dve.tensor_tensor(hidden[:, bass.ds(TILES * i, TILES), :], conv_gate[:], conv_up[:], ALU.mult)\
                        .then_inc(hidden_ready, 1)

            def ffn_pair(i, first):
                for s in range(SLOTS):
                    if not first:
                        split_lo(2 * i + JOB_UP, s)
                        up_steps(i - 1, s)
                for s in range(SLOTS):
                    split_lo(2 * i + JOB_UP + 1, s)
                    gate_steps(i, s)

            ffn_pair(0, True)
            with dve.Fori(1, FF_GROUPS) as i:
                ffn_pair(i, False)

            def down_job(i, first, last=False):
                for s in range(SLOTS):
                    split_lo(i + JOB_DOWN, s)
                    t = s if last else s // 2
                    if (last and s < TILES) or (not last and s % 2 == 0):
                        dve.wait_ge(f_hi_ready, TILES * i + t + 1)
                        dve.tensor_tensor(f_lo[:, t:t + 1, :], hidden[:, bass.ds(TILES * i + t, 1), :],
                                          f_hi[:, t:t + 1, :], ALU.subtract).then_inc(f_lo_ready, 1)
                    if first:
                        up_steps(FF_GROUPS - 1, s)

            def add_down(half):
                at = slice(half * UNIT, (half + 1) * UNIT)
                for t in range(TOK):
                    if half:
                        if t == 0:
                            dve.wait_ge(down_tile, 1)
                        else:
                            dve.wait_ge(used[7], JOB_DOWN + FF_GROUPS)
                    b = 4 * half + 2 * t
                    dve.tensor_tensor(final_tmp[:, t, at], ps[:, b:b + 2, :].rearrange("p a n -> p (a n)"),
                                      g2_rows[:, at], ALU.mult).then_inc(out3_gated, 1)
                    dve.wait_ge(out3_gated, 2 * half + t + 1)
                    dve.tensor_tensor(x2[:, t, at], x2[:, t, at], final_tmp[:, t, at], ALU.add)\
                        .then_inc(x3_ready, 1)

            def weigh(half, t):
                at = slice(half * UNIT, (half + 1) * UNIT)
                dve.wait_ge(x3_ready, TOK * half + t + 1)
                dve.tensor_tensor(final_tmp[:, t, at], x2[:, t, at], final_rows[:, at], ALU.mult)\
                    .then_inc(x3_weighted, 1)

            down_job(0, True)
            with dve.Fori(1, FF_GROUPS - 1) as i:
                down_job(i, False)
            down_job(FF_GROUPS - 1, False, last=True)

            dve.wait_ge(g2_ready, 1)
            dve.wait_ge(used[3], JOB_DOWN + FF_GROUPS)
            add_down(0)
            dve.wait_ge(final_landed, 16)
            for t in range(TOK):
                weigh(0, t)
            add_down(1)

            for t in range(TOK):
                factor = rms3[:, t:t + 1]
                dve.wait_ge(squares3, TOK + t + 1)
                dve.tensor_reduce(factor, ssq3[:, t, :], AX.X, ALU.add).then_inc(rms3_step, 1)
                dve.wait_ge(rms3_step, 4 * t + 1)
                dve.tensor_scalar(factor, factor, 1.0 / D, EPS, ALU.mult, ALU.add).then_inc(rms3_step, 1)
                weigh(1, t)
                dve.wait_ge(rms3_step, 4 * t + 3)
                dve.reciprocal(factor, factor).then_inc(rms3_step, 1)
                dve.wait_ge(rms3_step, 4 * t + 4)
                dve.wait_ge(x3_weighted, TOK + t + 1)
                for half in ((0, 1), (1,))[t]:
                    part = final_tmp[:, t, half * UNIT:(half + 1) * UNIT]
                    dve.tensor_scalar(part, part, factor, None, ALU.mult).then_inc(out_ready, 1)

        @block.tensor
        def _(pe):
            def take(j, s):
                pe.wait_ge(lo_ready[s], j + 1)

            def row4(s):
                return s % SPLIT_SLOTS

            pe.wait_ge(ident_landed, 16)
            pe.wait_ge(rows_landed, 32)
            pe.transpose(ps[:, 5, 0:2 * KC], param_rows[0:2 * KC, 0, :], consts[0:2 * KC, 0:2 * KC])\
                .then_inc(vecs_turned, 1)
            pe.wait_ge(c_ready, 2)
            pe.wait_ge(ones_ready, 1)

            def turn_tokens(kc):
                for t in range(2 * TOK):
                    mm = pe.transpose(ps[:, TURN_BANKS[kc], t * P:(t + 1) * P], tokens[:, t, kc * P:(kc + 1) * P],
                                      ident)
                mm.then_inc(tokens_turned, 1)

            def mod_cols(block, b):
                for n in range(block * KC // 2, (block + 1) * KC // 2):
                    mm = pe.matmul(ps[:, b, 2 * n:2 * n + 2], mod_rows[:, n * P:(n + 1) * P],
                                   consts[0:4, C_SEL:C_SEL + 2], start=True, stop=True)
                return mm

            def unit_ada(u, block, kc):
                i = ADA_BLOCKS.index(block)
                if kc == 0 and i == 1:
                    pe.wait_ge(vecs_ready, 3)
                if kc == 0 and i >= 2:
                    pe.wait_ge(mod_rows_ready, i - 1)
                if kc == 0 and i == 3:
                    pe.wait_ge(modulated_ready, 2 * 7)
                for half in range(2):
                    for w in (w_hi, w_lo):
                        mm = pe.matmul(ps[:, 4 + 2 * (i % 2) + half, :], c_parts[:, 4 * kc:4 * kc + P],
                                       w[:, row4(u % SLOTS), half * GROUP:(half + 1) * GROUP],
                                       start=(kc == 0 and w is w_hi), stop=(kc == KC - 1 and w is w_lo))
                return mm

            def unit_k(s, slot, t, b):
                for i in range(2):
                    kc = 2 * s + i
                    o = ps[:, b + t, :].rearrange("p (a n) -> p a n", a=2)
                    at = slice(i * GROUP + t * P, i * GROUP + (t + 1) * P)
                    pe.matmul(o, w_hi[:, row4(slot), at], hT[:, :, 0, kc, :], start=(kc == 0), stop=False)
                    pe.matmul(o, w_hi[:, row4(slot), at], hT[:, :, 1, kc, :], start=False, stop=False)
                    mm = pe.matmul(o, w_lo[:, row4(slot), at], hT[:, :, 0, kc, :], start=False,
                                   stop=(kc == KC - 1))
                return mm

            turns_before = {4: (11, 12), 5: (13, 14), 6: (15,)}
            for u, (kind, *unit) in enumerate(HEAD):
                if kind == "ada":
                    take(u // SLOTS, u % SLOTS)
                    mm = unit_ada(u, *unit)
                else:
                    s, = unit
                    pe.wait_ge(hT_ready, 2 * s + 2)
                    if s == 0:
                        pe.wait_ge(modulated_ready, 2 * 3)
                        pe.wait_ge(mod1_ready, 1)
                    if s == 4:
                        pe.wait_ge(mod1_ready, 2)
                    for kc in turns_before.get(s, ()):
                        turn_tokens(kc)
                    take(u // SLOTS, u % SLOTS)
                    for t in range(TILES):
                        mm = unit_k(s, u % SLOTS, t, 0)
                        if s == 3 and t == 1:
                            pe.wait_ge(mod_rows_ready, 4)
                            mod_cols(3, 5).then_inc(mod_cols_ready, 1)
                            turn_tokens(9)
                            turn_tokens(10)
                mm.then_inc(used[u % SLOTS], 1)
                if u == BLOCK_ENDS[0]:
                    pe.wait_ge(rows2_landed, 128)
                    pe.transpose(ps[:, 6, V_ADAB:V_ADAB + P], param_rows[:, 1, :], ident)
                    for tap in range(TAPS):
                        pe.transpose(ps[:, 6, V_CONV + 88 * tap:V_CONV + 88 * (tap + 1)], param_rows[0:88, 2 + tap, :],
                                     consts[0:88, 0:88])
                    pe.transpose(ps[:, 6, V_CONVB:V_CONVB + 88], param_rows[0:88, 5, :], consts[0:88, 0:88])
                    pe.transpose(ps[:, 7, 0:89], param_rows[0:89, 5, :], consts[0:89, 0:89]).then_inc(vecs_turned, 1)
                if u == BLOCK_ENDS[0] + 4:
                    pe.wait_ge(consts_landed, 16)
                    pe.wait_ge(mod_rows_ready, 1)
                    mod_cols(0, 3)
                if u == MID + 3:
                    pe.wait_ge(mod_rows_ready, 2)
                    mod_cols(2, 3).then_inc(mod_cols_ready, 1)
                for kc in TURN_AFTER.get(u - MID, ()):
                    if kc == 0:
                        pe.wait_ge(normed1, 4)
                    elif kc in (5, 6):
                        pe.wait_ge(modulated_ready, 2 * (kc - 1))
                    elif kc == 7:
                        pe.wait_ge(mod_rows_ready, 3)
                    turn_tokens(kc)
                if u == MID + 23:
                    mod_cols(1, 5)
                if u == K_UNITS[2]:
                    pe.wait_ge(modulated_ready, 2 * 8)
                    turn_tokens(8)

            def sum_mod(g, j):
                b, col = ada_bank(j), TILES * ada_groups(j - 1).index(g)
                pe.wait_ge(ada_summed, KC * (g + 1))
                for n in range(TILES):
                    mm = pe.matmul(ps[:, b, col + n:col + n + 1], ada_acc[:, g % 2, n * P:(n + 1) * P], ones[:],
                                   start=True, stop=True)
                mm.then_inc(mod_summed, 1)

            def unit_paired(s, t, b, both, high):
                for i in range(2):
                    kc = 2 * s + i
                    o = ps[:, b + t, :].rearrange("p (a n) -> p a n", a=2)
                    at = slice(i * GROUP + t * P, i * GROUP + (t + 1) * P)
                    if kc == 0:
                        pe.matmul(o, w_hi[:, row4(s), at], both(kc), start=True, stop=False)
                        mm = pe.matmul(ps[:, b + t, 0:SEQ], w_lo[:, row4(s), at], high(kc), start=False, stop=False)
                    else:
                        pe.matmul(ps[:, b + t, 0:SEQ], w_lo[:, row4(s), at], high(kc), start=False, stop=False)
                        mm = pe.matmul(o, w_hi[:, row4(s), at], both(kc), start=False, stop=(kc == KC - 1))
                return mm

            def moving_weights(s, banks, stationary_hi, stationary_lo, kcs, last):
                for n, b in enumerate(banks):
                    for i, kc in enumerate(kcs):
                        at = slice(i * GROUP, (i + 1) * GROUP)
                        hi, lo = stationary_hi(kc, n), stationary_lo(kc, n)
                        pe.matmul(ps[:, b, :], hi, w_hi[:, row4(s), at], start=(kc == 0), stop=False)
                        pe.matmul(ps[:, b, :], hi, w_lo[:, row4(s), at], start=False, stop=False)
                        mm = pe.matmul(ps[:, b, :], lo, w_hi[:, row4(s), at], start=False, stop=(kc == last))
                return mm

            def tok(part):
                return lambda kc, n: hT[:, n // TOK, part, kc, (n % TOK) * P:(n % TOK + 1) * P]

            def na_scores(n):
                h, t = divmod(n, TOK)
                if n >= 2:
                    pe.wait_ge(na_biased, n - 1)
                    pe.wait_ge(na_ctx_scaled, n - 1)
                for b, keys in ((0, slice(0, SEQ)), (2, slice(SEQ, 2 * SEQ))):
                    mm = pe.matmul(ps[:, b + n % 2, 0:SEQ], qT[:, h, t * P:(t + 1) * P], kT[:, h, keys],
                                   start=True, stop=True)
                mm.then_inc(na_scored, 1)

            def df_scores(n):
                h, t = divmod(n, TOK)
                pe.wait_ge(roped, max(6, 5 + h // 2))
                if n >= 2:
                    pe.wait_ge(df_exp, 2 * n - 2)
                for m in range(2):
                    half = slice(m * MAP_DIM, (m + 1) * MAP_DIM)
                    pe.matmul(ps[:, 2 * (n % 2) + m, :], qT[half, h, t * P:(t + 1) * P], kT[half, h, :],
                              start=True, stop=True).then_inc(df_scored, 1)

            def projection(j):
                kind, _ = PROJECTIONS[j - JOB_NA]
                b = 4 * (j % 2)
                if j >= JOB_NA + 2:
                    pe.wait_ge(*results_read(j - 2))
                if j == JOB_MERGE - 1:
                    pe.wait_ge(rope_sin, 4)
                done = ada_groups(j - 1)
                if done:
                    sum_mod(done[-1], j)
                for s in range(SLOTS):
                    if s == SLOTS - 1 and j in (JOB_DIFF - 1, JOB_MERGE - 1):
                        pe.wait_ge(*results_read(j - 1))
                        for n in range(2):
                            (na_scores if j < JOB_DIFF else df_scores)(n)
                    take(j, s)
                    for t in range(TILES):
                        if s == 0 and t == 3 and done:
                            pe.wait_ge(mod_ready, done[-1] + 1)
                        if kind == "k":
                            mm = unit_k(s, s, t, b)
                        elif kind == "v":
                            mm = moving_weights(s, (b + t,), lambda kc, _: tok(0)(kc, t),
                                                lambda kc, _: tok(1)(kc, t), (2 * s, 2 * s + 1), KC - 1)
                        else:
                            mm = unit_paired(s, t, b, lambda kc: hT[:, 0, :, kc, :], lambda kc: hT[:, 0, 0, kc, :])
                    mm.then_inc(used[s], 1)
                    if s == 5 and len(ada_groups(j)) == 2:
                        pe.wait_ge(*results_read(j - 1))
                        sum_mod(ada_groups(j)[0], j + 1)
                    if s == 1 and j == JOB_MERGE - 2:
                        pe.wait_ge(*results_read(j - 1))
                        for n in range(4):
                            rotate(n)
                    if s == 2 and j == JOB_MERGE - 1:
                        pe.wait_ge(*results_read(j - 1))
                        for n in range(4, 6):
                            rotate(n)

            def rotate(n):
                t, h, b = rotation(n)
                for i in range(2):
                    mm = pe.matmul(ps[:, b, i * SEQ:(i + 1) * SEQ], consts[:, C_ROT:C_ROT + P], t[:, h + i, 0:SEQ],
                                   start=True, stop=True)
                mm.then_inc(rotated, 1)

            pe.wait_ge(modulated_ready, 2 * KC)
            for j in range(JOB_NA + 1, JOB_DIFF):
                projection(j)

            N = HEADS * TOK

            def na_turn(n):
                pe.wait_ge(na_probs, n + 1)
                if n >= 2:
                    pe.wait_ge(na_pT_ready, n - 1)
                for k in range(2 * TOK):
                    mm = pe.transpose(ps[:, 6 + n % 2, k * P:(k + 1) * P], scores[:, n % 3, k * P:(k + 1) * P], ident)
                mm.then_inc(na_turned, 1)

            def na_values(n):
                h = n // TOK
                pe.wait_ge(na_pT_ready, n + 1)
                if n >= 2:
                    pe.wait_ge(na_out, n - 1)
                for k in range(2 * TOK):
                    mm = pe.matmul(ps[:, 4 + n % 2, 0:P], v_sb[:, k, h * HD:(h + 1) * HD], na_pT[:, k, :],
                                   start=(k == 0), stop=(k == 2 * TOK - 1))
                mm.then_inc(na_summed, 1)

            for n in range(N):
                if n + 2 < N:
                    na_scores(n + 2)
                if n == 0:
                    pe.wait_ge(*results_read(JOB_DIFF - 1))
                if n:
                    na_values(n - 1)
                na_turn(n)
            na_values(N - 1)
            pe.wait_ge(na_out, N)
            pe.wait_ge(na_pT_ready, N)

            for j in range(JOB_DIFF, JOB_MERGE):
                projection(j)

            def df_turn(n):
                pe.wait_ge(df_probs, n + 1)
                if n >= 1:
                    pe.wait_ge(df_pT_ready, n)
                for k in range(2 * TOK):
                    mm = pe.transpose(ps[:, 4, k * P:(k + 1) * P], diff_e[:, n % 2, 0, k * P:(k + 1) * P],
                                      ident)
                mm.then_inc(df_turned, 1)

            def df_values(n):
                h = n // TOK
                pe.wait_ge(df_pT_ready, n + 1)
                if n >= 2:
                    pe.wait_ge(df_out, n - 1)
                for k in range(2 * TOK):
                    mm = pe.matmul(ps[:, 6 + n % 2, 0:P], diff_pT[:, n % 2, k, :],
                                   v_sb[:, k, h * HD:(h + 1) * HD], start=(k == 0), stop=(k == 2 * TOK - 1))
                mm.then_inc(df_summed, 1)

            for n in range(N):
                if n + 2 < N:
                    df_scores(n + 2)
                if n == 0:
                    pe.wait_ge(*results_read(JOB_MERGE - 1))
                if n in LATE_ROTATIONS:
                    if LATE_ROTATIONS[n] == 7:
                        pe.wait_ge(rope_sin, 7)
                    rotate(LATE_ROTATIONS[n])
                if n:
                    df_values(n - 1)
                df_turn(n)
            df_values(N - 1)

            def part(t):
                return lambda kc, n: t[:, kc, n * P:(n + 1) * P]

            def spread(n, col, b):
                for kc in range(KC):
                    mm = pe.matmul(ps[:, b + kc // 4, (kc % 4) * P:(kc % 4 + 1) * P],
                                   mod[:, col + kc:col + kc + 1].to_broadcast([P, P]), ident,
                                   start=True, stop=True)
                mm.then_inc(n, 1)

            def turn_y(g):
                pe.wait_ge(y_ready, g + 1)
                for n in range(TILES):
                    for t in range(TOK):
                        at = ((n % 2) * TOK + t) * P
                        mm = pe.transpose(ps[:, 4 + n // 2, at:at + P], y[:, t, n * P:(n + 1) * P], ident)
                mm.then_inc(y_turned, 1)

            def merge_group(g, first):
                j = 3 * g + JOB_MERGE
                if not first:
                    pe.wait_ge(sig_a_ready, g)
                for s in range(SLOTS):
                    take(j, s)
                    moving_weights(s, (0, 1), tok(0), tok(1), (2 * s, 2 * s + 1), KC - 1).then_inc(used[s], 1)
                    if s == 5 and first:
                        pe.wait_ge(o_normed, 1)
                        for n in range(HEADS * TOK):
                            mm = pe.transpose(ps[:, 4 + n // 4, (n % 4) * P:(n % 4 + 1) * P], diff_o[:, n, :],
                                              ident)
                        mm.then_inc(o_turned, 1)
                    if s == 3 and not first:
                        turn_y(g - 1)
                if not first:
                    pe.wait_ge(sig_b_ready, g)
                for s in range(SLOTS):
                    take(j + 1, s)
                    moving_weights(s, (2, 3), tok(0), tok(1), (2 * s, 2 * s + 1), KC - 1).then_inc(used[s], 1)
                    if s == 3 and first:
                        pe.wait_ge(bT_scaled, 1)
                        pe.wait_ge(mod_ready, ADA_GROUPS)
                        spread(g1_spread, 0, 4)
                if first:
                    pe.wait_ge(g1_ready, 1)
                    pe.wait_ge(bT_ready, 1)
                    pe.wait_ge(aT_ready, 1)
                else:
                    pe.wait_ge(yT_ready, g)
                for s in range(SLOTS):
                    take(j + 2, s)
                    kcs = (2 * (s % 4), 2 * (s % 4) + 1)
                    if s < 4:
                        mm = moving_weights(s, (4, 5), part(aT_hi), part(aT_lo), kcs, HEADS - 1)
                    else:
                        mm = moving_weights(s, (6, 7), part(bT_hi), part(bT_lo), kcs, HEADS - 1)
                    mm.then_inc(used[s], 1)

            merge_group(0, True)
            with pe.Fori(1, D // GROUP) as g:
                merge_group(g, False)

            for g in range(4):
                if g == 0:
                    pe.wait_ge(sig_a_ready, 4)
                if g == 1:
                    pe.wait_ge(sig_b_ready, 4)
                if g == 2:
                    pe.wait_ge(yT_ready, 4)
                for s in range(SLOTS):
                    if g == 0 and s == 6:
                        pe.wait_ge(yT_ready, 4)
                    elif g == 0 and s == 0:
                        pe.wait_ge(yT_ready, 3)
                    take(JOB_OUT + g, s)
                    for t in range(TOK):
                        mm = moving_weights(s, (2 * g + t,), lambda kc, _: part(yT_hi)(kc, t),
                                            lambda kc, _: part(yT_lo)(kc, t), (2 * s, 2 * s + 1), KC - 1)
                        if g == 3 and s == SLOTS - 1 and t == 0:
                            mm.then_inc(out_tile, 1)
                    mm.then_inc(used[s], 1)
                    if g == 0 and s == 3:
                        turn_y(3)
            pe.wait_ge(x2_added, 2 * TOK)
            spread(g2_spread, 3 * KC, 0)

            def turn_x2(m):
                for h in range(2):
                    kc = 2 * m + h
                    for t in range(TOK):
                        at = (h * TOK + t) * P
                        mm = pe.transpose(ps[:, 4 + m % 4, at:at + P], x2_normed[:, t, kc * P:(kc + 1) * P], ident)
                mm.then_inc(x2_turned, 1)

            for m in range(4):
                pe.wait_ge(x2_norm_ready, TOK * (m // 2 + 1))
                turn_x2(m)
            pe.wait_ge(g2_ready, 1)

            def both(kc):
                return h2T[:, kc, :, :]

            def high(kc):
                return h2T[:, kc, 0, :]

            def up_job(n, b, ready):
                for s in range(SLOTS):
                    if ready:
                        pe.wait_ge(h2T_ready, s + 1)
                    take(n + JOB_UP, s)
                    for t in range(TILES):
                        mm = unit_paired(s, t, b, both, high)
                    mm.then_inc(used[s], 1)
                    if ready and s + 4 < KC // 2:
                        pe.wait_ge(modulated2_ready, 2 * s + 2)
                        pe.wait_ge(x2_norm_ready, TOK * ((s + 4) // 2 + 1))
                        turn_x2(s + 4)

            up_job(0, 0, True)
            pe.wait_ge(modulated2_ready, KC)
            up_job(1, 4, False)
            with pe.Fori(1, FF_GROUPS) as i:
                for half in range(2):
                    pe.wait_ge(up_read, 2 * i + half - 1)
                    up_job(2 * i + half, 4 * half, False)

            def down_job(i, first, last):
                for s in range(SLOTS):
                    take(i + JOB_DOWN, s)
                    half, t = divmod(s, TILES) if last else (s % 2, s // 2)
                    if half == 0:
                        pe.wait_ge(f_lo_ready, TILES * i + t + 1)
                    if first and s < 2:
                        pe.wait_ge(up_read, 2 * FF_GROUPS - 1 + s)
                    for n in range(TOK):
                        for q in range(2):
                            b = 4 * half + 2 * n + q
                            at = slice(q * GROUP, (q + 1) * GROUP)
                            hi, lo = f_hi[:, t, n * P:(n + 1) * P], f_lo[:, t, n * P:(n + 1) * P]
                            pe.matmul(ps[:, b, :], hi, w_hi[:, row4(s), at], start=(first and t == 0), stop=False)
                            pe.matmul(ps[:, b, :], hi, w_lo[:, row4(s), at], start=False, stop=False)
                            mm = pe.matmul(ps[:, b, :], lo, w_hi[:, row4(s), at], start=False,
                                           stop=(last and t == 3))
                        if last and s == SLOTS - 1 and n == 0:
                            mm.then_inc(down_tile, 1)
                    mm.then_inc(used[s], 1)

            down_job(0, True, False)
            with pe.Fori(1, FF_GROUPS - 1) as i:
                down_job(i, False, False)
            down_job(FF_GROUPS - 1, False, True)


_INS = ["x", "c", "ctx", "c_ctx", "ada_w", "ada_b", "norm1_g", "w_in", "na_rpb", "diff_lambda", "diff_norm_g",
        "w_branch_a", "w_branch_b", "w_out", "norm2_g", "ffn_w_up", "ffn_conv_w", "ffn_conv_b", "ffn_w_down",
        "final_norm_g"]


def kernel(**inputs):
    import concourse.bacc as bacc
    from concourse.bass_utils import run_bass_kernel_spmd

    nc = bacc.Bacc("TRN2", target_bir_lowering=False, num_devices=1)
    arrays, args = {}, []
    for name in _INS:
        a = np.ascontiguousarray(inputs[name])
        arrays[f"in_{name}"] = a
        args.append(nc.dram_tensor(f"in_{name}", a.shape, F32, kind="ExternalInput").ap())
    arrays["in_constants"] = shape_constants()
    args.append(nc.dram_tensor("in_constants", (P, C_ALL), F32, kind="ExternalInput").ap())
    result = nc.dram_tensor("out_0", (1, SEQ, D), F32, kind="ExternalOutput").ap()
    block_program(nc, *args, result)
    r = run_bass_kernel_spmd(nc, [arrays], core_ids=[0])
    return r.results[0]["out_0"]
```
